# Optimizing a Trainium2 kernel written in Bass

```python
import math
import jax, jax.numpy as jnp
from jax import lax
import numpy as np

D_MODEL = 1024
BATCH = 1
SEQ = 256
DEPTH = 1

CHUNK = 64
D_MIX = 2 * D_MODEL
SSD_WIDTH = D_MIX // 2
SSD_HEAD_DIM = 64
SSD_HEADS = SSD_WIDTH // SSD_HEAD_DIM
SSD_GROUPS = 2
SSD_HPG = SSD_HEADS // SSD_GROUPS
SSD_STATE = 128
SSD_CONV = 4
SSD_CONV_CH = SSD_WIDTH + 2 * SSD_GROUPS * SSD_STATE
SC_WIDTH = D_MIX - SSD_WIDTH
SC_GROUP_DIM = 64
SC_GROUPS = SC_WIDTH // SC_GROUP_DIM
SC_CONV = 3
IN_COLS = SSD_WIDTH + SSD_CONV_CH + SSD_HEADS + 3 * SC_WIDTH
N_EXPERT_GROUPS = 4
EXPERTS_PER_GROUP = 8
N_EXPERTS = N_EXPERT_GROUPS * EXPERTS_PER_GROUP
TOP_K_IN_GROUP = 2
D_FF_EXPERT = D_MODEL // 2
EXPERT_BLOCK = 128
EPS = 1e-6


def rmsnorm(x, g):
    xf = x.astype(jnp.float32)
    y = xf * lax.rsqrt(jnp.mean(xf * xf, axis=-1, keepdims=True) + EPS)
    return (y * g.astype(jnp.float32)).astype(x.dtype)

def grouped_rmsnorm(x, g, n_groups):
    shp = x.shape
    xf = x.astype(jnp.float32).reshape(*shp[:-1], n_groups, shp[-1] // n_groups)
    y = xf * lax.rsqrt(jnp.mean(xf * xf, axis=-1, keepdims=True) + EPS)
    return (y.reshape(shp) * g.astype(jnp.float32)).astype(x.dtype)

def causal_depthwise_conv(x, w):
    k = w.shape[0]
    return lax.conv_general_dilated(
        x, w[:, None, :].astype(x.dtype), window_strides=(1,), padding=[(k - 1, 0)],
        dimension_numbers=("NWC", "WIO", "NWC"), feature_group_count=x.shape[-1])

def ssd_chunked_scan(x, dt, a, bmat, cmat):
    bsz, seqlen = x.shape[0], x.shape[1]
    nc = seqlen // CHUNK
    f32 = jnp.float32
    xdt = (x.astype(f32) * dt[..., None]).reshape(bsz, nc, CHUNK, SSD_GROUPS, SSD_HPG, SSD_HEAD_DIM)
    bc = bmat.astype(f32).reshape(bsz, nc, CHUNK, SSD_GROUPS, SSD_STATE)
    cc = cmat.astype(f32).reshape(bsz, nc, CHUNK, SSD_GROUPS, SSD_STATE)
    a_dt = (dt * a.astype(f32)).reshape(bsz, nc, CHUNK, SSD_GROUPS, SSD_HPG)
    ac = jnp.cumsum(a_dt, axis=2).transpose(0, 1, 3, 4, 2)
    seg = ac[..., :, None] - ac[..., None, :]
    causal = jnp.tril(jnp.ones((CHUNK, CHUNK), dtype=bool))
    decay_in = jnp.exp(jnp.where(causal, seg, -jnp.inf))
    cb = jnp.einsum("bclgn,bcsgn->bcgls", cc, bc)
    y_diag = jnp.einsum("bcgls,bcgrls,bcsgrp->bclgrp", cb, decay_in, xdt)
    decay_to_end = jnp.exp(ac[..., -1:] - ac)
    states = jnp.einsum("bclgn,bcgrl,bclgrp->bcgrpn", bc, decay_to_end, xdt)
    chunk_decay = jnp.exp(ac[..., -1])

    def step(carry, inp):
        st, dec = inp
        return carry * dec[..., None, None] + st, carry

    init = jnp.zeros((bsz, SSD_GROUPS, SSD_HPG, SSD_HEAD_DIM, SSD_STATE), f32)
    _, prev = lax.scan(step, init, (jnp.moveaxis(states, 1, 0), jnp.moveaxis(chunk_decay, 1, 0)))
    prev = jnp.moveaxis(prev, 0, 1)
    y_off = jnp.einsum("bclgn,bcgrpn,bcgrl->bclgrp", cc, prev, jnp.exp(ac))
    return (y_diag + y_off).reshape(bsz, seqlen, SSD_HEADS, SSD_HEAD_DIM)

def hybrid_mixer(hn, w_in, ssd_conv_w, ssd_conv_b, dt_bias, a_log, d_skip, ssd_norm,
                 sc_conv_w, sc_norm, w_out):
    bsz, seqlen, _ = hn.shape
    proj = hn @ w_in
    o1 = SSD_WIDTH
    o2 = o1 + SSD_CONV_CH
    o3 = o2 + SSD_HEADS
    o4 = o3 + SC_WIDTH
    o5 = o4 + SC_WIDTH
    z, xbc, dt_raw, sc_b, sc_c, sc_v = jnp.split(proj, [o1, o2, o3, o4, o5], axis=-1)
    xbc = jax.nn.silu(causal_depthwise_conv(xbc, ssd_conv_w) + ssd_conv_b)
    xs, bm, cm = jnp.split(xbc, [SSD_WIDTH, SSD_WIDTH + SSD_GROUPS * SSD_STATE], axis=-1)
    dt = jax.nn.softplus(dt_raw.astype(jnp.float32) + dt_bias.astype(jnp.float32))
    a = -jnp.exp(a_log.astype(jnp.float32))
    xh = xs.reshape(bsz, seqlen, SSD_HEADS, SSD_HEAD_DIM)
    y = ssd_chunked_scan(xh, dt, a,
                         bm.reshape(bsz, seqlen, SSD_GROUPS, SSD_STATE),
                         cm.reshape(bsz, seqlen, SSD_GROUPS, SSD_STATE))
    y = y + d_skip.astype(jnp.float32)[:, None] * xh.astype(jnp.float32)
    y = y.reshape(bsz, seqlen, SSD_WIDTH).astype(hn.dtype)
    ssd_out = grouped_rmsnorm(y * jax.nn.silu(z), ssd_norm, SSD_GROUPS)
    sc = sc_b * causal_depthwise_conv(sc_c * sc_v, sc_conv_w)
    sc_out = grouped_rmsnorm(sc, sc_norm, SC_GROUPS)
    return jnp.concatenate([ssd_out, sc_out], axis=-1) @ w_out

def hierarchical_moe(hn, w_router_group, w_router_expert, w_gate, w_up, w_down):
    bsz, seqlen, d = hn.shape
    tokens = hn.reshape(-1, d)
    n = tokens.shape[0]
    g_logits = (tokens @ w_router_group).astype(jnp.float32)
    g_probs = jax.nn.softmax(g_logits, axis=-1)
    g_idx = jnp.argmax(g_logits, axis=-1)
    g_w = jnp.take_along_axis(g_probs, g_idx[:, None], axis=1)
    e_logits = jnp.einsum("nd,gde->nge", tokens, w_router_expert).astype(jnp.float32)
    e_sel = jnp.take_along_axis(e_logits, g_idx[:, None, None], axis=1)[:, 0]
    top_v, top_i = lax.top_k(e_sel, TOP_K_IN_GROUP)
    gates = g_w * jax.nn.softmax(top_v, axis=-1)
    expert_id = (g_idx[:, None] * EXPERTS_PER_GROUP + top_i).reshape(-1).astype(jnp.int32)
    token_id = jnp.repeat(jnp.arange(n, dtype=jnp.int32), TOP_K_IN_GROUP)
    gate_flat = gates.reshape(-1)
    m = n * TOP_K_IN_GROUP
    order = jnp.argsort(expert_id)
    sorted_e = expert_id[order]
    counts = jnp.bincount(expert_id, length=N_EXPERTS)
    padded_counts = ((counts + EXPERT_BLOCK - 1) // EXPERT_BLOCK) * EXPERT_BLOCK
    padded_end = jnp.cumsum(padded_counts)
    padded_start = padded_end - padded_counts
    start = jnp.cumsum(counts) - counts
    rank = jnp.arange(m, dtype=jnp.int32) - start[sorted_e]
    dest = padded_start[sorted_e] + rank
    p_rows = ((m + N_EXPERTS * EXPERT_BLOCK + EXPERT_BLOCK - 1) // EXPERT_BLOCK) * EXPERT_BLOCK
    n_blocks = p_rows // EXPERT_BLOCK
    row_token = jnp.zeros((p_rows,), jnp.int32).at[dest].set(token_id[order])
    row_gate = jnp.zeros((p_rows,), jnp.float32).at[dest].set(gate_flat[order])
    block_expert = jnp.clip(
        jnp.searchsorted(padded_end, jnp.arange(n_blocks) * EXPERT_BLOCK, side="right"),
        0, N_EXPERTS - 1).astype(jnp.int32)
    xs = tokens[row_token].reshape(n_blocks, EXPERT_BLOCK, d)

    def run_block(args):
        xb, e = args
        return (jax.nn.silu(xb @ w_gate[e]) * (xb @ w_up[e])) @ w_down[e]

    ys = lax.map(run_block, (xs, block_expert)).reshape(p_rows, d)
    out = jnp.zeros((n, d), jnp.float32).at[row_token].add(ys.astype(jnp.float32) * row_gate[:, None])
    return out.reshape(bsz, seqlen, d).astype(hn.dtype)

def first_inputs(seed: int = 0) -> dict:
    key = jax.random.key(seed)
    ks = jax.random.split(key, 24)
    f32 = jnp.float32

    def nrm(k, shape, scale):
        return jax.random.normal(k, shape, f32) * scale

    x = nrm(ks[0], (BATCH, SEQ, D_MODEL), 1.0)
    norm_mix = 1.0 + nrm(ks[1], (DEPTH, D_MODEL), 0.02)
    w_in = nrm(ks[2], (DEPTH, D_MODEL, IN_COLS), D_MODEL ** -0.5)
    ssd_conv_w = nrm(ks[3], (DEPTH, SSD_CONV, SSD_CONV_CH), SSD_CONV ** -0.5)
    ssd_conv_b = nrm(ks[4], (DEPTH, SSD_CONV_CH), 0.01)
    dt0 = jnp.exp(jax.random.uniform(ks[5], (DEPTH, SSD_HEADS), f32,
                                     minval=math.log(1e-3), maxval=math.log(1e-1)))
    dt_bias = dt0 + jnp.log(-jnp.expm1(-dt0))
    a_log = jnp.log(jax.random.uniform(ks[6], (DEPTH, SSD_HEADS), f32, minval=1.0, maxval=16.0))
    d_skip = 1.0 + nrm(ks[7], (DEPTH, SSD_HEADS), 0.1)
    ssd_norm = 1.0 + nrm(ks[8], (DEPTH, SSD_WIDTH), 0.02)
    sc_conv_w = nrm(ks[9], (DEPTH, SC_CONV, SC_WIDTH), SC_CONV ** -0.5)
    sc_norm = 1.0 + nrm(ks[10], (DEPTH, SC_WIDTH), 0.02)
    w_out = nrm(ks[11], (DEPTH, D_MIX, D_MODEL), D_MIX ** -0.5)
    norm_ffn = 1.0 + nrm(ks[12], (DEPTH, D_MODEL), 0.02)
    w_router_group = nrm(ks[13], (DEPTH, D_MODEL, N_EXPERT_GROUPS), D_MODEL ** -0.5)
    w_router_expert = nrm(ks[14], (DEPTH, N_EXPERT_GROUPS, D_MODEL, EXPERTS_PER_GROUP), D_MODEL ** -0.5)
    w_gate = nrm(ks[15], (DEPTH, N_EXPERTS, D_MODEL, D_FF_EXPERT), D_MODEL ** -0.5)
    w_up = nrm(ks[16], (DEPTH, N_EXPERTS, D_MODEL, D_FF_EXPERT), D_MODEL ** -0.5)
    w_down = nrm(ks[17], (DEPTH, N_EXPERTS, D_FF_EXPERT, D_MODEL), D_FF_EXPERT ** -0.5)
    final_norm = 1.0 + nrm(ks[18], (D_MODEL,), 0.02)
    return {"x": x, "norm_mix": norm_mix, "w_in": w_in, "ssd_conv_w": ssd_conv_w,
            "ssd_conv_b": ssd_conv_b, "dt_bias": dt_bias, "a_log": a_log, "d_skip": d_skip,
            "ssd_norm": ssd_norm, "sc_conv_w": sc_conv_w, "sc_norm": sc_norm, "w_out": w_out,
            "norm_ffn": norm_ffn, "w_router_group": w_router_group,
            "w_router_expert": w_router_expert, "w_gate": w_gate, "w_up": w_up,
            "w_down": w_down, "final_norm": final_norm}

def first_block(x, norm_mix, w_in, ssd_conv_w, ssd_conv_b, dt_bias, a_log, d_skip, ssd_norm,
              sc_conv_w, sc_norm, w_out, norm_ffn, w_router_group, w_router_expert,
              w_gate, w_up, w_down, final_norm):
    h = x
    for i in range(DEPTH):
        hn = rmsnorm(h, norm_mix[i])
        h = h + hybrid_mixer(hn, w_in[i], ssd_conv_w[i], ssd_conv_b[i], dt_bias[i], a_log[i],
                             d_skip[i], ssd_norm[i], sc_conv_w[i], sc_norm[i], w_out[i])
        hn = rmsnorm(h, norm_ffn[i])
        h = h + hierarchical_moe(hn, w_router_group[i], w_router_expert[i],
                                 w_gate[i], w_up[i], w_down[i])
    return rmsnorm(h, final_norm)


D_MIX_2 = D_MODEL
D_LRU = D_MIX_2 // 2
LRU_BLOCKS = 8
LRU_BLOCK = D_LRU // LRU_BLOCKS
CONV_WIDTH = 4
LRU_C = 8.0
GLA_HEADS = 4
GLA_DV = (D_MIX_2 - D_LRU) // GLA_HEADS
GLA_DK = GLA_DV // 2
GLA_K = GLA_HEADS * GLA_DK
GLA_V = GLA_HEADS * GLA_DV
GATE_RANK = 16
GATE_TAU = 16.0
D_FF = ((8 * D_MODEL // 3 + 255) // 256) * 256

SPLIT_SIZES = (D_LRU, D_LRU, GLA_K, GLA_K, GLA_V, GLA_V, GATE_RANK)
P_IN = sum(SPLIT_SIZES)
SPLIT_IDX = tuple(int(v) for v in np.cumsum(SPLIT_SIZES)[:-1])


def rms_norm(x, gain):
    xf = x.astype(jnp.float32)
    y = xf * lax.rsqrt(jnp.mean(xf * xf, axis=-1, keepdims=True) + EPS)
    return (y * gain.astype(jnp.float32)).astype(x.dtype)

def causal_depthwise_conv_2(x, w, b):
    seq = x.shape[1]
    xp = jnp.pad(x, ((0, 0), (CONV_WIDTH - 1, 0), (0, 0)))
    y = xp[:, 0:seq, :] * w[0]
    for j in range(1, CONV_WIDTH):
        y = y + xp[:, j:j + seq, :] * w[j]
    return y + b

def block_diag_linear(x, w, b):
    xb = x.reshape(x.shape[:-1] + (LRU_BLOCKS, LRU_BLOCK))
    y = jnp.einsum("bsni,nij->bsnj", xb, w.astype(x.dtype))
    return y.reshape(x.shape) + b.astype(x.dtype)

def rg_lru(x, w_a, b_a, w_i, b_i, lam):
    xf = x.astype(jnp.float32)
    r = jax.nn.sigmoid(block_diag_linear(xf, w_a, b_a))
    i = jax.nn.sigmoid(block_diag_linear(xf, w_i, b_i))
    log_a = -LRU_C * r * jax.nn.softplus(-lam.astype(jnp.float32))
    a = jnp.exp(log_a)
    u = jnp.sqrt(-jnp.expm1(2.0 * log_a)) * (i * xf)

    def step(h, au):
        a_t, u_t = au
        h = a_t * h + u_t
        return h, h

    h0 = jnp.zeros((xf.shape[0], xf.shape[2]), jnp.float32)
    _, hs = lax.scan(step, h0, (a.swapaxes(0, 1), u.swapaxes(0, 1)))
    return hs.swapaxes(0, 1).astype(x.dtype)

def gla_chunk_causal(q, k, v, log_alpha):
    bsz, seq = q.shape[:2]
    nc = seq // CHUNK

    def rs(t):
        return t.astype(jnp.float32).reshape(bsz, nc, CHUNK, GLA_HEADS, t.shape[-1])

    q, k, v, la = rs(q), rs(k), rs(v), rs(log_alpha)
    bcum = jnp.cumsum(la, axis=2)
    b_end = bcum[:, :, -1:]
    k_dec = k * jnp.exp(b_end - bcum)
    q_dec = q * jnp.exp(b_end)
    scores = jnp.einsum("bnshd,bnthd->bnhst", q, k_dec)
    o_intra = jnp.einsum("bnhst,bnthv->bnshv", scores, v)
    updates = jnp.einsum("bnthd,bnthv->bnhdv", k_dec, v)
    decay = jnp.exp(b_end[:, :, 0])

    def step(state, inp):
        d, upd = inp
        return d[..., None] * state + upd, state

    s0 = jnp.zeros((bsz, GLA_HEADS, GLA_DK, GLA_DV), jnp.float32)
    _, s_prev = lax.scan(step, s0, (decay.swapaxes(0, 1), updates.swapaxes(0, 1)))
    s_prev = s_prev.swapaxes(0, 1)
    o_inter = jnp.einsum("bnshd,bnhdv->bnshv", q_dec, s_prev)
    return (o_intra + o_inter).reshape(bsz, seq, GLA_HEADS, GLA_DV)

def second_inputs(seed: int = 0) -> dict:
    key = jax.random.key(seed)
    ks = jax.random.split(key, 24)
    f32 = jnp.float32

    def nrm(k, shape, scale):
        return jax.random.normal(k, shape, f32) * scale

    def gain(k, shape):
        return 1.0 + 0.02 * jax.random.normal(k, shape, f32)

    u = jax.random.uniform(ks[10], (DEPTH, D_LRU), f32, 0.9, 0.999)
    s = u ** (1.0 / LRU_C)
    lam = jnp.log(s) - jnp.log1p(-s)
    return {
        "x": jax.random.normal(ks[0], (BATCH, SEQ, D_MODEL), f32),
        "norm1": gain(ks[1], (DEPTH, D_MODEL)),
        "w_in": nrm(ks[2], (DEPTH, D_MODEL, P_IN), D_MODEL ** -0.5),
        "conv_w": nrm(ks[3], (DEPTH, CONV_WIDTH, D_LRU), CONV_WIDTH ** -0.5),
        "conv_b": nrm(ks[4], (DEPTH, D_LRU), 0.02),
        "lru_wa": nrm(ks[5], (DEPTH, LRU_BLOCKS, LRU_BLOCK, LRU_BLOCK), LRU_BLOCK ** -0.5),
        "lru_ba": nrm(ks[6], (DEPTH, D_LRU), 0.02),
        "lru_wi": nrm(ks[7], (DEPTH, LRU_BLOCKS, LRU_BLOCK, LRU_BLOCK), LRU_BLOCK ** -0.5),
        "lru_bi": nrm(ks[8], (DEPTH, D_LRU), 0.02),
        "lru_lambda": lam,
        "gla_w_alpha": nrm(ks[11], (DEPTH, GATE_RANK, GLA_K), GATE_RANK ** -0.5),
        "gla_b_alpha": nrm(ks[12], (DEPTH, GLA_K), 0.02),
        "gla_norm": gain(ks[13], (DEPTH, GLA_DV)),
        "w_out": nrm(ks[14], (DEPTH, D_MIX_2, D_MODEL), D_MIX_2 ** -0.5),
        "norm2": gain(ks[15], (DEPTH, D_MODEL)),
        "w_ffn_in": nrm(ks[16], (DEPTH, D_MODEL, 2 * D_FF), D_MODEL ** -0.5),
        "w_ffn_out": nrm(ks[17], (DEPTH, D_FF, D_MODEL), D_FF ** -0.5),
        "final_norm": gain(ks[18], (D_MODEL,)),
    }

def second_block(x, norm1, w_in, conv_w, conv_b, lru_wa, lru_ba, lru_wi, lru_bi,
              lru_lambda, gla_w_alpha, gla_b_alpha, gla_norm, w_out, norm2,
              w_ffn_in, w_ffn_out, final_norm):
    bsz, seq, _ = x.shape
    q_scale = GLA_DK ** -0.5
    for l in range(DEPTH):
        h = rms_norm(x, norm1[l])
        p = h @ w_in[l]
        lru_x, lru_g, q, k, v, g, z = jnp.split(p, SPLIT_IDX, axis=-1)

        lru_x = causal_depthwise_conv_2(lru_x, conv_w[l], conv_b[l])
        lru_o = rg_lru(lru_x, lru_wa[l], lru_ba[l], lru_wi[l], lru_bi[l],
                       lru_lambda[l]) * jax.nn.gelu(lru_g)

        zf = z.astype(jnp.float32) @ gla_w_alpha[l].astype(jnp.float32) + gla_b_alpha[l]
        log_alpha = jax.nn.log_sigmoid(zf) / GATE_TAU
        qh = (q * q_scale).reshape(bsz, seq, GLA_HEADS, GLA_DK)
        kh = k.reshape(bsz, seq, GLA_HEADS, GLA_DK)
        vh = v.reshape(bsz, seq, GLA_HEADS, GLA_DV)
        lah = log_alpha.reshape(bsz, seq, GLA_HEADS, GLA_DK)
        o = gla_chunk_causal(qh, kh, vh, lah)
        o = rms_norm(o, gla_norm[l]).reshape(bsz, seq, GLA_V).astype(x.dtype)
        gla_o = o * jax.nn.silu(g)

        mix = jnp.concatenate([lru_o, gla_o], axis=-1) @ w_out[l]
        x = x + mix

        h = rms_norm(x, norm2[l])
        gate, up = jnp.split(h @ w_ffn_in[l], 2, axis=-1)
        x = x + (jax.nn.silu(gate) * up) @ w_ffn_out[l]
    return rms_norm(x, final_norm)


def setup_inputs(seed=0):
    out = dict(first_inputs(seed))
    for name, value in second_inputs(seed + 1).items():
        if name != "x":
            out[name + "_2"] = value
    return out


def reference(
    x, norm_mix, w_in, ssd_conv_w, ssd_conv_b, dt_bias, a_log, d_skip, ssd_norm, sc_conv_w,
    sc_norm, w_out, norm_ffn, w_router_group, w_router_expert, w_gate, w_up, w_down, final_norm,
    norm1_2, w_in_2, conv_w_2, conv_b_2, lru_wa_2, lru_ba_2, lru_wi_2, lru_bi_2, lru_lambda_2,
    gla_w_alpha_2, gla_b_alpha_2, gla_norm_2, w_out_2, norm2_2, w_ffn_in_2, w_ffn_out_2,
    final_norm_2,
):
    x = first_block(
        x, norm_mix, w_in, ssd_conv_w, ssd_conv_b, dt_bias, a_log, d_skip, ssd_norm, sc_conv_w,
        sc_norm, w_out, norm_ffn, w_router_group, w_router_expert, w_gate, w_up, w_down,
        final_norm,
    )
    return second_block(
        x, norm1_2, w_in_2, conv_w_2, conv_b_2, lru_wa_2, lru_ba_2, lru_wi_2, lru_bi_2,
        lru_lambda_2, gla_w_alpha_2, gla_b_alpha_2, gla_norm_2, w_out_2, norm2_2, w_ffn_in_2,
        w_ffn_out_2, final_norm_2,
    )


_drawn_inputs = setup_inputs


def setup_inputs(seed=0):
    import zlib

    import numpy as np

    out = dict(_drawn_inputs(seed))
    spreads = {}
    factors = {'norm1_2': 2.931,
     'lru_ba_2': 42.729,
     'lru_bi_2': 33.63,
     'gla_b_alpha_2': 8.0,
     'gla_norm_2': 6.733,
     'norm2_2': 4.272,
     'final_norm_2': 7.755,
     'conv_b_2': 4.27}
    for name, (base, spread) in spreads.items():
        noise = np.random.default_rng([zlib.crc32(name.encode()), seed]).standard_normal(out[name].shape)
        drawn = base * np.exp(spread * noise) if base else spread * noise
        out[name] = __import__('jax').numpy.asarray(drawn.astype(out[name].dtype))
    for name, factor in factors.items():
        out[name] = (out[name] * factor).astype(out[name].dtype)
    return out
```

```python
from contextlib import ExitStack

import numpy as np

import concourse.bass as bass
from concourse import mybir

F32 = mybir.dt.float32
F32R = mybir.dt.float32r
I32 = mybir.dt.int32
ALU = mybir.AluOpType
ACT = mybir.ActivationFunctionType
AX_X = mybir.AxisListType.X

P = 128
T = 256
TB = T // P
D = 1024
KC = D // P
EPS = 1e-6
SSD_W, HEADS, HD, STATE, GROUPS = 1024, 16, 64, 128, 2
GW = SSD_W // GROUPS
XBC = SSD_W + 2 * GROUPS * STATE
XC = XBC // P
O_XBC, O_DT = SSD_W, SSD_W + XBC
O_SCB = O_DT + HEADS
O_SCC, O_SCV = O_SCB + 1024, O_SCB + 2048
NG, EPG, NE, FF = 4, 8, 32, 512
CAP = 32
ROUND = NE * CAP
LRU = 512
LC = LRU // P
O_LG, O_Q, O_K, O_V, O_G, O_Z = 512, 1024, 1280, 1536, 2048, 2560
RANK = 16
FF2 = 2816
FC = FF2 // P
UNIT = 4096
GR = 1024
SLOTS = 6

PCOLS, PROWS = {}, []
for _tile, _items in enumerate((
        (("norm_mix", 8), ("ssd_conv_w", 48), ("ssd_conv_b", 12), ("sc_conv_w", 24), ("sc_norm", 8),
         ("ssd_norm", 8), ("norm_ffn", 8)),
        (("norm1_2", 8), ("conv_w_2", 16), ("conv_b_2", 4), ("lru_ba_2", 4), ("lru_bi_2", 4),
         ("lru_lambda_2", 4), ("norm2_2", 8)))):
    _row = 0
    for _name, _n in _items:
        PCOLS[_name] = P * _tile + _row
        PROWS.append((_name, _tile, _row, _n))
        _row += _n
ROWS_A, ROWS_B = 116, 48


def bcast(ap, shape):
    return ap.broadcast_to(shape)


def two_block_layer(nc, x, w, out):
    with ExitStack() as ctx:
        build(nc, ctx, x, w, out)


def build(nc, ctx, x, w, out):
    def sb(name, shape, dt=F32, where=ctx):
        return where.enter_context(nc.sbuf_tensor(name, shape, dt))

    def sem(name):
        return ctx.enter_context(nc.semaphore(name))

    ring = sb("ring", [P, SLOTS, UNIT])
    w_hi = sb("w_hi", [P, 2, GR], F32R)
    w_lo = sb("w_lo", [P, 2, GR], F32R)
    act_p = sb("act_p", [P, 2, KC, T], F32R)
    act_q = sb("act_q", [P, 2, KC, T], F32R)
    res = sb("res", [P, TB, D])
    ident = sb("ident", [P, P])
    m_le = sb("m_le", [P, P])
    m_gt = sb("m_gt", [P, P])
    ones = sb("ones", [P, P])
    blk64 = sb("blk64", [P, P])
    iota_f = sb("iota_f", [P, P])
    iota_p = sb("iota_p", [P, 1])
    par = sb("par", [P, 2 * P])
    bc16 = sb("bc16", [P, 3, HEADS])
    w_dt = sb("w_dt", [P, KC, HEADS])
    w_z = sb("w_z", [P, KC, RANK])
    ws_hi = sb("ws_hi", [P, KC, 16], F32R)
    ws_lo = sb("ws_lo", [P, KC, 16], F32R)
    w_rt = sb("w_rt", [P, KC, NG + NE])
    w_al = sb("w_al", [RANK + 1, 256])
    sm = sb("sm", [P, 96])
    rounds_i = sb("rounds_i", [1, 2], I32)
    sp4 = sb("sp4", [P, 8, LC])

    bank = [ctx.enter_context(nc.psum_tensor(f"bank{i}", [P, 512], F32)) for i in range(8)]

    ph = ExitStack()
    xdt = sb("xdt", [P, TB, D], where=ph)
    x_tok = sb("x_tok", [P, TB, D], where=ph)
    z_tok = sb("z_tok", [P, TB, D], where=ph)
    bc_t = sb("bc_t", [P, 4, T], where=ph)
    cbm = sb("cbm", [P, GROUPS, 3, P], where=ph)
    seg_l = sb("seg_l", [P, 4, P], where=ph)
    seg_e = sb("seg_e", [P, 2, 4, P], where=ph)
    sc_t = sb("sc_t", [P, 4, T], where=ph)
    pad = sb("pad", [P, 2, T + 3], where=ph)
    cv = sb("cv", [P, 2, T], where=ph)
    prow = seg_l[:, 0:2, :]
    adt = sb("adt", [P, 8, TB, HEADS], where=ph)
    ef = sb("ef", [P, 2, HEADS], where=ph)
    ph.close()
    ph = ExitStack()
    tok = sb("tok", [P, TB, D], where=ph)
    moe = sb("moe", [P, TB, D], where=ph)
    x_t = sb("x_t", [P, 2, KC, P], where=ph)
    tok_t = x_t[:, :, :, :].rearrange("p a c t -> p (a c t)").rearrange("p (c t) -> p c t", c=KC)
    y_e = sb("y_e", [P, D], where=ph)
    fgain = sb("fgain", [P, D], where=ph)
    onehot = sb("onehot", [P, 2, TB, P], where=ph)
    gmat = sb("gmat", [P, 2, T], where=ph)
    gtmp = sb("gtmp", [P, 2, T], where=ph)
    h_e = sb("h_e", [P, P], where=ph)
    h_t = sb("h_t", [P, P], where=ph)
    rows = sb("rows", [P, 4, T], where=ph)
    pos = sb("pos", [P, TB, 4], where=ph)
    diag = y_e[:, :].rearrange("p (b k j) -> p b k j", b=TB, j=P)
    rt = moe[:, 0, 0:12 * TB * NE].rearrange("p (n b e) -> p n b e", n=12, b=TB)
    r8 = moe[:, 1, 0:16 * TB * EPG].rearrange("p (n b e) -> p n b e", n=16, b=TB)
    r1 = moe[:, 1, 256:256 + 16 * TB].rearrange("p (n b) -> p n b", b=TB)
    m_lt = sb("m_lt", [P, P], where=ph)
    ph.close()
    ph = ExitStack()
    nrm = sb("nrm", [P, TB, D], where=ph)
    lpad = sb("lpad", [P, LC, T + 3], where=ph)
    lx = sb("lx", [P, LC, T], where=ph)
    lgate = sb("lgate", [P, LC, T], where=ph)
    lr = nrm[:, 0, :].rearrange("p (c t) -> p c t", c=LC)
    lru_w = sb("lru_w", [P, 2, LC, P], where=ph)
    k_tok = sb("k_tok", [P, TB, 256], where=ph)
    v_tok = sb("v_tok", [P, TB, 512], where=ph)
    g_tok = sb("g_tok", [P, TB, 512], where=ph)
    q_t = sb("q_t", [P, 2, T], where=ph)
    la = sb("la", [P, TB, 256], where=ph)
    st = sb("st", [P, 4, 2, P], where=ph)
    m_gtc = sb("m_gtc", [P, P], where=ph)
    z_sb = sb("z_sb", [P, TB, RANK], where=ph)
    z_t = sb("z_t", [RANK + 1, T], where=ph)
    gnorm = sb("gnorm", [P, P], where=ph)
    dec = sb("dec", [P, 2, 4], where=ph)
    fg2 = v_tok[:, :, :].rearrange("p b n -> p (b n)")
    ph.close()

    units = []
    grans = []

    def whole(u):
        return ring[:, u % SLOTS, :]

    def cols_unit(wt, *spans):
        u = len(units)
        parts, at = [], 0
        for c0, n in spans:
            dst = whole(u).rearrange("p (k n) -> p k n", k=KC)[:, :, at:at + n]
            parts.append((dst, wt.rearrange("(k p) n -> p k n", p=P)[:, :, c0:c0 + n]))
            at += n
        units.append(parts)
        return u

    def rows_unit(wt, chunk, n):
        u = len(units)
        dst = whole(u)[:, 0:n * D].rearrange("p (k n) -> p k n", k=n)
        src = wt[chunk * P:(chunk + n) * P, :].rearrange("(k p) n -> p k n", p=P)
        units.append([(dst, src)])
        return u

    def turn_grans(u, js):
        for j in js:
            grans.append((u, whole(u).rearrange("p (k n) -> p k n", k=KC)[:, :, j * P:(j + 1) * P], None))

    def flow_grans(u, c0, n):
        kn = GR // n
        for k in range(0, KC, kn):
            grans.append((u, whole(u).rearrange("p (k n) -> p k n", k=KC)[:, k:k + kn, c0:c0 + n], None))

    def row_grans(u, gains):
        for j, gain in enumerate(gains):
            grans.append((u, whole(u)[:, j * GR:(j + 1) * GR], gain))

    def pcol(name, i):
        return par[:, PCOLS[name] + i:PCOLS[name] + i + 1]

    for c in range(3):
        turn_grans(cols_unit(w["w_in"], (O_XBC + 512 * c, 512)), range(4))
    for c in range(2):
        flow_grans(cols_unit(w["w_in"], (512 * c, 512)), 0, 512)
    for c in range(2):
        for o in (O_SCC, O_SCV, O_SCB):
            turn_grans(cols_unit(w["w_in"], (o + 512 * c, 512)), range(4))
    G_Z, G_SC, G_WO = 12, 20, 44
    MIX = [8, 9, 10, 11, 0, 1, 2, 3, 4, 5, 6, 7, 12, 13, 14, 15]
    for c in range(0, 16, 4):
        ks = MIX[c:c + 4]
        row_grans(rows_unit(w["w_out"], ks[0], 4),
                  [pcol("sc_norm", k - 8) if k >= 8 else pcol("ssd_norm", k) for k in ks])
    UA, GA = len(units), len(grans)
    G_Q, G_K, G_V, G_G, G_LG = GA + 4, GA + 6, GA + 8, GA + 12, GA + 16
    turn_grans(cols_unit(w["w_in_2"], (0, 512)), range(4))
    u = cols_unit(w["w_in_2"], (O_Q, 512))
    turn_grans(u, range(2))
    flow_grans(u, 256, 256)
    flow_grans(cols_unit(w["w_in_2"], (O_V, 512)), 0, 512)
    flow_grans(cols_unit(w["w_in_2"], (O_G, 512)), 0, 512)
    turn_grans(cols_unit(w["w_in_2"], (O_LG, 512)), range(4))
    G_WO2 = len(grans)
    for c in (0, 4):
        row_grans(rows_unit(w["w_out_2"], c, 4), [None] * 4)
    G_FF = len(grans)
    GU, GO = {}, {}

    def ffn_in(j):
        u = cols_unit(w["w_ffn_in_2"], (256 * j, 256), (FF2 + 256 * j, 256))
        for f in range(2):
            turn_grans(u, (f, 2 + f))
            GU[2 * j + f] = len(grans) - 1

    def ffn_out(f0, n):
        row_grans(rows_unit(w["w_ffn_out_2"], f0, n), [None] * n)
        for i in range(n):
            GO[f0 + i] = len(grans) - n + i

    for j in range(FC // 2):
        ffn_in(j)
        if j >= 2 and j % 2 == 0 and j < FC // 2 - 1:
            ffn_out(2 * j - 4, 4)
    ffn_out(16, 4)
    ffn_out(20, 2)
    GEND = len(grans)
    assert (UA, GA) == (15, 60) and sorted(GO) == list(range(FC)), sorted(GO)

    ld_x = sem("ld_x")
    ld_par = sem("ld_par")
    landed = [sem(f"landed{s}") for s in range(SLOTS)]
    const_ready = sem("const_ready")
    split_hi = sem("split_hi")
    split_lo = sem("split_lo")
    gran_used = sem("gran_used")
    landed_c = [sem(f"landed_c{s}") for s in range(SLOTS)]
    dve_chain = sem("dve_chain")
    act_chain = sem("act_chain")
    pool_chain = sem("pool_chain")
    par_turned = sem("par_turned")
    par_ready = sem("par_ready")
    ss_act = sem("ss_act")
    ms_ready = sem("ms_ready")
    rstd_ready = sem("rstd_ready")
    nrm_dve = sem("nrm_dve")
    nrm_act = sem("nrm_act")
    turned = sem("turned")
    turn_hi = sem("turn_hi")
    turn_lo = sem("turn_lo")
    xbc_copied = sem("xbc_copied")
    conv_done = sem("conv_done")
    silu_done = sem("silu_done")
    x_turned = sem("x_turned")
    x_kept = sem("x_kept")
    narrow_hi = sem("narrow_hi")
    narrow_lo = sem("narrow_lo")
    dt_raw = sem("dt_raw")
    dt_ready = sem("dt_ready")
    ef_raw = sem("ef_raw")
    ef_ready = sem("ef_ready")
    cb_raw = sem("cb_raw")
    cb_ready = sem("cb_ready")
    xdt_ready = sem("xdt_ready")
    skip_ready = sem("skip_ready")
    seg_lhs = sem("seg_lhs")
    seg_raw = sem("seg_raw")
    seg_exp = sem("seg_exp")
    seg_m = sem("seg_m")
    y_raw = sem("y_raw")
    y_kept = sem("y_kept")
    xdt_decayed = sem("xdt_decayed")
    yoff_raw = sem("yoff_raw")
    yoff_kept = sem("yoff_kept")
    z_kept = sem("z_kept")
    zy_ready = sem("zy_ready")
    ssd_ss = sem("ssd_ss")
    ssd_ms = sem("ssd_ms")
    ssd_rstd = sem("ssd_rstd")
    ssd_norm = sem("ssd_norm")
    ssd_turned = sem("ssd_turned")
    ssd_hi = sem("ssd_hi")
    ssd_lo = sem("ssd_lo")
    c_kept = sem("c_kept")
    v_used = sem("v_used")
    b_used = sem("b_used")
    sc_sq = sem("sc_sq")
    sc_sum = sem("sc_sum")
    sc_sqrt = sem("sc_sqrt")
    sc_scaled = sem("sc_scaled")
    sc_hi = sem("sc_hi")
    sc_lo = sem("sc_lo")
    res_mix = sem("res_mix")
    stored = sem("stored")

    ld_fgain = sem("ld_fgain")
    lt_ready = sem("lt_ready")
    tok_turned = sem("tok_turned")
    tok_act = sem("tok_act")
    tok_dve = sem("tok_dve")
    logits_raw = sem("logits_raw")
    member = sem("member")
    rank_raw = sem("rank_raw")
    diag_ready = sem("diag_ready")
    rows_raw = sem("rows_raw")
    routed = sem("routed")
    built = sem("built")
    xt_raw = sem("xt_raw")
    xt_kept = sem("xt_kept")
    gu_raw = sem("gu_raw")
    gate_silu = sem("gate_silu")
    h_ready = sem("h_ready")
    ht_raw = sem("ht_raw")
    ht_kept = sem("ht_kept")
    ye_raw = sem("ye_raw")
    ye_act = sem("ye_act")
    ye_dve = sem("ye_dve")
    moe_raw = sem("moe_raw")
    moe_added = sem("moe_added")
    res_moe = sem("res_moe")
    res_mid = sem("res_mid")

    lam_ready = sem("lam_ready")
    c_const = sem("c_const")
    c_mask = sem("c_mask")
    ld_c = sem("ld_c")
    ld_gain2 = sem("ld_gain2")
    z_raw = sem("z_raw")
    zsb_kept = sem("zsb_kept")
    zt_raw = sem("zt_raw")
    zt_kept = sem("zt_kept")
    zf_raw = sem("zf_raw")
    zf_kept = sem("zf_kept")
    zf_log = sem("zf_log")
    la_ready = sem("la_ready")
    suffix_raw = sem("suffix_raw")
    decay_exp = sem("decay_exp")
    kdec_ready = sem("kdec_ready")
    lx_copied = sem("lx_copied")
    lx_ready = sem("lx_ready")
    lg_raw = sem("lg_raw")
    lg_sig = sem("lg_sig")
    l_tanh = sem("l_tanh")
    l_neg = sem("l_neg")
    l_sqrt = sem("l_sqrt")
    lru_scan = sem("lru_scan")
    lgate_kept = sem("lgate_kept")
    lru_prod = sem("lru_prod")
    lru_hi = sem("lru_hi")
    lru_lo = sem("lru_lo")
    q_kept = sem("q_kept")
    k_kept = sem("k_kept")
    v_kept = sem("v_kept")
    g_kept = sem("g_kept")
    g_gain = sem("g_gain")
    upd_raw = sem("upd_raw")
    st_ready = sem("st_ready")
    o_raw = sem("o_raw")
    o_sq = sem("o_sq")
    o_ms = sem("o_ms")
    o_rstd = sem("o_rstd")
    gla_ready = sem("gla_ready")
    gla_turned = sem("gla_turned")
    gla_hi = sem("gla_hi")
    gla_lo = sem("gla_lo")
    res_mix2 = sem("res_mix2")
    f_silu = sem("f_silu")
    f_prod = sem("f_prod")
    f_hi = sem("f_hi")
    f_lo = sem("f_lo")
    res_ffn = sem("res_ffn")
    out_ready = sem("out_ready")

    exp_ready = sem("exp_ready")

    neg_abs = sem("neg_abs")

    margin = sem("margin")

    neg_half = sm[:, 8:24]
    N_SMALL = len(PROWS) + 3 + 2 + 1 + NG + 2

    def counter(semaphore):
        n = [0]

        def link(eng, ins):
            n[0] += 1
            ins.then_inc(semaphore, 1)
            eng.wait_ge(semaphore, n[0])
        return link

    link_dve, link_act, link_pool = counter(dve_chain), counter(act_chain), counter(pool_chain)

    def norm_act(act, n, src, dst):
        nc.scalar.activation(dst[:, 0, :], src[:, 0, :], ACT.Square, accum_out=sm[:, 0:1]).then_inc(ss_act, 1)
        act.wait_ge(rstd_ready, n + 1)
        nc.scalar.activation(dst[:, 1, :], src[:, 1, :], ACT.Copy, scale=sm[:, 5:6]).then_inc(nrm_act, 1)

    def norm_dve(dve, n, src, dst):
        link_dve(dve, nc.vector.tensor_tensor_reduce(
            out=dst[:, 1, :], in0=src[:, 1, :], in1=src[:, 1, :], scale=1.0, scalar=0.0,
            op0=ALU.mult, op1=ALU.add, accum_out=sm[:, 1:2]))
        dve.wait_ge(ss_act, n + 1)
        nc.vector.tensor_scalar(sm[:, 2:4], sm[:, 0:2], 1.0 / D, EPS, ALU.mult, ALU.add).then_inc(ms_ready, 1)
        dve.wait_ge(rstd_ready, n + 1)
        nc.vector.tensor_scalar(dst[:, 0, :], src[:, 0, :], sm[:, 4:5], None, ALU.mult).then_inc(nrm_dve, 1)

    def norm_pool(pool, n):
        pool.wait_ge(ms_ready, n + 1)
        nc.gpsimd.tensor_tensor(sm[:, 4:6], sm[:, 2:4], neg_half[:, 0:2], ALU.pow).then_inc(rstd_ready, 1)

    def turn_pe(pe, n, t, src):
        pe.wait_ge(nrm_act, n + 1)
        pe.wait_ge(nrm_dve, n + 1)
        for c in range(KC):
            if c >= 4:
                pe.wait_ge(turn_lo, KC * t + c - 3)
            for b in range(TB):
                mm = nc.tensor.transpose(bank[c % 4][:, b * P:(b + 1) * P], src[:, b, c * P:(c + 1) * P], ident[:, :])
            mm.then_inc(turned, 1)

    def turn_act(act, t, gain):
        for c in range(KC):
            act.wait_ge(turned, KC * t + c + 1)
            nc.scalar.activation(act_p[:, 0, c, :], bank[c % 4][:, 0:T], ACT.Copy,
                                 scale=pcol(gain, c)).then_inc(turn_hi, 1)

    def turn_dve(dve, t, gain):
        for c in range(KC):
            dve.wait_ge(turn_hi, KC * t + c + 1)
            nc.vector.scalar_tensor_tensor(out=act_p[:, 1, c, :], in0=bank[c % 4][:, 0:T], scalar=pcol(gain, c),
                                           in1=act_p[:, 0, c, :].bitcast(F32), op0=ALU.mult,
                                           op1=ALU.subtract).then_inc(turn_lo, 1)

    def parts(tile, g, view):
        if len(view.shape) == 2:
            return tile[:, g % 2, :]
        return tile[:, g % 2, :].rearrange("p (k n) -> p k n", k=view.shape[1])

    def landed_wait(eng, g):
        u = grans[g][0]
        if g == 0 or grans[g - 1][0] != u:
            eng.wait_ge(*unit_landed(u))

    def unit_landed(u):
        if u < UA:
            return landed[u % SLOTS], 16 * PARTS_OF[u]
        return landed_c[u % SLOTS], 16 * PARTS_OF[u]

    def hi(act, g):
        u, view, gain = grans[g]
        landed_wait(act, g)
        if g >= 2:
            act.wait_ge(gran_used, g - 1)
        if gain is None:
            nc.scalar.activation(parts(w_hi, g, view), view, ACT.Copy).then_inc(split_hi, 1)
        else:
            nc.scalar.activation(parts(w_hi, g, view), view, ACT.Copy, scale=gain).then_inc(split_hi, 1)

    def lo(dve, g):
        u, view, gain = grans[g]
        landed_wait(dve, g)
        dve.wait_ge(split_hi, g + 1)
        h = parts(w_hi, g, view).bitcast(F32)
        if gain is None:
            nc.vector.tensor_tensor(parts(w_lo, g, view), view, h, ALU.subtract).then_inc(split_lo, 1)
        else:
            nc.vector.scalar_tensor_tensor(out=parts(w_lo, g, view), in0=view, scalar=gain, in1=h,
                                           op0=ALU.mult, op1=ALU.subtract).then_inc(split_lo, 1)

    PASSES = ((w_hi, 0), (w_hi, 1), (w_lo, 0))

    def turn_gran(pe, g, dst, a):
        pe.wait_ge(split_lo, g + 1)
        pe.wait_ge(split_hi, g + 1)
        for k in range(KC):
            for i, (wt, x_part) in enumerate(PASSES):
                mm = nc.tensor.matmul(dst, parts(wt, g, grans[g][1])[:, k, :], a[:, x_part, k, :],
                                      start=(k == 0 and i == 0), stop=(k == KC - 1 and i == 2))
        mm.then_inc(gran_used, 1)

    def flow_gran(pe, g, dsts, a, k0):
        pe.wait_ge(split_lo, g + 1)
        pe.wait_ge(split_hi, g + 1)
        kn = grans[g][1].shape[1]
        for k in range(kn):
            for b in range(TB):
                for i, (wt, x_part) in enumerate(PASSES):
                    mm = nc.tensor.matmul(dsts[b], a[:, x_part, k0 + k, b * P:(b + 1) * P],
                                          parts(wt, g, grans[g][1])[:, k, :],
                                          start=(k0 + k == 0 and i == 0), stop=(k0 + k == KC - 1 and i == 2))
        mm.then_inc(gran_used, 1)

    def row_gran(pe, g, banks, a_chunk, first, last):
        pe.wait_ge(split_lo, g + 1)
        pe.wait_ge(split_hi, g + 1)
        for b in range(TB):
            for half in range(2):
                for i, (wt, x_part) in enumerate(PASSES):
                    mm = nc.tensor.matmul(banks[2 * b + half][:, :], a_chunk[:, x_part, b * P:(b + 1) * P],
                                          wt[:, g % 2, half * 512:(half + 1) * 512],
                                          start=(first and i == 0), stop=(last and i == 2))
        mm.then_inc(gran_used, 1)

    def add_res(dve, banks, done):
        for b in range(TB):
            for half in range(2):
                r = res[:, b, half * 512:(half + 1) * 512]
                ins = nc.vector.tensor_tensor(r, r, banks[2 * b + half][:, :], ALU.add)
        ins.then_inc(done, 1)

    def small(i, n):
        return adt[:, i, :, :]

    def log1p_dve(dve, e, u, u2, q, dst, add):
        link_dve(dve, nc.vector.tensor_scalar(u, e, 2.0, None, ALU.add))
        link_dve(dve, nc.vector.reciprocal(u, u))
        link_dve(dve, nc.vector.tensor_tensor(u, u, e, ALU.mult))
        link_dve(dve, nc.vector.tensor_tensor(u2, u, u, ALU.mult))
        link_dve(dve, nc.vector.tensor_scalar(q, u2, 1.0 / 15, None, ALU.mult))
        for n in (13, 11, 9, 7, 5, 3):
            link_dve(dve, nc.vector.scalar_tensor_tensor(out=q, in0=q, scalar=1.0 / n, in1=u2, op0=ALU.add,
                                                         op1=ALU.mult))
        link_dve(dve, nc.vector.scalar_tensor_tensor(out=q, in0=q, scalar=1.0, in1=u, op0=ALU.add, op1=ALU.mult))
        if add is None:
            link_dve(dve, nc.vector.tensor_scalar(dst, q, 2.0, None, ALU.mult))
        else:
            link_dve(dve, nc.vector.scalar_tensor_tensor(out=dst, in0=q, scalar=2.0, in1=add, op0=ALU.mult,
                                                         op1=ALU.add))

    PARTS_OF = []
    uses = [0] * SLOTS
    for u in range(UA):
        uses[u % SLOTS] += len(units[u])
        PARTS_OF.append(uses[u % SLOTS])

    uses_c = [0] * SLOTS
    for u in range(UA, len(units)):
        uses_c[u % SLOTS] += len(units[u])
        PARTS_OF.append(uses_c[u % SLOTS])

    last_gran = {}
    for g, (u, _, _) in enumerate(grans):
        last_gran[u] = g

    E_SLOT = (3, 0)
    M_BANK = (1, 3, 7, 1)
    E_LANDED = [16 * n for n in uses]

    block = ctx.enter_context(nc.Block())

    @block.sync
    def _(sp):
        sp.dma_start(res[:, :, :], x.rearrange("(b p) d -> p b d", p=P)).then_inc(ld_x, 16)
        for u in range(UA):
            if u >= SLOTS:
                sp.wait_ge(split_hi, last_gran[u - SLOTS] + 1)
                sp.wait_ge(split_lo, last_gran[u - SLOTS] + 1)
            for dst, src in units[u]:
                sp.dma_start(dst, src).then_inc(landed[u % SLOTS], 16)

        def load_expert(x, e, of_pair, free):
            s = E_SLOT[of_pair]
            for n, name in enumerate(("w_gate", "w_up", "w_down")):
                if free is not None and n != 1:
                    sp.wait_ge(gu_raw if n == 0 else ye_raw, free)
                k = KC if n < 2 else FF // P
                sp.dma_start(ring[:, s + n, :].rearrange("p (k n) -> p k n", k=k),
                             w[name][e].rearrange("(k p) n -> p k n", p=P)).then_inc(landed[s + n], 16)

        for i in range(2):
            for s in range(3):
                u = max(u for u in range(UA) if u % SLOTS == E_SLOT[i] + s)
                sp.wait_ge(split_hi, last_gran[u] + 1)
                sp.wait_ge(split_lo, last_gran[u] + 1)
            load_expert(i, i, i, None)
        with sp.Fori(1, NE // 2) as j:
            for i in range(2):
                load_expert(2 * j + i, 2 * j + i, i, 2 * j + i - 1)
        sp.wait_ge(routed, 1)
        n_rounds = sp.value_load(rounds_i[0:1, 0:1], min_val=1, max_val=T // CAP)
        with sp.If(n_rounds > 1):
            with sp.Fori(1, n_rounds) as r:
                with sp.Fori(0, NE // 2) as j:
                    for i in range(2):
                        load_expert(0, 2 * j + i, i, NE * r + 2 * j + i - 1)
        before_last = sp.value_load(rounds_i[0:1, 1:2], min_val=NE - 1, max_val=NE * T // CAP - 1)
        for u in range(UA, len(units)):
            s = u % SLOTS
            if u < UA + SLOTS:
                sp.wait_ge(ye_raw if s % 3 == 2 else gu_raw, before_last if s >= 3 else before_last + 1)
            else:
                sp.wait_ge(split_hi, last_gran[u - SLOTS] + 1)
                sp.wait_ge(split_lo, last_gran[u - SLOTS] + 1)
            for dst, src in units[u]:
                sp.dma_start(dst, src).then_inc(landed_c[s], 16)
        for b in range(TB):
            sp.wait_ge(out_ready, b + 1)
            sp.dma_start(out[b * P:(b + 1) * P, :], nrm[:, b, :]).then_inc(stored, 16)
        sp.wait_ge(stored, 16 * TB)

    @block.gpsimd
    def _(pool):
        def mask(tile, op, step, mult, base=0):
            link_pool(pool, nc.gpsimd.memset(tile, 1.0))
            link_pool(pool, nc.gpsimd.affine_select(out=tile, in_=tile, compare_op=op, fill=0.0, base=base,
                                                    pattern=[[step, P]], channel_multiplier=mult))
        nc.gpsimd.memset(neg_half, -0.5)
        mask(ident[:, :], ALU.is_equal, 1, -1)
        nc.gpsimd.memset(ones[:, :], 1.0)
        nc.gpsimd.iota(iota_f[:, :], pattern=[[1, P]], base=0, channel_multiplier=0,
                       allow_small_or_imprecise_dtypes=True)
        nc.gpsimd.iota(iota_p[:, :], pattern=[[0, 1]], base=0, channel_multiplier=1,
                       allow_small_or_imprecise_dtypes=True)
        nc.gpsimd.memset(pad[:, :, 0:3], 0.0).then_inc(const_ready, 1)
        norm_pool(pool, 0)
        mask(m_le[:, :], ALU.is_ge, 1, -1)
        mask(m_gt[:, :], ALU.is_gt, -1, 1)
        link_pool(pool, nc.gpsimd.memset(blk64[:, :], 1.0))
        v = blk64[:, :].rearrange("p (a j) -> p a j", a=2)
        link_pool(pool, nc.gpsimd.affine_select(out=v, in_=v, compare_op=ALU.is_ge, fill=0.0, base=0,
                                                pattern=[[-64, 2], [0, 64]], channel_multiplier=1))
        nc.gpsimd.affine_select(out=v, in_=v, compare_op=ALU.is_ge, fill=0.0, base=63,
                                pattern=[[64, 2], [0, 64]], channel_multiplier=-1).then_inc(const_ready, 1)

        def seg_left(it):
            b, q = divmod(it, 4)
            if it == 0:
                pool.wait_ge(dt_ready, 1)
                pool.wait_ge(par_turned, 1)
            else:
                pool.wait_ge(seg_raw, it)
            nc.gpsimd.tensor_tensor(seg_l[:, :, :], bcast(m_gt[:, :].unsqueeze(1), [P, 4, P]),
                                    bcast(adt[:, 0, b, 4 * q:4 * q + 4].unsqueeze(2), [P, 4, P]),
                                    ALU.mult).then_inc(seg_lhs, 1)
        seg_left(0)
        pool.wait_ge(xdt_ready, 1)
        for b in range(TB):
            v = x_tok[:, b, :].rearrange("p (h d) -> p h d", h=HEADS)
            ins = nc.gpsimd.tensor_tensor(v, v, bcast(bc16[:, 2, :].unsqueeze(2), [P, HEADS, HD]), ALU.mult)
            if b == 0:
                seg_left(1)
        ins.then_inc(skip_ready, 1)
        for it in range(2, 5):
            seg_left(it)
        pool.wait_ge(y_raw, 4)
        v = xdt[:, 0, :].rearrange("p (h d) -> p h d", h=HEADS)
        pool.wait_ge(ef_ready, 1)
        nc.gpsimd.tensor_tensor(v, v, bcast(ef[:, 0, :].unsqueeze(2), [P, HEADS, HD]),
                                ALU.mult).then_inc(xdt_decayed, 1)
        for it in range(5, 8):
            seg_left(it)
        for n in range(4):
            pool.wait_ge(ssd_ms, n + 1)
            nc.gpsimd.tensor_tensor(sm[:, 32 + n:33 + n], sm[:, 28 + n:29 + n], neg_half[:, 0:1],
                                    ALU.pow).then_inc(ssd_rstd, 1)
        pool.wait_ge(res_mix, 1)
        link_pool(pool, nc.gpsimd.memset(m_lt[:, :], 1.0))
        nc.gpsimd.affine_select(out=m_lt[:, :], in_=m_lt[:, :], compare_op=ALU.is_gt, fill=0.0, base=0,
                                pattern=[[1, P]], channel_multiplier=-1).then_inc(lt_ready, 1)
        norm_pool(pool, 1)
        norm_pool(pool, 2)
        pool.wait_ge(res_mid, 1)
        nc.gpsimd.memset(lru_w[:, :, :, :], 0.0).then_inc(c_const, 1)
        norm_pool(pool, 3)
        link_pool(pool, nc.gpsimd.memset(lpad[:, :, 0:3], 0.0))
        link_pool(pool, nc.gpsimd.memset(z_t[:, :], 1.0))
        link_pool(pool, nc.gpsimd.tensor_tensor(m_gtc[:, :], m_gt[:, :], blk64[:, :], ALU.mult))
        nc.gpsimd.memset(sm[:, 64:65], 1.0).then_inc(c_mask, 1)
        pool.wait_ge(o_ms, 1)
        nc.gpsimd.tensor_tensor(sm[:, 56:64], sm[:, 48:56], neg_half[:, 0:8], ALU.pow).then_inc(o_rstd, 1)
        norm_pool(pool, 4)
        norm_pool(pool, 5)

    @block.scalar
    def _(act):
        for name, tile, row, n in PROWS:
            v = w[name]
            v = v.rearrange("a (c j) -> (a c) j", j=P) if len(v.shape) == 2 else v.rearrange("(c j) -> c j", j=P)
            act.dma_start(prow[row:row + n, tile, :], v).then_inc(ld_par, 16)
        for i, name in enumerate(("dt_bias", "a_log", "d_skip")):
            act.dma_start(bc16[:, i, :], w[name].partition_broadcast(P)).then_inc(ld_par, 16)
        act.dma_start(w_dt[:, :, :], w["w_in"].rearrange("(k p) n -> p k n", p=P)[:, :, O_DT:O_DT + HEADS])\
           .then_inc(ld_par, 16)
        act.dma_start(w_z[:, :, :], w["w_in_2"].rearrange("(k p) n -> p k n", p=P)[:, :, O_Z:O_Z + RANK])\
           .then_inc(ld_par, 16)
        act.dma_start(w_rt[:, :, 0:NG], w["w_router_group"].rearrange("(k p) g -> p k g", p=P)).then_inc(ld_par, 16)
        for g in range(NG):
            act.dma_start(w_rt[:, :, NG + g * EPG:NG + (g + 1) * EPG],
                          w["w_router_expert"][g].rearrange("(k p) e -> p k e", p=P)).then_inc(ld_par, 16)
        act.dma_start(w_al[0:RANK, :], w["gla_w_alpha_2"]).then_inc(ld_par, 16)
        act.dma_start(w_al[RANK:RANK + 1, :], w["gla_b_alpha_2"].unsqueeze(0)).then_inc(ld_par, 16)

        act.wait_ge(ld_x, 16)
        norm_act(act, 0, res, xdt)
        act.wait_ge(par_turned, 1)
        nc.scalar.activation(par[:, 0:ROWS_A], bank[4][:, 0:ROWS_A], ACT.Copy)
        nc.scalar.activation(par[:, P:P + ROWS_B], bank[4][:, P:P + ROWS_B], ACT.Copy).then_inc(par_ready, 1)
        act.wait_ge(par_ready, 1)
        act.wait_ge(neg_abs, 1)
        nc.scalar.activation(sp4[:, 1, :], sp4[:, 0, :], ACT.Exp).then_inc(exp_ready, 1)
        turn_act(act, 0, "norm_mix")

        def copy_xbc(i):
            act.wait_ge(gran_used, i + 1)
            if i >= 2:
                act.wait_ge(conv_done, i - 1)
            nc.scalar.activation(pad[:, i % 2, 3:T + 3], bank[i % 4][:, 0:T], ACT.Copy).then_inc(xbc_copied, 1)

        def silu_xbc(i):
            act.wait_ge(conv_done, i + 1)
            dst = cv[:, i % 2, :] if i < KC else bc_t[:, i - KC, :]
            nc.scalar.activation(dst, cv[:, i % 2, :], ACT.Silu, bias=pcol("ssd_conv_b", i)).then_inc(silu_done, 1)

        def keep_x(i):
            act.wait_ge(x_turned, i + 1)
            src = bank[4 + i % 2][:, 0:T].rearrange("p (b c) -> p b c", b=TB)
            nc.scalar.activation(x_tok[:, :, i * P:(i + 1) * P], src, ACT.Copy).then_inc(x_kept, 1)

        def keep_z(t):
            act.wait_ge(gran_used, G_Z + 4 * t + 4)
            for b in range(TB):
                nc.scalar.activation(z_tok[:, b, t * 512:(t + 1) * 512], bank[2 * t + b][:, :],
                                     ACT.Silu).then_inc(z_kept, 1)

        def exp_seg(it):
            act.wait_ge(seg_raw, it + 1)
            if it >= 2:
                act.wait_ge(y_raw, it - 1)
            nc.scalar.activation(seg_e[:, it % 2, :, :], bank[5][:, :].rearrange("p (h l) -> p h l", h=4),
                                 ACT.Exp).then_inc(seg_exp, 1)

        def keep_c(hf, j):
            act.wait_ge(gran_used, G_SC + 12 * hf + j + 1)
            if hf:
                act.wait_ge(sc_lo, 1)
            nc.scalar.activation(sc_t[:, j, :], bank[j][:, 0:T], ACT.Copy).then_inc(c_kept, 1)

        def square_sc(hf, j):
            act.wait_ge(b_used, 4 * hf + j + 1)
            if 4 * hf + j >= 2:
                act.wait_ge(sc_sum, 4 * hf + j - 1)
            nc.scalar.activation(cv[:, j % 2, :], sc_t[:, j, :], ACT.Square).then_inc(sc_sq, 1)

        def sqrt_sc(hf):
            act.wait_ge(sc_sum, 4 * hf + 4)
            for n, bk in enumerate((bank[4], bank[7])):
                nc.scalar.activation(bk[:, :], bk[:, :], ACT.Sqrt, scale=1.0 / 64, bias=sm[:, 24:25])\
                  .then_inc(sc_sqrt, 1)

        def hi_sc(hf):
            act.wait_ge(sc_scaled, hf + 1)
            nc.scalar.activation(act_q[:, 0, 4 * hf:4 * hf + 4, :], sc_t[:, :, :], ACT.Copy).then_inc(sc_hi, 1)

        def square_y(n):
            b, g = divmod(n, GROUPS)
            act.wait_ge(zy_ready, n + 1)
            nc.scalar.activation(x_tok[:, b, g * GW:(g + 1) * GW], z_tok[:, b, g * GW:(g + 1) * GW], ACT.Square,
                                 accum_out=sm[:, 36 + n:37 + n]).then_inc(ssd_ss, 1)

        def hi_ssd(n):
            b, g = divmod(n, GROUPS)
            act.wait_ge(ssd_turned, n + 1)
            nc.scalar.activation(act_p[:, 0, 4 * g:4 * g + 4, b * P:(b + 1) * P],
                                 bank[5 + n % 2][:, :].rearrange("p (c t) -> p c t", c=4), ACT.Copy)\
              .then_inc(ssd_hi, 1)

        for g in range(GA):
            hi(act, g)
            if g == 0:
                nc.scalar.activation(ws_hi[:, :, :], w_dt[:, :, :], ACT.Copy).then_inc(narrow_hi, 1)
            if 2 <= g < 2 + XC:
                copy_xbc(g - 2)
            if 3 <= g < 3 + XC:
                silu_xbc(g - 3)
            if 5 <= g < 5 + KC:
                keep_x(g - 5)
            if g == G_Z + 4:
                act.wait_ge(neg_abs, 2)
                nc.scalar.activation(adt[:, 3, :, :], adt[:, 2, :, :], ACT.Exp).then_inc(exp_ready, 1)
                act.wait_ge(ld_par, 16 * N_SMALL)
                nc.scalar.activation(adt[:, 6, 0, :], bc16[:, 1, :], ACT.Exp).then_inc(exp_ready, 1)
            if g == G_Z + 5:
                keep_z(0)
            if g == G_Z + 9:
                keep_z(1)
                act.wait_ge(ef_raw, 1)
                nc.scalar.activation(ef[:, :, :], bank[7][:, 0:2 * HEADS].rearrange("p (a h) -> p a h", a=2),
                                     ACT.Exp).then_inc(ef_ready, 1)
            if G_SC + 2 <= g < G_SC + 18 and g % 2 == 0:
                exp_seg((g - G_SC - 2) // 2)
            for hf in range(2):
                base = G_SC + 12 * hf
                if hf == 0 and base + 2 <= g < base + 6:
                    keep_c(0, g - base - 2)
                if base + 11 <= g < base + 15:
                    square_sc(hf, g - base - 11)
                if g == base + 15:
                    sqrt_sc(hf)
            if g == G_SC + 16:
                hi_sc(0)
                for j in range(4):
                    keep_c(1, j)
            if g == G_WO:
                for n in range(4):
                    square_y(n)
            if g == G_WO + 2:
                for n in range(4):
                    hi_ssd(n)
            if g == G_WO + 4:
                hi_sc(1)

        act.wait_ge(res_mix, 1)
        act.dma_start(fgain[:, :], w["final_norm"].partition_broadcast(P)).then_inc(ld_fgain, 16)
        norm_act(act, 1, res, tok)
        for c in range(0, KC, 2):
            act.wait_ge(tok_turned, c + 1)
            nc.scalar.activation(tok_t[:, c, :], bank[c % 4][:, 0:T], ACT.Copy,
                                 scale=pcol("norm_ffn", c)).then_inc(tok_act, 1)
        act.wait_ge(margin, 1)
        nc.scalar.activation(r8[:, 5, :, 0:NG], r8[:, 4, :, 0:NG], ACT.Exp).then_inc(exp_ready, 1)
        act.wait_ge(margin, 2)
        nc.scalar.activation(r1[:, 5, :], r1[:, 4, :], ACT.Exp).then_inc(exp_ready, 1)
        act.wait_ge(routed, 1)
        n_rounds = act.value_load(rounds_i[0:1, 0:1], min_val=1, max_val=T // CAP)

        def expert_act(x, e):
            act.wait_ge(gu_raw, x + 1)
            nc.scalar.activation(h_e[:, :], bank[0][:, 0:P], ACT.Silu).then_inc(gate_silu, 1)
            act.wait_ge(ht_raw, x + 1)
            nc.scalar.activation(h_t[:, :], bank[4][:, 0:P], ACT.Copy).then_inc(ht_kept, 1)
            act.wait_ge(ye_raw, x + 1)
            for j in range(2):
                ins = nc.scalar.activation(y_e[CAP * e:CAP * (e + 1), 256 * j:256 * (j + 1)],
                                           bank[2][CAP * j:CAP * (j + 1), 0:256], ACT.Copy)
            ins.then_inc(ye_act, 1)

        with act.Fori(0, n_rounds) as r:
            with act.Fori(0, NE // 4) as k:
                for e in range(4):
                    expert_act(NE * r + 4 * k + e, e)
        act.wait_ge(res_moe, 1)
        norm_act(act, 2, res, tok)

        act.wait_ge(c_const, 1)
        for n, name in enumerate(("lru_wa_2", "lru_wi_2")):
            for q in range(2):
                lo_, hi_ = 64 * q, 64 * q + 64
                act.dma_start(lru_w[lo_:hi_, n, :, lo_:hi_],
                              w[name].rearrange("(c q) i j -> q i c j", q=2)[q]).then_inc(ld_c, 16)
        act.dma_start(gnorm[:, :], w["gla_norm_2"].partition_broadcast(P)).then_inc(ld_c, 16)
        norm_act(act, 3, res, nrm)
        nc.scalar.activation(ws_hi[:, :, :], w_z[:, :, :], ACT.Copy).then_inc(narrow_hi, 1)
        for g in range(GA, GA + 2):
            hi(act, g)
        turn_act(act, 1, "norm1_2")
        li = lpad[:, :, 0:T]
        t1 = st[:, 0:2, :, :].rearrange("p n c d -> p n (c d)")

        def sigmoids(c):
            act.wait_ge(lg_raw, c + 1)
            nc.scalar.activation(lr[:, c, :], bank[4 + c % 2][:, 0:T], ACT.Sigmoid, bias=pcol("lru_ba_2", c))
            nc.scalar.activation(li[:, c, :], bank[4 + c % 2][:, T:2 * T], ACT.Sigmoid,
                                 bias=pcol("lru_bi_2", c)).then_inc(lg_sig, 1)

        for g in range(GA + 2, G_FF):
            hi(act, g)
            if g == GA + 2:
                act.wait_ge(z_raw, 1)
                nc.scalar.activation(z_sb[:, :, :], bank[6][:, 0:TB * RANK].rearrange("p (b n) -> p b n", b=TB),
                                     ACT.Copy).then_inc(zsb_kept, 1)
                act.wait_ge(c_mask, 1)
            if g == GA + 3:
                act.wait_ge(zt_raw, 1)
                nc.scalar.activation(z_t[0:RANK, :], bank[7][0:RANK, 0:T], ACT.Copy).then_inc(zt_kept, 1)
            if GA + 2 <= g < GA + 6:
                c = g - GA - 2
                act.wait_ge(gran_used, GA + c + 1)
                nc.scalar.activation(lpad[:, c, 3:T + 3], bank[c][:, 0:T], ACT.Copy).then_inc(lx_copied, 1)
            if g == GA + 5:
                act.wait_ge(zf_raw, 1)
                nc.scalar.activation(la[:, :, :], bank[6][:, :].rearrange("p (b n) -> p b n", b=TB),
                                     ACT.Copy).then_inc(zf_kept, 1)
            if g == GA + 6:
                act.wait_ge(neg_abs, 3)
                link_act(act, nc.scalar.activation(t1, t1, ACT.Exp))
                nc.scalar.activation(t1, t1, ACT.Ln, bias=1.0).then_inc(zf_log, 1)
            if g in (G_Q + 2, G_Q + 3):
                c = g - G_Q - 2
                act.wait_ge(gran_used, G_Q + c + 1)
                nc.scalar.activation(q_t[:, c, :], bank[c][:, 0:T], ACT.Copy, scale=0.125).then_inc(q_kept, 1)
            if g == GA + 7:
                sigmoids(0)
                sigmoids(1)
            if g == GA + 9:
                act.wait_ge(gran_used, G_K + 2)
                for b in range(TB):
                    ins = nc.scalar.activation(k_tok[:, b, :], bank[2 + b][:, 0:256], ACT.Copy)
                ins.then_inc(k_kept, 1)
                act.wait_ge(suffix_raw, 1)
                act.wait_ge(la_ready, 1)
                nc.scalar.activation(t1, bank[6][:, :].rearrange("p (b n) -> p b n", b=TB), ACT.Exp,
                                     scale=1.0 / 16)
                nc.scalar.activation(dec[:, :, :], bank[7][:, 0:8].rearrange("p (c n) -> p c n", c=2), ACT.Exp,
                                     scale=1.0 / 16).then_inc(decay_exp, 1)
            if g == GA + 10:
                sigmoids(2)
                sigmoids(3)
                act.wait_ge(lg_sig, 4)
                act.wait_ge(lam_ready, 1)
                for c in range(LC):
                    ins = nc.scalar.activation(lr[:, c, :], lr[:, c, :], ACT.Tanh, scale=sp4[:, 7, c:c + 1])
                ins.then_inc(l_tanh, 1)
            if g == GA + 12:
                act.wait_ge(l_neg, 1)
                nc.scalar.activation(li, li, ACT.Sqrt).then_inc(l_sqrt, 1)
            if g == G_V + 5:
                act.wait_ge(gran_used, G_V + 4)
                for b in range(TB):
                    nc.scalar.activation(v_tok[:, b, :], bank[b][:, :], ACT.Copy).then_inc(v_kept, 1)
            if g == G_G + 5:
                act.wait_ge(gran_used, G_G + 4)
                for b in range(TB):
                    nc.scalar.activation(g_tok[:, b, :], bank[2 + b][:, :], ACT.Silu).then_inc(g_kept, 1)
            if G_LG + 2 <= g < G_LG + 6:
                c = g - G_LG - 2
                act.wait_ge(gran_used, G_LG + c + 1)
                nc.scalar.activation(lgate[:, c, :], bank[c][:, 0:T], ACT.Gelu_apprx_tanh).then_inc(lgate_kept, 1)
            if g == G_LG + 3:
                act.wait_ge(o_raw, 1)
                act.wait_ge(upd_raw, 1)
                for n in range(2):
                    nc.scalar.activation(v_tok[:, n, :], bank[4 + n][:, :], ACT.Square).then_inc(o_sq, 1)
            if G_LG + 4 <= g < G_LG + 8:
                c = g - G_LG - 4
                act.wait_ge(lru_prod, c + 1)
                nc.scalar.activation(act_q[:, 0, c, :], nrm[:, 1, c * T:(c + 1) * T], ACT.Copy).then_inc(lru_hi, 1)
            if g == G_WO2 + 4:
                for b in range(TB):
                    act.wait_ge(gla_turned, b + 1)
                    nc.scalar.activation(act_q[:, 0, 4:8, b * P:(b + 1) * P],
                                         bank[6 + b][:, :].rearrange("p (c t) -> p c t", c=4), ACT.Copy)\
                      .then_inc(gla_hi, 1)
        for g in range(G_FF, G_FF + 2):
            hi(act, g)
        act.wait_ge(res_mix2, 1)
        norm_act(act, 4, res, nrm)
        act.dma_start(fg2, w["final_norm_2"].partition_broadcast(P)).then_inc(ld_gain2, 16)
        turn_act(act, 2, "norm2_2")
        for g in range(G_FF + 2, GEND):
            hi(act, g)
            for f in range(FC):
                if g == GU[f] + 2:
                    act.wait_ge(gran_used, GU[f] + 1)
                    if f >= 4:
                        act.wait_ge(f_lo, f - 3)
                    nc.scalar.activation(lx[:, f % 4, :], bank[f % 4][:, 0:T], ACT.Silu).then_inc(f_silu, 1)
                if g == GU[f] + 3:
                    act.wait_ge(f_prod, f + 1)
                    if f >= 8:
                        act.wait_ge(gran_used, GO[f - 8] + 1)
                    nc.scalar.activation(act_q[:, 0, f % 8, :], lx[:, f % 4, :], ACT.Copy).then_inc(f_hi, 1)
        act.wait_ge(res_ffn, 1)
        norm_act(act, 5, res, nrm)

    @block.vector
    def _(dve):
        dve.wait_ge(ld_x, 16)
        dve.wait_ge(const_ready, 1)
        link_dve(dve, nc.vector.memset(sm[:, 24:25], EPS))
        norm_dve(dve, 0, res, xdt)
        dve.wait_ge(par_ready, 1)
        lam = par[:, PCOLS["lru_lambda_2"]:PCOLS["lru_lambda_2"] + LC]
        nc.vector.tensor_scalar(sp4[:, 6, :], lam, -1.0, 0.0, ALU.mult, ALU.max)
        nc.vector.scalar_tensor_tensor(out=sp4[:, 0, :], in0=lam, scalar=-1.0, in1=lam, op0=ALU.mult,
                                       op1=ALU.min).then_inc(neg_abs, 1)
        dve.wait_ge(exp_ready, 1)
        log1p_dve(dve, sp4[:, 1, :], sp4[:, 2, :], sp4[:, 3, :], sp4[:, 4, :], sp4[:, 5, :], sp4[:, 6, :])
        nc.vector.tensor_scalar(sp4[:, 7, :], sp4[:, 5, :], -4.0, None, ALU.mult).then_inc(lam_ready, 1)
        turn_dve(dve, 0, "norm_mix")

        def conv_xbc(i):
            dve.wait_ge(xbc_copied, i + 1)
            if 2 <= i < KC + 2:
                dve.wait_ge(x_turned, i - 1)
            elif i >= KC + 2:
                dve.wait_ge(silu_done, i - 1)
            for tap in range(4):
                wc = pcol("ssd_conv_w", tap * XC + i)
                src = pad[:, i % 2, tap:tap + T]
                if tap == 0:
                    link_dve(dve, nc.vector.tensor_scalar(cv[:, i % 2, :], src, wc, None, ALU.mult))
                    continue
                ins = nc.vector.scalar_tensor_tensor(out=cv[:, i % 2, :], in0=src, scalar=wc,
                                                     in1=cv[:, i % 2, :], op0=ALU.mult, op1=ALU.add)
                if tap < 3:
                    link_dve(dve, ins)
            ins.then_inc(conv_done, 1)

        def dt_chain():
            dve.wait_ge(dt_raw, 1)
            dve.wait_ge(ld_par, 16 * N_SMALL)
            link_dve(dve, nc.vector.tensor_tensor(
                adt[:, 1, :, :], bank[6][:, 0:2 * HEADS].rearrange("p (b h) -> p b h", b=TB),
                bcast(bc16[:, 0, :].unsqueeze(1), [P, TB, HEADS]), ALU.add))
            nc.vector.scalar_tensor_tensor(out=adt[:, 2, :, :], in0=adt[:, 1, :, :], scalar=-1.0,
                                           in1=adt[:, 1, :, :], op0=ALU.mult, op1=ALU.min).then_inc(neg_abs, 1)
            dve.wait_ge(neg_abs, 2)
            nc.vector.tensor_scalar(adt[:, 1, :, :], adt[:, 1, :, :], 0.0, None, ALU.max)
            dve.wait_ge(exp_ready, 2)
            log1p_dve(dve, adt[:, 3, :, :], adt[:, 4, :, :], adt[:, 5, :, :], adt[:, 2, :, :], adt[:, 7, :, :],
                      adt[:, 1, :, :])
            dve.wait_ge(exp_ready, 3)
            nc.vector.scalar_tensor_tensor(out=adt[:, 0, :, :], in0=adt[:, 7, :, :], scalar=-1.0,
                                           in1=bcast(adt[:, 6, 0, :].unsqueeze(1), [P, TB, HEADS]),
                                           op0=ALU.mult, op1=ALU.mult).then_inc(dt_ready, 1)

        def scale_x():
            dve.wait_ge(x_kept, KC)
            for b in range(TB):
                ins = nc.vector.tensor_tensor(xdt[:, b, :].rearrange("p (h d) -> p h d", h=HEADS),
                                              x_tok[:, b, :].rearrange("p (h d) -> p h d", h=HEADS),
                                              bcast(adt[:, 7, b, :].unsqueeze(2), [P, HEADS, HD]), ALU.mult)
            ins.then_inc(xdt_ready, 1)

        def keep_cb():
            for g in range(GROUPS):
                dve.wait_ge(cb_raw, g + 1)
                dve.wait_ge(const_ready, 2)
                bk = bank[5 + g]
                nc.vector.tensor_tensor(cbm[:, g, 0, :], bk[:, 0:P], m_le[:, :], ALU.mult)
                nc.vector.tensor_copy(cbm[:, g, 1, :], bk[:, P:2 * P])
                nc.vector.tensor_tensor(cbm[:, g, 2, :], bk[:, 2 * P:3 * P], m_le[:, :], ALU.mult)\
                  .then_inc(cb_ready, 1)

        def mask_seg(it):
            b, q = divmod(it, 4)
            dve.wait_ge(seg_exp, it + 1)
            if it == 0:
                dve.wait_ge(cb_ready, GROUPS)
            nc.vector.tensor_tensor(seg_e[:, it % 2, :, :], seg_e[:, it % 2, :, :],
                                    bcast(cbm[:, q // 2, 2 * b, :].unsqueeze(1), [P, 4, P]),
                                    ALU.mult).then_inc(seg_m, 1)

        def keep_y(n):
            b, g = divmod(n, GROUPS)
            dve.wait_ge(y_raw, 2 * n + 2)
            dve.wait_ge(skip_ready, 1)
            v = x_tok[:, b, g * GW:(g + 1) * GW]
            nc.vector.tensor_tensor(v, v, bank[6][:, :], ALU.add).then_inc(y_kept, 1)

        def keep_yoff(g):
            dve.wait_ge(yoff_raw, g + 1)
            t = xdt[:, 1, g * GW:(g + 1) * GW]
            dve.wait_ge(y_raw, 8)
            dve.wait_ge(ef_ready, 1)
            link_dve(dve, nc.vector.tensor_tensor(
                t.rearrange("p (h d) -> p h d", h=8), bank[5][:, :].rearrange("p (h d) -> p h d", h=8),
                bcast(ef[:, 1, 8 * g:8 * g + 8].unsqueeze(2), [P, 8, HD]), ALU.mult))
            v = x_tok[:, 1, g * GW:(g + 1) * GW]
            dve.wait_ge(y_kept, 3 + g)
            nc.vector.tensor_tensor(v, v, t, ALU.add).then_inc(yoff_kept, 1)

        def gate_y(n):
            b, g = divmod(n, GROUPS)
            z = z_tok[:, b, g * GW:(g + 1) * GW]
            dve.wait_ge(z_kept, 4)
            dve.wait_ge(y_kept, n + 1)
            if b == 1:
                dve.wait_ge(yoff_kept, g + 1)
            nc.vector.tensor_tensor(z, z, x_tok[:, b, g * GW:(g + 1) * GW], ALU.mult).then_inc(zy_ready, 1)

        def norm_y(n):
            b, g = divmod(n, GROUPS)
            dve.wait_ge(ssd_ss, n + 1)
            nc.vector.tensor_scalar(sm[:, 28 + n:29 + n], sm[:, 36 + n:37 + n], 1.0 / GW, EPS, ALU.mult,
                                    ALU.add).then_inc(ssd_ms, 1)

        def scale_y(n):
            b, g = divmod(n, GROUPS)
            z = z_tok[:, b, g * GW:(g + 1) * GW]
            dve.wait_ge(ssd_rstd, n + 1)
            nc.vector.tensor_scalar(z, z, sm[:, 32 + n:33 + n], None, ALU.mult).then_inc(ssd_norm, 1)

        def lo_ssd(n):
            b, g = divmod(n, GROUPS)
            dve.wait_ge(ssd_hi, n + 1)
            nc.vector.tensor_tensor(act_p[:, 1, 4 * g:4 * g + 4, b * P:(b + 1) * P],
                                    bank[5 + n % 2][:, :].rearrange("p (c t) -> p c t", c=4),
                                    act_p[:, 0, 4 * g:4 * g + 4, b * P:(b + 1) * P].bitcast(F32),
                                    ALU.subtract).then_inc(ssd_lo, 1)

        def conv_sc(hf, j):
            dve.wait_ge(gran_used, G_SC + 12 * hf + 4 + j + 1)
            dve.wait_ge(c_kept, 4 * hf + j + 1)
            if hf == 0 and j == 0:
                dve.wait_ge(silu_done, XC)
            link_dve(dve, nc.vector.tensor_tensor(pad[:, j % 2, 3:T + 3], bank[j][:, 0:T], sc_t[:, j, :],
                                                  ALU.mult))
            for tap in range(3):
                wc = pcol("sc_conv_w", tap * 8 + 4 * hf + j)
                src = pad[:, j % 2, 1 + tap:1 + tap + T]
                if tap == 0:
                    link_dve(dve, nc.vector.tensor_scalar(sc_t[:, j, :], src, wc, None, ALU.mult))
                    continue
                ins = nc.vector.scalar_tensor_tensor(out=sc_t[:, j, :], in0=src, scalar=wc, in1=sc_t[:, j, :],
                                                     op0=ALU.mult, op1=ALU.add)
                if tap < 2:
                    link_dve(dve, ins)
            ins.then_inc(v_used, 1)

        def gate_sc(hf, j):
            dve.wait_ge(gran_used, G_SC + 12 * hf + 8 + j + 1)
            dve.wait_ge(v_used, 4 * hf + j + 1)
            nc.vector.tensor_tensor(sc_t[:, j, :], bank[j][:, 0:T], sc_t[:, j, :], ALU.mult).then_inc(b_used, 1)

        def norm_sc(hf):
            for n, bk in enumerate((bank[4], bank[7])):
                dve.wait_ge(sc_sqrt, 2 * hf + n + 1)
                link_dve(dve, nc.vector.reciprocal(bk[:, :], bk[:, :]))
                v = sc_t[:, 2 * n:2 * n + 2, :]
                ins = nc.vector.tensor_tensor(v, v, bk[:, :].rearrange("p (c t) -> p c t", c=2), ALU.mult)
            ins.then_inc(sc_scaled, 1)

        def lo_sc(hf):
            dve.wait_ge(sc_hi, hf + 1)
            nc.vector.tensor_tensor(act_q[:, 1, 4 * hf:4 * hf + 4, :], sc_t[:, :, :],
                                    act_q[:, 0, 4 * hf:4 * hf + 4, :].bitcast(F32), ALU.subtract)\
              .then_inc(sc_lo, 1)

        for g in range(GA):
            lo(dve, g)
            if g == 0:
                dve.wait_ge(narrow_hi, 1)
                nc.vector.tensor_tensor(ws_lo[:, :, :], w_dt[:, :, :], ws_hi[:, :, :].bitcast(F32),
                                        ALU.subtract).then_inc(narrow_lo, 1)
            if 2 <= g < 2 + XC:
                conv_xbc(g - 2)
            if g == G_Z + 3:
                dt_chain()
            if g == G_Z + 4:
                scale_x()
            if g == G_SC + 1:
                keep_cb()
            if G_SC + 3 <= g < G_SC + 19 and g % 2 == 1:
                mask_seg((g - G_SC - 3) // 2)
            if G_SC + 5 <= g < G_SC + 21 and (g - G_SC - 5) % 4 == 0:
                keep_y((g - G_SC - 5) // 4)
            for hf in range(2):
                base = G_SC + 12 * hf
                if base + 6 <= g < base + 10:
                    conv_sc(hf, g - base - 6)
                if base + 10 <= g < base + 14:
                    gate_sc(hf, g - base - 10)
                if g == base + 16:
                    norm_sc(hf)
                    lo_sc(hf)
            if g == G_SC + 21:
                for n in range(2):
                    gate_y(n)
            if g == G_SC + 23:
                keep_yoff(0)
                keep_yoff(1)
                gate_y(2)
                gate_y(3)
            if g == G_WO:
                for n in range(4):
                    norm_y(n)
            if g == G_WO + 1:
                for n in range(4):
                    scale_y(n)
            if g == G_WO + 2:
                for n in range(4):
                    lo_ssd(n)
        dve.wait_ge(gran_used, GA)
        add_res(dve, bank[0:4], res_mix)

        dve.wait_ge(res_mix, 1)
        norm_dve(dve, 1, res, tok)
        for c in range(1, KC, 2):
            dve.wait_ge(tok_turned, c + 1)
            nc.vector.tensor_scalar(tok_t[:, c, :], bank[c % 4][:, 0:T], pcol("norm_ffn", c), None,
                                    ALU.mult).then_inc(tok_dve, 1)

        def by_token(v, n):
            return bcast(v.unsqueeze(2), [P, TB, n])

        def first_max(v, top, n, eq, at, best, hot):
            link_dve(dve, nc.vector.tensor_reduce(top, v, AX_X, ALU.max))
            link_dve(dve, nc.vector.tensor_tensor(eq, v, by_token(top, n), ALU.is_equal))
            link_dve(dve, nc.vector.scalar_tensor_tensor(
                out=at, in0=eq, scalar=-100.0, in1=bcast(iota_f[:, 0:n].unsqueeze(1), [P, TB, n]),
                op0=ALU.mult, op1=ALU.add))
            link_dve(dve, nc.vector.tensor_reduce(best, at, AX_X, ALU.min))
            link_dve(dve, nc.vector.tensor_tensor(hot, at, by_token(best, n), ALU.is_equal))

        dve.wait_ge(logits_raw, 1)
        lg = bank[6][:, 0:TB * 64].rearrange("p (b n) -> p b n", b=TB)
        glog, g_hot = r8[:, 0, :, 0:NG], r8[:, 1, :, 0:NG]
        nc.vector.tensor_copy(rt[:, 0, :, :], lg[:, :, NG:NG + NE])
        link_dve(dve, nc.vector.tensor_copy(glog, lg[:, :, 0:NG]))
        first_max(glog, r1[:, 0, :], NG, r8[:, 2, :, 0:NG], r8[:, 3, :, 0:NG], r1[:, 7, :], g_hot)
        nc.vector.tensor_tensor(r8[:, 4, :, 0:NG], glog, by_token(r1[:, 0, :], NG), ALU.subtract)\
          .then_inc(margin, 1)

        def by_group(v):
            return v.rearrange("p b (g e) -> p b g e", g=NG)

        def over_experts(v):
            return bcast(v.unsqueeze(3), [P, TB, NG, EPG])

        def over_groups(v):
            return bcast(v.unsqueeze(2), [P, TB, NG, EPG])
        link_dve(dve, nc.vector.tensor_tensor(by_group(rt[:, 1, :, :]), by_group(rt[:, 0, :, :]),
                                              over_experts(g_hot), ALU.mult))
        link_dve(dve, nc.vector.tensor_reduce(r8[:, 6, :, :], rt[:, 1, :, :].rearrange("p b (g e) -> p b e g", g=NG),
                                              AX_X, ALU.add))
        first_max(r8[:, 6, :, :], r1[:, 2, :], EPG, r8[:, 2, :, :], r8[:, 3, :, :], r1[:, 7, :], r8[:, 7, :, :])
        link_dve(dve, nc.vector.scalar_tensor_tensor(out=r8[:, 8, :, :], in0=r8[:, 7, :, :], scalar=-3e38,
                                                     in1=r8[:, 6, :, :], op0=ALU.mult, op1=ALU.add))
        first_max(r8[:, 8, :, :], r1[:, 3, :], EPG, r8[:, 2, :, :], r8[:, 3, :, :], r1[:, 7, :], r8[:, 9, :, :])
        nc.vector.tensor_tensor(r1[:, 4, :], r1[:, 3, :], r1[:, 2, :], ALU.subtract).then_inc(margin, 1)
        nc.vector.tensor_tensor(by_group(rt[:, 2, :, :]), over_experts(g_hot), over_groups(r8[:, 7, :, :]), ALU.mult)
        link_dve(dve, nc.vector.tensor_tensor(by_group(rt[:, 3, :, :]), over_experts(g_hot),
                                              over_groups(r8[:, 9, :, :]), ALU.mult))
        nc.vector.tensor_tensor(rt[:, 4, :, :], rt[:, 2, :, :], rt[:, 3, :, :], ALU.add).then_inc(member, 1)
        dve.wait_ge(exp_ready, 4)
        nc.vector.tensor_reduce(r1[:, 1, :], r8[:, 5, :, 0:NG], AX_X, ALU.add)
        dve.wait_ge(exp_ready, 5)
        link_dve(dve, nc.vector.tensor_scalar(r1[:, 6, :], r1[:, 5, :], 1.0, None, ALU.add))
        link_dve(dve, nc.vector.tensor_tensor(r1[:, 6, :], r1[:, 6, :], r1[:, 1, :], ALU.mult))
        link_dve(dve, nc.vector.reciprocal(pos[:, :, 2], r1[:, 6, :]))
        link_dve(dve, nc.vector.tensor_tensor(pos[:, :, 3], pos[:, :, 2], r1[:, 5, :], ALU.mult))
        dve.wait_ge(rank_raw, 1)
        nc.vector.tensor_copy(rt[:, 6, 0, :], bank[5][:, 2 * NE:3 * NE])
        link_dve(dve, nc.vector.tensor_copy(rt[:, 5, :, :],
                                            bank[5][:, 0:2 * NE].rearrange("p (b e) -> p b e", b=TB)))
        nc.vector.tensor_reduce(r1[:, 8, 0:1], rt[:, 6, 0, :], AX_X, ALU.max)
        link_dve(dve, nc.vector.tensor_scalar(rt[:, 7, :, :], rt[:, 5, :, :], float(CAP), None, ALU.is_ge))
        link_dve(dve, nc.vector.tensor_scalar(r1[:, 9, 0:1], r1[:, 8, 0:1], float(CAP), 1.0, ALU.is_gt, ALU.add))
        for n in range(2, T // CAP):
            nc.vector.scalar_tensor_tensor(out=rt[:, 7, :, :], in0=rt[:, 5, :, :], scalar=float(CAP * n),
                                           in1=rt[:, 7, :, :], op0=ALU.is_ge, op1=ALU.add)
            link_dve(dve, nc.vector.scalar_tensor_tensor(
                out=r1[:, 9, 0:1], in0=r1[:, 8, 0:1], scalar=float(CAP * n), in1=r1[:, 9, 0:1],
                op0=ALU.is_gt, op1=ALU.add))
        nc.vector.tensor_copy(rounds_i[:, 0:1], r1[0:1, 9, 0:1])
        nc.vector.tensor_scalar(rounds_i[:, 1:2], r1[0:1, 9, 0:1], float(NE), -1.0, ALU.mult, ALU.add)
        link_dve(dve, nc.vector.scalar_tensor_tensor(
            out=rt[:, 8, :, :], in0=rt[:, 7, :, :], scalar=float(ROUND - CAP), in1=rt[:, 5, :, :],
            op0=ALU.mult, op1=ALU.add))
        link_dve(dve, nc.vector.scalar_tensor_tensor(
            out=rt[:, 8, :, :], in0=bcast(iota_f[:, 0:NE].unsqueeze(1), [P, TB, NE]), scalar=float(CAP),
            in1=rt[:, 8, :, :], op0=ALU.mult, op1=ALU.add))
        for choice in range(2):
            link_dve(dve, nc.vector.tensor_tensor(rt[:, 9 + choice, :, :], rt[:, 2 + choice, :, :],
                                                  rt[:, 8, :, :], ALU.mult))
            link_dve(dve, nc.vector.tensor_reduce(pos[:, :, choice], rt[:, 9 + choice, :, :], AX_X, ALU.add))
        for b in range(TB):
            nc.vector.tensor_tensor(diag[:, b, :, :], bcast(ident[:, :].unsqueeze(1), [P, 4, P]),
                                    bcast(pos[:, b, :].unsqueeze(2), [P, 4, P]), ALU.mult).then_inc(diag_ready, 1)
        nc.vector.memset(moe[:, :, :], 0.0).then_inc(routed, 1)
        for b in range(TB):
            dve.wait_ge(rows_raw, b + 1)
            ins = nc.vector.tensor_copy(rows[:, :, b * P:(b + 1) * P],
                                        bank[b][:, :].rearrange("p (k j) -> p k j", k=4))
        ins.then_inc(moe_added, 1)
        dve.wait_ge(moe_added, 1)

        def build_group(s, last):
            for b in range(TB):
                nc.vector.tensor_scalar(onehot[:, s, b, :], iota_f[:, :], pos[:, b, 0:1], None, ALU.is_equal)
            for c in range(2):
                ins = nc.vector.scalar_tensor_tensor(out=gtmp[:, c, :], in0=rows[:, c, :], scalar=iota_p[:, 0:1],
                                                     in1=rows[:, 2 + c, :], op0=ALU.is_equal, op1=ALU.mult)
            ins.then_inc(built, 1)
            dve.wait_ge(built, 3 * last + 1)
            for b in range(TB):
                nc.vector.scalar_tensor_tensor(out=onehot[:, s, b, :], in0=iota_f[:, :], scalar=pos[:, b, 1:2],
                                               in1=onehot[:, s, b, :], op0=ALU.is_equal, op1=ALU.add)
            nc.vector.tensor_tensor(gmat[:, s, :], gtmp[:, 0, :], gtmp[:, 1, :], ALU.add).then_inc(built, 1)
            dve.wait_ge(built, 3 * last + 2)
            nc.vector.tensor_scalar(rows[:, 0:2, :], rows[:, 0:2, :], -float(P), None, ALU.add)
            nc.vector.tensor_scalar(pos[:, :, 0:2], pos[:, :, 0:2], -float(P), None, ALU.add).then_inc(built, 1)

        build_group(0, 0)
        dve.wait_ge(built, 3)
        n_rounds = dve.value_load(rounds_i[0:1, 0:1], min_val=1, max_val=T // CAP)
        with dve.Fori(0, n_rounds) as r:
            with dve.Fori(0, NE // 8) as i:
                for s in range(2):
                    k = 8 * r + 2 * i + s
                    for half in range(2):
                        dve.wait_ge(xt_raw, 2 * k + half + 1)
                        nc.vector.tensor_tensor(
                            x_t[:, s, 4 * half:4 * half + 4, :],
                            bank[5 + half][:, :].rearrange("p (c j) -> p c j", c=4),
                            bcast(par[:, PCOLS["norm_ffn"] + 4 * half:PCOLS["norm_ffn"] + 4 * half + 4].unsqueeze(2),
                                  [P, 4, P]), ALU.mult).then_inc(xt_kept, 1)
                    dve.wait_ge(built, 3 * k + 3)
                    build_group(1 - s, k + 1)
                    for e in range(4):
                        x = 4 * k + e
                        dve.wait_ge(gate_silu, x + 1)
                        nc.vector.tensor_tensor(h_e[:, :], h_e[:, :], bank[0][:, P:2 * P], ALU.mult)\
                          .then_inc(h_ready, 1)
                        dve.wait_ge(ye_raw, x + 1)
                        for j in range(2, 4):
                            ins = nc.vector.tensor_copy(y_e[CAP * e:CAP * (e + 1), 256 * j:256 * (j + 1)],
                                                        bank[2][CAP * j:CAP * (j + 1), 0:256])
                        ins.then_inc(ye_dve, 1)
                    for q in range(4):
                        b, half = divmod(q, 2)
                        v = moe[:, b, half * 512:(half + 1) * 512]
                        dve.wait_ge(moe_raw, 4 * k + q + 1)
                        nc.vector.tensor_tensor(v, v, bank[M_BANK[q]][:, :], ALU.add).then_inc(moe_added, 1)
        dve.wait_ge(moe_added, NE * n_rounds + 1)
        nc.vector.tensor_tensor(res[:, :, :], res[:, :, :], moe[:, :, :], ALU.add).then_inc(res_moe, 1)
        dve.wait_ge(res_moe, 1)
        norm_dve(dve, 2, res, tok)
        dve.wait_ge(ld_fgain, 16)
        dve.wait_ge(nrm_dve, 3)
        dve.wait_ge(nrm_act, 3)
        for b in range(TB):
            ins = nc.vector.tensor_tensor(res[:, b, :], tok[:, b, :], fgain[:, :], ALU.mult)
        ins.then_inc(res_mid, 1)

        dve.wait_ge(res_mid, 1)
        norm_dve(dve, 3, res, nrm)
        dve.wait_ge(narrow_hi, 2)
        nc.vector.tensor_tensor(ws_lo[:, :, :], w_z[:, :, :], ws_hi[:, :, :].bitcast(F32),
                                ALU.subtract).then_inc(narrow_lo, 1)
        for g in range(GA, GA + 2):
            lo(dve, g)
        turn_dve(dve, 1, "norm1_2")
        li = lpad[:, :, 0:T]
        t1 = st[:, 0:2, :, :].rearrange("p n c d -> p n (c d)")
        lq = nrm[:, 1, :].rearrange("p (c t) -> p c t", c=LC)

        def conv_lru(c):
            dve.wait_ge(lx_copied, c + 1)
            dve.wait_ge(c_mask, 1)
            for tap in range(4):
                wc = pcol("conv_w_2", tap * LC + c)
                src = lpad[:, c, tap:tap + T]
                if tap == 0:
                    link_dve(dve, nc.vector.tensor_scalar(lx[:, c, :], src, wc, pcol("conv_b_2", c), ALU.mult,
                                                          ALU.add))
                    continue
                ins = nc.vector.scalar_tensor_tensor(out=lx[:, c, :], in0=src, scalar=wc, in1=lx[:, c, :],
                                                     op0=ALU.mult, op1=ALU.add)
                if tap < 3:
                    link_dve(dve, ins)
            ins.then_inc(lx_ready, 1)

        for g in range(GA + 2, G_FF):
            lo(dve, g)
            if GA + 2 <= g < GA + 6:
                conv_lru(g - GA - 2)
            if g == GA + 5:
                dve.wait_ge(zf_kept, 1)
                nc.vector.scalar_tensor_tensor(out=t1, in0=la[:, :, :], scalar=-1.0, in1=la[:, :, :],
                                               op0=ALU.mult, op1=ALU.min).then_inc(neg_abs, 1)
            if g == GA + 7:
                dve.wait_ge(zf_log, 1)
                nc.vector.scalar_tensor_tensor(out=la[:, :, :], in0=la[:, :, :], scalar=0.0, in1=t1, op0=ALU.min,
                                               op1=ALU.subtract).then_inc(la_ready, 1)
            if g == GA + 10:
                dve.wait_ge(decay_exp, 1)
                dve.wait_ge(k_kept, 1)
                nc.vector.tensor_tensor(k_tok[:, :, :], k_tok[:, :, :], t1, ALU.mult).then_inc(kdec_ready, 1)
            if g == GA + 11:
                dve.wait_ge(l_tanh, 1)
                link_dve(dve, nc.vector.tensor_tensor(lx[:, :, :], lx[:, :, :], li, ALU.mult))
                nc.vector.tensor_scalar(li, lr[:, :, :], -1.0, 1e-30, ALU.mult, ALU.max).then_inc(l_neg, 1)
                link_dve(dve, nc.vector.tensor_scalar(lq, lr[:, :, :], -1.0, 1.0, ALU.mult, ALU.add))
                link_dve(dve, nc.vector.reciprocal(lq, lq))
                link_dve(dve, nc.vector.scalar_tensor_tensor(out=lr[:, :, :], in0=lr[:, :, :], scalar=1.0, in1=lq,
                                                             op0=ALU.add, op1=ALU.mult))
            if g == GA + 13:
                dve.wait_ge(l_sqrt, 1)
                link_dve(dve, nc.vector.scalar_tensor_tensor(out=li, in0=li, scalar=2.0, in1=lq, op0=ALU.mult,
                                                             op1=ALU.mult))
                link_dve(dve, nc.vector.tensor_tensor(li, li, lx[:, :, :], ALU.mult))
            if g in (GA + 14, GA + 15):
                for c in range(2 * (g - GA - 14), 2 * (g - GA - 14) + 2):
                    nc.vector.tensor_tensor_scan(lq[:, c, :], lr[:, c, :], li[:, c, :], 0.0, ALU.mult, ALU.add)\
                      .then_inc(lru_scan, 1)
            if g == G_G + 4:
                dve.wait_ge(upd_raw, 1)
                dve.wait_ge(kdec_ready, 1)
                dve.wait_ge(decay_exp, 1)
                link_dve(dve, nc.vector.tensor_copy(st[:, 0, :, :],
                                                    bank[6][:, 0:256].rearrange("p (c d) -> p c d", c=2)))
                for n in range(1, 4):
                    for c in range(2):
                        o = (n // 2) * 256 + c * P
                        ins = nc.vector.scalar_tensor_tensor(
                            out=st[:, n, c, :], in0=st[:, n - 1, c, :], scalar=dec[:, c, n:n + 1],
                            in1=bank[6 + n % 2][:, o:o + P], op0=ALU.mult, op1=ALU.add)
                    if n < 3:
                        link_dve(dve, ins)
                ins.then_inc(st_ready, 1)
            if g == G_G + 6:
                dve.wait_ge(g_kept, 2)
                dve.wait_ge(ld_c, 16 * 5)
                v = g_tok[:, :, :].rearrange("p b (h d) -> p (b h) d", h=4)
                nc.vector.tensor_tensor(v, v, bcast(gnorm[:, :].unsqueeze(1), [P, 8, P]), ALU.mult)\
                  .then_inc(g_gain, 1)
            if g == G_LG + 3:
                dve.wait_ge(o_sq, 2)
                link_dve(dve, nc.vector.tensor_reduce(sm[:, 40:48], v_tok[:, :, :].rearrange(
                    "p n (c d) -> p (n c) d", c=4), AX_X, ALU.add))
                nc.vector.tensor_scalar(sm[:, 48:56], sm[:, 40:48], 1.0 / P, EPS, ALU.mult, ALU.add)\
                  .then_inc(o_ms, 1)
            if g == G_LG + 4:
                dve.wait_ge(o_rstd, 1)
                dve.wait_ge(g_gain, 1)
                for n in range(2):
                    v = v_tok[:, n, :].rearrange("p (c d) -> p c d", c=4)
                    nc.vector.tensor_tensor(v, bank[4 + n][:, :].rearrange("p (c d) -> p c d", c=4),
                                            bcast(sm[:, 56 + 4 * n:60 + 4 * n].unsqueeze(2), [P, 4, P]), ALU.mult)
                link_dve(dve, nc.vector.tensor_copy(sm[:, 66:67], sm[:, 56:57]))
                for n in range(2):
                    v = v_tok[:, n, :].rearrange("p (c d) -> p c d", c=4)
                    gv = g_tok[:, :, :].rearrange("p b (c q d) -> p q (b c) d", c=2, q=2)[:, n]
                    ins = nc.vector.tensor_tensor(v, v, gv, ALU.mult)
                ins.then_inc(gla_ready, 1)
            if G_LG + 4 <= g < G_LG + 8:
                c = g - G_LG - 4
                if c == 0:
                    dve.wait_ge(lru_scan, LC)
                dve.wait_ge(lgate_kept, c + 1)
                nc.vector.tensor_tensor(lq[:, c, :], lq[:, c, :], lgate[:, c, :], ALU.mult).then_inc(lru_prod, 1)
                dve.wait_ge(lru_hi, c + 1)
                nc.vector.tensor_tensor(act_q[:, 1, c, :], lq[:, c, :], act_q[:, 0, c, :].bitcast(F32),
                                        ALU.subtract).then_inc(lru_lo, 1)
            if g == G_WO2 + 4:
                for b in range(TB):
                    dve.wait_ge(gla_hi, b + 1)
                    nc.vector.tensor_tensor(act_q[:, 1, 4:8, b * P:(b + 1) * P],
                                            bank[6 + b][:, :].rearrange("p (c t) -> p c t", c=4),
                                            act_q[:, 0, 4:8, b * P:(b + 1) * P].bitcast(F32), ALU.subtract)\
                      .then_inc(gla_lo, 1)
        dve.wait_ge(gran_used, G_FF)
        add_res(dve, bank[0:4], res_mix2)
        dve.wait_ge(res_mix2, 1)
        norm_dve(dve, 4, res, nrm)
        for g in range(G_FF, G_FF + 2):
            lo(dve, g)
        turn_dve(dve, 2, "norm2_2")
        for g in range(G_FF + 2, GEND):
            lo(dve, g)
            for f in range(FC):
                if g == GU[f] + 2:
                    dve.wait_ge(f_silu, f + 1)
                    nc.vector.tensor_tensor(lx[:, f % 4, :], lx[:, f % 4, :], bank[f % 4][:, T:2 * T],
                                            ALU.mult).then_inc(f_prod, 1)
                if g == GU[f] + 3:
                    dve.wait_ge(f_hi, f + 1)
                    nc.vector.tensor_tensor(act_q[:, 1, f % 8, :], lx[:, f % 4, :],
                                            act_q[:, 0, f % 8, :].bitcast(F32), ALU.subtract).then_inc(f_lo, 1)
        dve.wait_ge(gran_used, GEND)
        add_res(dve, bank[4:8], res_ffn)
        dve.wait_ge(res_ffn, 1)
        norm_dve(dve, 5, res, nrm)
        dve.wait_ge(ld_gain2, 16)
        for b in range(TB):
            dve.wait_ge(nrm_dve if b == 0 else nrm_act, 6)
            nc.vector.tensor_tensor(nrm[:, b, :], nrm[:, b, :], fg2, ALU.mult).then_inc(out_ready, 1)

    @block.tensor
    def _(pe):
        pe.wait_ge(ld_par, 16 * N_SMALL)
        pe.wait_ge(const_ready, 1)
        nc.tensor.transpose(bank[4][:, 0:ROWS_A], prow[0:ROWS_A, 0, :], ident[0:ROWS_A, 0:ROWS_A])
        nc.tensor.transpose(bank[4][:, P:P + ROWS_B], prow[0:ROWS_B, 1, :], ident[0:ROWS_B, 0:ROWS_B])\
          .then_inc(par_turned, 1)
        turn_pe(pe, 0, 0, xdt)
        pe.wait_ge(turn_lo, KC)

        def turn_x(i):
            pe.wait_ge(silu_done, i + 1)
            if i >= 2:
                pe.wait_ge(x_kept, i - 1)
            elif i == 0:
                pe.wait_ge(par_ready, 1)
            for b in range(TB):
                mm = nc.tensor.transpose(bank[4 + i % 2][:, b * P:(b + 1) * P], cv[:, i % 2, b * P:(b + 1) * P],
                                         ident[:, :])
            mm.then_inc(x_turned, 1)

        def ssd_start():
            pe.wait_ge(dt_ready, 1)
            pe.wait_ge(const_ready, 2)
            nc.tensor.matmul(bank[7][:, 0:HEADS], m_gt[:, :], adt[:, 0, 0, :], start=True, stop=True)
            nc.tensor.matmul(bank[7][:, HEADS:2 * HEADS], m_le[:, :], adt[:, 0, 1, :], start=True, stop=True)\
              .then_inc(ef_raw, 1)
            pe.wait_ge(silu_done, XC)
            pe.wait_ge(x_kept, KC)
            for g in range(GROUPS):
                nc.tensor.matmul(bank[5 + g][:, 0:T], bc_t[:, g, 0:P], bc_t[:, 2 + g, :], start=True, stop=True)
                nc.tensor.matmul(bank[5 + g][:, T:T + P], bc_t[:, g, P:T], bc_t[:, 2 + g, P:T], start=True,
                                 stop=True).then_inc(cb_raw, 1)

        def seg(it):
            pe.wait_ge(seg_lhs, it + 1)
            if it == 0:
                pe.wait_ge(cb_ready, GROUPS)
            else:
                pe.wait_ge(seg_exp, it)
            for j in range(4):
                mm = nc.tensor.matmul(bank[5][:, j * P:(j + 1) * P], seg_l[:, j, :], m_le[:, :], start=True,
                                      stop=True)
            mm.then_inc(seg_raw, 1)

        def y_same(it):
            b, q = divmod(it, 4)
            pe.wait_ge(seg_m, it + 1)
            if it == 0:
                pe.wait_ge(xdt_ready, 1)
            if it % 2 == 0 and it >= 2:
                pe.wait_ge(y_kept, it // 2)
            for j in range(4):
                o = (q % 2) * 256 + j * HD
                mm = nc.tensor.matmul(bank[6][:, o:o + HD], seg_e[:, it % 2, j, :],
                                      xdt[:, b, (4 * q + j) * HD:(4 * q + j + 1) * HD], start=True, stop=True)
            mm.then_inc(y_raw, 1)

        def y_off(g):
            pe.wait_ge(xdt_decayed, 1)
            if g == 0:
                pe.wait_ge(seg_exp, 8)
            else:
                pe.wait_ge(yoff_kept, g)
            nc.tensor.matmul(bank[5][:, :], cbm[:, g, 1, :], xdt[:, 0, g * GW:(g + 1) * GW], start=True,
                             stop=True).then_inc(yoff_raw, 1)

        def sum_sc(hf, j):
            n = 4 * hf + j
            pe.wait_ge(sc_sq, n + 1)
            if n == 0:
                pe.wait_ge(ef_ready, 1)
                pe.wait_ge(x_kept, KC)
            if hf and j == 0:
                pe.wait_ge(sc_scaled, 1)
            bk = bank[4] if j < 2 else bank[7]
            nc.tensor.matmul(bk[:, (j % 2) * T:(j % 2 + 1) * T], blk64[:, :], cv[:, j % 2, :], start=True,
                             stop=True).then_inc(sc_sum, 1)

        def turn_ssd(n):
            b, g = divmod(n, GROUPS)
            pe.wait_ge(ssd_norm, n + 1)
            if n >= 2:
                pe.wait_ge(ssd_lo, n - 1)
            else:
                pe.wait_ge(yoff_kept, 2)
            for j in range(4):
                mm = nc.tensor.transpose(bank[5 + n % 2][:, j * P:(j + 1) * P],
                                         z_tok[:, b, g * GW + j * P:g * GW + (j + 1) * P], ident[:, :])
            mm.then_inc(ssd_turned, 1)

        for g in range(G_Z):
            if g >= 4:
                pe.wait_ge(xbc_copied, g - 3)
            turn_gran(pe, g, bank[g % 4][:, 0:T], act_p)
            if 3 <= g < 3 + KC:
                turn_x(g - 3)
        pe.wait_ge(narrow_lo, 1)
        for b in range(TB):
            for k in range(KC):
                for i, (wt, x_part) in enumerate(((ws_hi, 0), (ws_hi, 1), (ws_lo, 0))):
                    mm = nc.tensor.matmul(bank[6][:, b * HEADS:(b + 1) * HEADS],
                                          act_p[:, x_part, k, b * P:(b + 1) * P], wt[:, k, :],
                                          start=(k == 0 and i == 0), stop=(k == KC - 1 and i == 2))
        mm.then_inc(dt_raw, 1)
        for t in range(2):
            pe.wait_ge(xbc_copied, 10 + 2 * t)
            for j in range(4):
                g = G_Z + 4 * t + j
                flow_gran(pe, g, [bank[2 * t + b][:, :] for b in range(TB)], act_p, 2 * j)
        ssd_start()
        for g in range(G_SC, G_WO):
            hf, j = divmod(g - G_SC, 12)
            kind, c = divmod(j, 4)
            if kind == 0 and hf == 0:
                pe.wait_ge(z_kept, c + 1)
            elif kind == 0:
                pe.wait_ge(b_used, c + 1)
            elif kind == 1:
                pe.wait_ge(c_kept, 4 * hf + c + 1)
            else:
                pe.wait_ge(v_used, 4 * hf + c + 1)
            turn_gran(pe, g, bank[c][:, 0:T], act_p)
            if g % 2 == 0 and g < G_SC + 16:
                seg((g - G_SC) // 2)
            if g % 2 == 0 and G_SC + 2 <= g < G_SC + 18:
                y_same((g - G_SC - 2) // 2)
            for h in range(2):
                if G_SC + 12 * h + 11 <= g < G_SC + 12 * h + 15 and g < G_WO:
                    sum_sc(h, g - G_SC - 12 * h - 11)
            if g == G_SC + 20:
                y_off(0)
            if g == G_WO - 1:
                y_off(1)
        pe.wait_ge(b_used, 8)
        for g in range(G_WO, GA):
            k = MIX[g - G_WO]
            if k == 8:
                pe.wait_ge(sc_lo, 1)
            if k == 11:
                for n in range(4):
                    turn_ssd(n)
            if k == 0:
                pe.wait_ge(ssd_lo, 4)
            if k == 12:
                pe.wait_ge(sc_lo, 2)
            a = act_q[:, :, k - 8, :] if k >= 8 else act_p[:, :, k, :]
            row_gran(pe, g, bank[0:4], a, g == G_WO, g == GA - 1)
            if g < G_WO + 3:
                sum_sc(1, g - G_WO + 1)

        pe.wait_ge(res_mix, 1)
        pe.wait_ge(nrm_act, 2)
        pe.wait_ge(nrm_dve, 2)
        for c in range(KC):
            if c >= 4:
                if c % 2 == 0:
                    pe.wait_ge(tok_act, (c - 4) // 2 + 1)
                else:
                    pe.wait_ge(tok_dve, (c - 5) // 2 + 1)
            for b in range(TB):
                mm = nc.tensor.transpose(bank[c % 4][:, b * P:(b + 1) * P], tok[:, b, c * P:(c + 1) * P], ident[:, :])
            mm.then_inc(tok_turned, 1)
        pe.wait_ge(tok_act, KC // 2)
        pe.wait_ge(tok_dve, KC // 2)
        for b in range(TB):
            for k in range(KC):
                mm = nc.tensor.matmul(bank[6][:, b * 64:b * 64 + NG + NE], tok_t[:, k, b * P:(b + 1) * P],
                                      w_rt[:, k, :], start=(k == 0), stop=(k == KC - 1))
        mm.then_inc(logits_raw, 1)
        pe.wait_ge(lt_ready, 1)
        pe.wait_ge(member, 1)
        nc.tensor.matmul(bank[5][:, 0:NE], m_lt[:, :], rt[:, 4, 0, :], start=True, stop=True)
        for o, last in ((NE, m_lt), (2 * NE, ones)):
            nc.tensor.matmul(bank[5][:, o:o + NE], ones[:, :], rt[:, 4, 0, :], start=True, stop=False)
            mm = nc.tensor.matmul(bank[5][:, o:o + NE], last[:, :], rt[:, 4, 1, :], start=False, stop=True)
        mm.then_inc(rank_raw, 1)
        for b in range(TB):
            pe.wait_ge(diag_ready, b + 1)
            nc.tensor.matmul(bank[b][:, :], ones[:, :], diag[:, b, :, :], start=True, stop=True)\
              .then_inc(rows_raw, 1)

        pe.wait_ge(routed, 1)
        n_rounds = pe.value_load(rounds_i[0:1, 0:1], min_val=1, max_val=T // CAP)
        with pe.Fori(0, n_rounds) as r:
            with pe.Fori(0, NE // 8) as i:
                for s in range(2):
                    k = 8 * r + 2 * i + s
                    pe.wait_ge(built, 3 * k + 3)
                    for half in range(2):
                        for c in range(4):
                            for b in range(TB):
                                o = (4 * half + c) * P
                                mm = nc.tensor.matmul(bank[5 + half][:, c * P:(c + 1) * P], tok[:, b, o:o + P],
                                                      onehot[:, s, b, :], start=(b == 0), stop=(b == TB - 1))
                        mm.then_inc(xt_raw, 1)
                    pe.wait_ge(xt_kept, 2 * k + 2)
                    for e in range(4):
                        x = 4 * k + e
                        s0 = E_SLOT[e % 2]
                        turn = 16 * r + 4 * i + 2 * s + e // 2 + 1
                        for n in range(2):
                            pe.wait_ge(landed[s0 + n], 16 * turn + E_LANDED[s0 + n])
                        gu = ring[:, s0:s0 + 2, :].rearrange("p s (k n) -> p s k n", k=KC)
                        for c in range(KC):
                            for j in range(4):
                                mm = nc.tensor.matmul(bank[0][CAP * j:CAP * (j + 1), 0:2 * P],
                                                      x_t[:, s, c, CAP * e:CAP * (e + 1)],
                                                      gu[:, :, c, j * P:(j + 1) * P],
                                                      start=(c == 0), stop=(c == KC - 1))
                        mm.then_inc(gu_raw, 1)
                        pe.wait_ge(h_ready, x + 1)
                        nc.tensor.transpose(bank[4][:, 0:P], h_e[:, :], ident[:, :]).then_inc(ht_raw, 1)
                        pe.wait_ge(ht_kept, x + 1)
                        pe.wait_ge(landed[s0 + 2], 16 * turn + E_LANDED[s0 + 2])
                        if e:
                            pe.wait_ge(ye_act, x)
                            pe.wait_ge(ye_dve, x)
                        dn = ring[:, s0 + 2, :].rearrange("p (k n) -> p k n", k=FF // P)
                        for c in range(FF // P):
                            for j in range(4):
                                mm = nc.tensor.matmul(bank[2][CAP * j:CAP * (j + 1), 0:256],
                                                      h_t[:, CAP * c:CAP * (c + 1)],
                                                      dn[:, c, 256 * j:256 * (j + 1)],
                                                      start=(c == 0), stop=(c == FF // P - 1))
                        mm.then_inc(ye_raw, 1)
                    pe.wait_ge(ye_act, 4 * k + 4)
                    pe.wait_ge(ye_dve, 4 * k + 4)
                    for q in range(4):
                        b, half = divmod(q, 2)
                        pe.wait_ge(moe_added, 4 * k + (2 if q == 3 else 1))
                        nc.tensor.matmul(bank[M_BANK[q]][:, :], gmat[:, s, b * P:(b + 1) * P],
                                         y_e[:, half * 512:(half + 1) * 512], start=True, stop=True)\
                          .then_inc(moe_raw, 1)

        pe.wait_ge(res_mid, 1)
        turn_pe(pe, 3, 1, nrm)
        pe.wait_ge(turn_lo, 2 * KC)
        pe.wait_ge(narrow_lo, 2)
        for b in range(TB):
            for k in range(KC):
                for i, (wt, x_part) in enumerate(((ws_hi, 0), (ws_hi, 1), (ws_lo, 0))):
                    mm = nc.tensor.matmul(bank[6][:, b * RANK:(b + 1) * RANK],
                                          act_p[:, x_part, k, b * P:(b + 1) * P], wt[:, k, :],
                                          start=(k == 0 and i == 0), stop=(k == KC - 1 and i == 2))
        mm.then_inc(z_raw, 1)

        def lru_gates(c):
            pe.wait_ge(lx_ready, c + 1)
            if c == 0:
                pe.wait_ge(ld_c, 16 * 5)
            if c >= 2:
                pe.wait_ge(lg_sig, c - 1)
            for n in range(2):
                mm = nc.tensor.matmul(bank[4 + c % 2][:, n * T:(n + 1) * T], lru_w[:, n, c, :], lx[:, c, :],
                                      start=True, stop=True)
            mm.then_inc(lg_raw, 1)

        for g in range(GA, G_WO2):
            if g < G_Q:
                turn_gran(pe, g, bank[g - GA][:, 0:T], act_p)
            elif g < G_K:
                pe.wait_ge(lx_copied, g - G_Q + 1)
                turn_gran(pe, g, bank[g - G_Q][:, 0:T], act_p)
            elif g < G_V:
                pe.wait_ge(lx_copied, 4)
                flow_gran(pe, g, [bank[2 + b][:, 0:256] for b in range(TB)], act_p, 4 * (g - G_K))
            elif g < G_G:
                pe.wait_ge(q_kept, 2)
                flow_gran(pe, g, [bank[b][:, :] for b in range(TB)], act_p, 2 * (g - G_V))
            elif g < G_LG:
                pe.wait_ge(k_kept, 1)
                flow_gran(pe, g, [bank[2 + b][:, :] for b in range(TB)], act_p, 2 * (g - G_G))
            else:
                c = g - G_LG
                if c < 2:
                    pe.wait_ge(v_kept, c + 1)
                else:
                    pe.wait_ge(g_kept, c - 1)
                turn_gran(pe, g, bank[c][:, 0:T], act_p)
            if g == GA + 1:
                pe.wait_ge(zsb_kept, 1)
                for b in range(TB):
                    mm = nc.tensor.transpose(bank[7][0:RANK, b * P:(b + 1) * P], z_sb[:, b, :], ident[:, :])
                mm.then_inc(zt_raw, 1)
            if g == GA + 3:
                pe.wait_ge(zt_kept, 1)
                for b in range(TB):
                    mm = nc.tensor.matmul(bank[6][:, b * 256:(b + 1) * 256], z_t[:, b * P:(b + 1) * P], w_al[:, :],
                                          start=True, stop=True)
                mm.then_inc(zf_raw, 1)
            if g == GA + 5:
                lru_gates(0)
                lru_gates(1)
            if g == GA + 7:
                pe.wait_ge(la_ready, 1)
                for b in range(TB):
                    nc.tensor.matmul(bank[6][:, b * 256:(b + 1) * 256], m_gtc[:, :], la[:, b, :], start=True,
                                     stop=True)
                for c in range(2):
                    for b in range(TB):
                        o = 4 * c + 2 * b
                        mm = nc.tensor.matmul(bank[7][:, o:o + 2], la[:, b, c * P:(c + 1) * P],
                                              blk64[:, 0:P:64], start=True, stop=True)
                mm.then_inc(suffix_raw, 1)
            if g == GA + 8:
                lru_gates(2)
                lru_gates(3)
            if g == G_G + 2:
                pe.wait_ge(kdec_ready, 1)
                pe.wait_ge(v_kept, 2)
                for n in range(4):
                    b, r0 = n // 2, 64 * (n % 2)
                    for h in range(4):
                        o = b * 256 + (h // 2) * P
                        mm = nc.tensor.matmul(bank[6 + n % 2][64 * (h % 2):64 * (h % 2) + 64, o:o + P],
                                              k_tok[r0:r0 + 64, b, h * 64:(h + 1) * 64],
                                              v_tok[r0:r0 + 64, b, h * P:(h + 1) * P], start=True, stop=True)
                mm.then_inc(upd_raw, 1)
            if g == G_G + 5:
                pe.wait_ge(st_ready, 1)
                pe.wait_ge(q_kept, 2)
                pe.wait_ge(lg_sig, 4)
                for n in range(4):
                    for h in range(4):
                        r0, o = 64 * (h % 2), (n // 2) * 256 + (h // 2) * P
                        mm = nc.tensor.matmul(bank[4 + h % 2][64 * (n % 2):64 * (n % 2) + 64, o:o + P],
                                              q_t[r0:r0 + 64, h // 2, n * 64:(n + 1) * 64],
                                              st[r0:r0 + 64, n, h // 2, :], start=True, stop=True)
                mm.then_inc(o_raw, 1)
        pe.wait_ge(lgate_kept, LC)
        for g in range(G_WO2, G_FF):
            c = g - G_WO2
            if c < LC:
                pe.wait_ge(lru_lo, c + 1)
            else:
                pe.wait_ge(gla_lo, TB)
            row_gran(pe, g, bank[0:4], act_q[:, :, c, :], c == 0, c == KC - 1)
            if c == 2:
                pe.wait_ge(gla_ready, 1)
                for b in range(TB):
                    for h in range(4):
                        o = (2 * b + h // 2) * P
                        mm = nc.tensor.transpose(bank[6 + b][:, h * P:(h + 1) * P], v_tok[:, h % 2, o:o + P],
                                                 ident[:, :])
                    mm.then_inc(gla_turned, 1)

        pe.wait_ge(res_mix2, 1)
        turn_pe(pe, 4, 2, nrm)
        pe.wait_ge(turn_lo, 3 * KC)
        in_of = {}
        for f in range(FC):
            in_of[GU[f] - 1], in_of[GU[f]] = (f, 0), (f, 1)
        out_of = {g: f for f, g in GO.items()}
        for g in range(G_FF, GEND):
            if g in in_of:
                f, up = in_of[g]
                if not up and f >= 4:
                    pe.wait_ge(f_prod, f - 3)
                turn_gran(pe, g, bank[f % 4][:, up * T:(up + 1) * T], act_p)
            else:
                f = out_of[g]
                pe.wait_ge(f_lo, f + 1)
                row_gran(pe, g, bank[4:8], act_q[:, :, f % 8, :], f == 0, f == FC - 1)


_OUTS = [((1, 256, 1024), "float32")]


def kernel(**inputs):
    import numpy as _np
    import concourse.bacc as _bacc
    from concourse import mybir as _mybir
    from concourse.bass_utils import run_bass_kernel_spmd as _run

    nc = _bacc.Bacc("TRN2", target_bir_lowering=False, num_devices=1)
    arrays, aps = {}, {}
    for name, value in inputs.items():
        a = _np.ascontiguousarray(value)
        arrays[f"in_{name}_dram"] = a
        ap = nc.dram_tensor(f"in_{name}_dram", a.shape, _mybir.dt.from_np(a.dtype), kind="ExternalInput").ap()
        aps[name] = ap if name in ("final_norm", "final_norm_2") else ap[0]
    out = nc.dram_tensor("out_0_dram", _OUTS[0][0], _mybir.dt.from_np(_np.dtype(_OUTS[0][1])),
                         kind="ExternalOutput").ap()
    two_block_layer(nc, aps.pop("x"), aps, out[0])
    r = _run(nc, [arrays], core_ids=[0])
    return r.results[0]["out_0_dram"]
```

```python
from contextlib import ExitStack

import numpy as np

import concourse.bass as bass
from concourse import mybir

F32 = mybir.dt.float32
F32R = mybir.dt.float32r
I32 = mybir.dt.int32
ALU = mybir.AluOpType
ACT = mybir.ActivationFunctionType
AX_X = mybir.AxisListType.X

P = 128
T = 256
TB = T // P
D = 1024
KC = D // P
EPS = 1e-6
SSD_W, HEADS, HD, STATE, GROUPS = 1024, 16, 64, 128, 2
GW = SSD_W // GROUPS
XBC = SSD_W + 2 * GROUPS * STATE
XC = XBC // P
O_XBC, O_DT = SSD_W, SSD_W + XBC
O_SCB = O_DT + HEADS
O_SCC, O_SCV = O_SCB + 1024, O_SCB + 2048
NG, EPG, NE, FF = 4, 8, 32, 512
CAP = 32
ROUND = NE * CAP
LRU = 512
LC = LRU // P
O_LG, O_Q, O_K, O_V, O_G, O_Z = 512, 1024, 1280, 1536, 2048, 2560
RANK = 16
FF2 = 2816
FC = FF2 // P
UNIT = 4096
GR = 1024
SLOTS = 6

PCOLS, PROWS = {}, []
for _tile, _items in enumerate((
        (("norm_mix", 8), ("ssd_conv_w", 48), ("ssd_conv_b", 12), ("sc_conv_w", 24), ("sc_norm", 8),
         ("ssd_norm", 8), ("norm_ffn", 8)),
        (("norm1_2", 8), ("conv_w_2", 16), ("conv_b_2", 4), ("lru_ba_2", 4), ("lru_bi_2", 4),
         ("lru_lambda_2", 4), ("norm2_2", 8)))):
    _row = 0
    for _name, _n in _items:
        PCOLS[_name] = P * _tile + _row
        PROWS.append((_name, _tile, _row, _n))
        _row += _n
ROWS_A, ROWS_B = 116, 48


def bcast(ap, shape):
    return ap.broadcast_to(shape)


def two_block_layer(nc, x, w, out):
    with ExitStack() as ctx:
        build(nc, ctx, x, w, out)


def build(nc, ctx, x, w, out):
    def sb(name, shape, dt=F32, where=ctx):
        return where.enter_context(nc.sbuf_tensor(name, shape, dt))

    def sem(name):
        return ctx.enter_context(nc.semaphore(name))

    ring = sb("ring", [P, SLOTS, UNIT])
    with ExitStack() as same:
        down_b = sb("down_b", [P, UNIT], where=same)
    w_hi = sb("w_hi", [P, 2, GR], F32R)
    w_lo = sb("w_lo", [P, 2, GR], F32R)
    with ExitStack() as same:
        pair_d = sb("pair_d", [P, 2, UNIT], where=same)
    act_p = sb("act_p", [P, 2, KC, T], F32R)
    with ExitStack() as same:
        act_q = sb("act_q", [P, 2, KC, T], F32R, where=same)
    sc_f = sb("sc_f", [P, 2, KC, T])
    res = sb("res", [P, TB, D])
    ident = sb("ident", [P, P])
    m_le = sb("m_le", [P, P])
    m_gt = sb("m_gt", [P, P])
    ones = sb("ones", [P, P])
    blk64 = sb("blk64", [P, P])
    iota_f = sb("iota_f", [P, P])
    par = sb("par", [P, 2 * P])
    bc16 = sb("bc16", [P, 3, HEADS])
    w_dt = sb("w_dt", [P, KC, HEADS])
    w_z = sb("w_z", [P, KC, RANK])
    ws_hi = sb("ws_hi", [P, KC, 16], F32R)
    ws_lo = sb("ws_lo", [P, KC, 16], F32R)
    w_rt = sb("w_rt", [P, KC, NG + NE])
    w_al = sb("w_al", [RANK + 1, 256])
    sm = sb("sm", [P, 96])
    rounds_i = sb("rounds_i", [1, 2], I32)
    sp4 = sb("sp4", [P, 8, LC])

    bank = [ctx.enter_context(nc.psum_tensor(f"bank{i}", [P, 512], F32)) for i in range(8)]

    ph = ExitStack()
    xdt = sb("xdt", [P, TB, D], where=ph)
    x_tok = sb("x_tok", [P, TB, D], where=ph)
    z_tok = sb("z_tok", [P, TB, D], where=ph)
    bc_t = sb("bc_t", [P, 4, T], where=ph)
    cbm = sb("cbm", [P, GROUPS, 3, P], where=ph)
    seg_l = sb("seg_l", [P, 4, P], where=ph)
    seg_e = sb("seg_e", [P, 2, 4, P], where=ph)
    pad = sb("pad", [P, 3, T + 3], where=ph)
    cv = sb("cv", [P, 3, T], where=ph)
    prow = seg_l[:, 0:2, :]
    dt_t = sb("dt_t", [HEADS, T], where=ph)
    adt = sb("adt", [P, 8, TB, HEADS], where=ph)
    ef = sb("ef", [P, 2, HEADS], where=ph)
    ph.close()
    ph = ExitStack()
    tok = sb("tok", [P, TB, D], where=ph)
    x_t = sb("x_t", [P, 2, KC, P], where=ph)
    tok_t = x_t[:, :, :, :].rearrange("p a c t -> p (a c t)").rearrange("p (c t) -> p c t", c=KC)
    y_e = sb("y_e", [P, D], where=ph)
    fgain = sb("fgain", [P, D], where=ph)
    onehot = sb("onehot", [P, 2, TB, P], where=ph)
    gated = sb("gated", [P, TB, P], where=ph)
    gtmp = sb("gtmp", [P, TB, P], where=ph)
    gmat = sb("gmat", [P, T], where=ph)
    h_e = sb("h_e", [P, P], where=ph)
    h_t = sb("h_t", [P, P], where=ph)
    pos = sb("pos", [P, TB, 4], where=ph)
    with ExitStack() as same:
        down_a = sb("down_a", [P, UNIT], where=same)
    lgt = sb("lgt", [P, TB, NG + NE], where=ph)
    rt = sb("rt", [P, 12, TB, NE], where=ph)
    r8 = sb("r8", [P, 10, TB, EPG], where=ph)
    r1 = sb("r1", [P, 16, TB], where=ph)
    rank_i = sb("rank_i", [P, TB * NE + 1], I32, where=ph)
    m_lt = sb("m_lt", [P, P], where=ph)
    ph.close()
    ph = ExitStack()
    lpad = sb("lpad", [P, LC, T + 3], where=ph)
    lx = sb("lx", [P, LC, T], where=ph)
    nrm = sb("nrm", [P, TB, D], where=ph)
    lgate = sb("lgate", [P, LC, T], where=ph)
    lr = nrm[:, 0, :].rearrange("p (c t) -> p c t", c=LC)
    lru_w = sb("lru_w", [P, 2, LC, P], where=ph)
    k_tok = sb("k_tok", [P, TB, 256], where=ph)
    v_tok = sb("v_tok", [P, TB, 512], where=ph)
    g_tok = sb("g_tok", [P, TB, 512], where=ph)
    q_t = sb("q_t", [P, 2, T], where=ph)
    la = sb("la", [P, TB, 256], where=ph)
    st = sb("st", [P, 4, 2, P], where=ph)
    m_gtc = sb("m_gtc", [P, P], where=ph)
    z_t = sb("z_t", [RANK + 1, T], where=ph)
    gnorm = sb("gnorm", [P, P], where=ph)
    dec = sb("dec", [P, 2, 4], where=ph)
    fg2 = v_tok[:, :, :].rearrange("p b n -> p (b n)")
    ph.close()

    units = []
    grans = []

    def whole(u):
        return ring[:, u % SLOTS, :]

    def cols_unit(wt, *spans):
        u = len(units)
        parts, at = [], 0
        for c0, n in spans:
            dst = whole(u).rearrange("p (k n) -> p k n", k=KC)[:, :, at:at + n]
            parts.append((dst, wt.rearrange("(k p) n -> p k n", p=P)[:, :, c0:c0 + n]))
            at += n
        units.append(parts)
        return u

    def rows_unit(wt, chunk, n):
        u = len(units)
        dst = whole(u)[:, 0:n * D].rearrange("p (k n) -> p k n", k=n)
        src = wt[chunk * P:(chunk + n) * P, :].rearrange("(k p) n -> p k n", p=P)
        units.append([(dst, src)])
        return u

    def turn_grans(u, js):
        for j in js:
            grans.append((u, whole(u).rearrange("p (k n) -> p k n", k=KC)[:, :, j * P:(j + 1) * P], None))

    def flow_grans(u, c0, n):
        kn = GR // n
        for k in range(0, KC, kn):
            grans.append((u, whole(u).rearrange("p (k n) -> p k n", k=KC)[:, k:k + kn, c0:c0 + n], None))

    def row_grans(u, gains):
        for j, gain in enumerate(gains):
            grans.append((u, whole(u)[:, j * GR:(j + 1) * GR], gain))

    def sc_raw(c0, c1):
        return sc_f[:, 1, c0:c1, :]

    def pcol(name, i):
        return par[:, PCOLS[name] + i:PCOLS[name] + i + 1]

    for c in range(3):
        turn_grans(cols_unit(w["w_in"], (O_XBC + 512 * c, 512)), range(4))
    for c in range(2):
        flow_grans(cols_unit(w["w_in"], (512 * c, 512)), 0, 512)
    for c in range(2):
        for o in (O_SCC, O_SCV, O_SCB):
            turn_grans(cols_unit(w["w_in"], (o + 512 * c, 512)), range(4))
    G_Z, G_SC, G_WO = 12, 20, 44
    MIX = [8, 9, 10, 11, 0, 1, 2, 3, 4, 5, 6, 7, 12, 13, 14, 15]
    for c in range(0, 16, 4):
        ks = MIX[c:c + 4]
        row_grans(rows_unit(w["w_out"], ks[0], 4),
                  [pcol("sc_norm", k - 8) if k >= 8 else pcol("ssd_norm", k) for k in ks])
    UA, GA = len(units), len(grans)
    G_Q, G_K, G_V, G_G, G_LG = GA + 4, GA + 6, GA + 8, GA + 12, GA + 16
    turn_grans(cols_unit(w["w_in_2"], (0, 512)), range(4))
    u = cols_unit(w["w_in_2"], (O_Q, 512))
    turn_grans(u, range(2))
    flow_grans(u, 256, 256)
    flow_grans(cols_unit(w["w_in_2"], (O_V, 512)), 0, 512)
    flow_grans(cols_unit(w["w_in_2"], (O_G, 512)), 0, 512)
    turn_grans(cols_unit(w["w_in_2"], (O_LG, 512)), range(4))
    G_WO2 = len(grans)
    for c in (0, 4):
        row_grans(rows_unit(w["w_out_2"], c, 4), [None] * 4)
    G_FF = len(grans)
    GU, GO = {}, {}

    def ffn_in(j):
        u = cols_unit(w["w_ffn_in_2"], (256 * j, 256), (FF2 + 256 * j, 256))
        for f in range(2):
            turn_grans(u, (f, 2 + f))
            GU[2 * j + f] = len(grans) - 1

    def ffn_out(f0, n):
        row_grans(rows_unit(w["w_ffn_out_2"], f0, n), [None] * n)
        for i in range(n):
            GO[f0 + i] = len(grans) - n + i

    for j in range(FC // 2):
        ffn_in(j)
        if j >= 2 and j % 2 == 0 and j < FC // 2 - 1:
            ffn_out(2 * j - 4, 4)
    ffn_out(16, 4)
    ffn_out(20, 2)
    GEND = len(grans)
    assert (UA, GA) == (15, 60) and sorted(GO) == list(range(FC)), sorted(GO)

    ld_x = sem("ld_x")
    ld_par = sem("ld_par")
    landed = [sem(f"landed{s}") for s in range(SLOTS)]
    landed_pair = [sem(f"landed_pair{n}") for n in range(2)]
    landed_down = [sem(f"landed_down{n}") for n in range(2)]
    const_ready = sem("const_ready")
    split_hi = sem("split_hi")
    split_lo = sem("split_lo")
    bank_done = sem("bank_done")
    gran_used = sem("gran_used")
    landed_c = [sem(f"landed_c{s}") for s in range(SLOTS)]
    dve_chain = sem("dve_chain")
    act_chain = sem("act_chain")
    pool_chain = sem("pool_chain")
    par_turned = sem("par_turned")
    par_ready = sem("par_ready")
    ss_act = sem("ss_act")
    ms_ready = sem("ms_ready")
    rstd_ready = sem("rstd_ready")
    nrm_dve = sem("nrm_dve")
    nrm_act = sem("nrm_act")
    turned = sem("turned")
    turn_hi = sem("turn_hi")
    turn_lo = sem("turn_lo")
    xbc_copied = sem("xbc_copied")
    conv_done = sem("conv_done")
    u_ready = sem("u_ready")
    silu_done = sem("silu_done")
    x_turned = sem("x_turned")
    x_kept = sem("x_kept")
    narrow_hi = sem("narrow_hi")
    narrow_lo = sem("narrow_lo")
    dt_raw = sem("dt_raw")
    dt_kept = sem("dt_kept")
    dt_ready = sem("dt_ready")
    ef_raw = sem("ef_raw")
    ef_ready = sem("ef_ready")
    cb_raw = sem("cb_raw")
    cb_ready = sem("cb_ready")
    xdt_ready = sem("xdt_ready")
    skip_ready = sem("skip_ready")
    seg_lhs = sem("seg_lhs")
    seg_raw = sem("seg_raw")
    seg_exp = sem("seg_exp")
    seg_m = sem("seg_m")
    y_raw = sem("y_raw")
    y_kept = sem("y_kept")
    xdt_decayed = sem("xdt_decayed")
    yoff_raw = sem("yoff_raw")
    yoff_kept = sem("yoff_kept")
    z_kept = sem("z_kept")
    zy_ready = sem("zy_ready")
    ssd_ss = sem("ssd_ss")
    ssd_ms = sem("ssd_ms")
    ssd_rstd = sem("ssd_rstd")
    ssd_norm = sem("ssd_norm")
    ssd_turned = sem("ssd_turned")
    ssd_hi = sem("ssd_hi")
    ssd_lo = sem("ssd_lo")
    c_kept = sem("c_kept")
    v_used = sem("v_used")
    b_used = sem("b_used")
    sc_sq = sem("sc_sq")
    sc_sum = sem("sc_sum")
    sc_log = sem("sc_log")
    sc_rstd = sem("sc_rstd")
    sc_scaled = sem("sc_scaled")
    sc_hi = sem("sc_hi")
    sc_lo = sem("sc_lo")
    res_mix = sem("res_mix")
    stored = sem("stored")

    ld_fgain = sem("ld_fgain")
    tok_turned = sem("tok_turned")
    tok_act = sem("tok_act")
    tok_dve = sem("tok_dve")
    logits_raw = sem("logits_raw")
    member = sem("member")
    rank_raw = sem("rank_raw")
    gmat_raw = sem("gmat_raw")
    gmat_kept = sem("gmat_kept")
    routed = sem("routed")
    built = sem("built")
    xt_raw = sem("xt_raw")
    xt_kept = sem("xt_kept")
    gu_raw = sem("gu_raw")
    gate_silu = sem("gate_silu")
    h_ready = sem("h_ready")
    ht_raw = sem("ht_raw")
    ht_kept = sem("ht_kept")
    ye_raw = sem("ye_raw")
    ye_act = sem("ye_act")
    ye_dve = sem("ye_dve")
    moe_raw = sem("moe_raw")
    moe_added = sem("moe_added")
    res_moe = sem("res_moe")
    res_mid = sem("res_mid")

    ld_c = sem("ld_c")
    sq_done = sem("sq_done")
    z_raw = sem("z_raw")
    zt_kept = sem("zt_kept")
    zf_raw = sem("zf_raw")
    zf_kept = sem("zf_kept")
    zf_log = sem("zf_log")
    la_ready = sem("la_ready")
    suffix_raw = sem("suffix_raw")
    decay_exp = sem("decay_exp")
    kdec_ready = sem("kdec_ready")
    lx_copied = sem("lx_copied")
    lx_ready = sem("lx_ready")
    lg_raw = sem("lg_raw")
    lg_sig = sem("lg_sig")
    l_tanh = sem("l_tanh")
    l_exp = sem("l_exp")
    l_neg = sem("l_neg")
    l_sqrt = sem("l_sqrt")
    lru_scan = sem("lru_scan")
    lgate_kept = sem("lgate_kept")
    lru_prod = sem("lru_prod")
    lru_hi = sem("lru_hi")
    lru_lo = sem("lru_lo")
    q_kept = sem("q_kept")
    k_kept = sem("k_kept")
    v_kept = sem("v_kept")
    g_kept = sem("g_kept")
    g_gain = sem("g_gain")
    upd_raw = sem("upd_raw")
    st_ready = sem("st_ready")
    o_raw = sem("o_raw")
    o_sq = sem("o_sq")
    o_ms = sem("o_ms")
    o_rstd = sem("o_rstd")
    gla_ready = sem("gla_ready")
    gla_turned = sem("gla_turned")
    gla_hi = sem("gla_hi")
    gla_lo = sem("gla_lo")
    res_mix2 = sem("res_mix2")
    f_silu = sem("f_silu")
    f_prod = sem("f_prod")
    f_hi = sem("f_hi")
    f_lo = sem("f_lo")
    res_ffn = sem("res_ffn")
    gained = sem("gained")

    exp_ready = sem("exp_ready")

    neg_abs = sem("neg_abs")

    margin = sem("margin")

    neg_half = sm[:, 8:24]
    N_ROWS_A = sum(tile == 0 for _, tile, _, _ in PROWS)
    N_SMALL = len(PROWS) + 3 + 2 + 1 + NG + 2

    def counter(semaphore):
        n = [0]

        def link(eng, ins):
            n[0] += 1
            ins.then_inc(semaphore, 1)
            eng.wait_ge(semaphore, n[0])
        return link

    link_dve, link_act, link_pool = counter(dve_chain), counter(act_chain), counter(pool_chain)

    def norm_act(act, n, src, dst, block_1=None, meanwhile=()):
        nc.scalar.activation(dst[:, 0, :], src[:, 0, :], ACT.Square, accum_out=sm[:, 0:1]).then_inc(ss_act, 1)
        for g in meanwhile:
            hi(act, g)
        if block_1 is not None:
            act.wait_ge(*block_1)
        act.wait_ge(rstd_ready, n + 1)
        nc.scalar.activation(dst[:, 1, :], src[:, 1, :], ACT.Copy, scale=sm[:, 5:6]).then_inc(nrm_act, 1)

    def norm_dve(dve, n, src, dst, meanwhile=()):
        link_dve(dve, nc.vector.tensor_tensor_reduce(
            out=dst[:, 1, :], in0=src[:, 1, :], in1=src[:, 1, :], scale=1.0, scalar=0.0,
            op0=ALU.mult, op1=ALU.add, accum_out=sm[:, 1:2]))
        dve.wait_ge(ss_act, n + 1)
        nc.vector.tensor_scalar(sm[:, 2:4], sm[:, 0:2], 1.0 / D, EPS, ALU.mult, ALU.add).then_inc(ms_ready, 1)
        for g in meanwhile:
            lo(dve, g)
        dve.wait_ge(rstd_ready, n + 1)
        nc.vector.tensor_scalar(dst[:, 0, :], src[:, 0, :], sm[:, 4:5], None, ALU.mult).then_inc(nrm_dve, 1)

    def norm_pool(pool, n):
        pool.wait_ge(ms_ready, n + 1)
        nc.gpsimd.tensor_tensor(sm[:, 4:6], sm[:, 2:4], neg_half[:, 0:2], ALU.pow).then_inc(rstd_ready, 1)

    def turn_pe(pe, n, t, src):
        pe.wait_ge(nrm_act, n + 1)
        pe.wait_ge(nrm_dve, n + 1)
        for c in range(KC):
            if t == 0 and TURN_BANK[c] == 4:
                pe.wait_ge(par_ready, 1)
            for b in range(TB):
                mm = nc.tensor.transpose(bank[TURN_BANK[c]][:, b * P:(b + 1) * P], src[:, b, c * P:(c + 1) * P], ident[:, :])
            mm.then_inc(turned, 1)

    def turn_act(act, t, gain):
        for c in range(KC):
            act.wait_ge(turned, KC * t + c + 1)
            nc.scalar.activation(act_p[:, 0, c, :], bank[TURN_BANK[c]][:, 0:T], ACT.Copy,
                                 scale=pcol(gain, c)).then_inc(turn_hi, 1)

    def turn_dve(dve, t, gain):
        for c in range(KC):
            dve.wait_ge(turn_hi, KC * t + c + 1)
            nc.vector.scalar_tensor_tensor(out=act_p[:, 1, c, :], in0=bank[TURN_BANK[c]][:, 0:T],
                                           scalar=pcol(gain, c), in1=act_p[:, 0, c, :].bitcast(F32), op0=ALU.mult,
                                           op1=ALU.subtract).then_inc(turn_lo, 1)

    def parts(tile, g, view):
        if len(view.shape) == 2:
            return tile[:, g % 2, :]
        return tile[:, g % 2, :].rearrange("p (k n) -> p k n", k=view.shape[1])

    def landed_wait(eng, g):
        u = grans[g][0]
        if g == 0 or grans[g - 1][0] != u:
            eng.wait_ge(*unit_landed(u))

    def unit_landed(u):
        if u < UA:
            return landed[u % SLOTS], 16 * PARTS_OF[u]
        return landed_c[u % SLOTS], 16 * PARTS_OF[u]

    def hi(act, g):
        u, view, gain = grans[g]
        landed_wait(act, g)
        if g >= 2:
            act.wait_ge(gran_used, g - 1)
        if gain is None:
            nc.scalar.activation(parts(w_hi, g, view), view, ACT.Copy).then_inc(split_hi, 1)
        else:
            nc.scalar.activation(parts(w_hi, g, view), view, ACT.Copy, scale=gain).then_inc(split_hi, 1)

    def lo(dve, g):
        u, view, gain = grans[g]
        landed_wait(dve, g)
        dve.wait_ge(split_hi, g + 1)
        h = parts(w_hi, g, view).bitcast(F32)
        if gain is None:
            nc.vector.tensor_tensor(parts(w_lo, g, view), view, h, ALU.subtract).then_inc(split_lo, 1)
        else:
            nc.vector.scalar_tensor_tensor(out=parts(w_lo, g, view), in0=view, scalar=gain, in1=h,
                                           op0=ALU.mult, op1=ALU.subtract).then_inc(split_lo, 1)

    PASSES = ((w_hi, 0), (w_hi, 1), (w_lo, 0))

    def turn_gran(pe, g, dst, a, t=None):
        pe.wait_ge(split_lo, g + 1)
        pe.wait_ge(split_hi, g + 1)
        for k in range(KC):
            if t is not None:
                pe.wait_ge(turn_lo, KC * t + k + 1)
            for i, (wt, x_part) in enumerate(PASSES):
                mm = nc.tensor.matmul(dst, parts(wt, g, grans[g][1])[:, k, :], a[:, x_part, k, :],
                                      start=(k == 0 and i == 0), stop=(k == KC - 1 and i == 2))
        mm.then_inc(gran_used, 1)

    def flow_gran(pe, g, dsts, a, k0):
        pe.wait_ge(split_lo, g + 1)
        pe.wait_ge(split_hi, g + 1)
        kn = grans[g][1].shape[1]
        for k in range(kn):
            for b in range(TB):
                for i, (wt, x_part) in enumerate(PASSES):
                    mm = nc.tensor.matmul(dsts[b], a[:, x_part, k0 + k, b * P:(b + 1) * P],
                                          parts(wt, g, grans[g][1])[:, k, :],
                                          start=(k0 + k == 0 and i == 0), stop=(k0 + k == KC - 1 and i == 2))
        mm.then_inc(gran_used, 1)

    def narrow_gran(pe, dst):
        for k in range(KC):
            for i, (wt, x_part) in enumerate(((ws_hi, 0), (ws_hi, 1), (ws_lo, 0))):
                mm = nc.tensor.matmul(dst, wt[:, k, :], act_p[:, x_part, k, :], start=(k == 0 and i == 0),
                                      stop=(k == KC - 1 and i == 2))
        return mm

    def row_gran(pe, g, banks, a_chunk, first, last, free=None):
        pe.wait_ge(split_lo, g + 1)
        pe.wait_ge(split_hi, g + 1)
        for b in range(TB):
            for half in range(2):
                if free is not None:
                    pe.wait_ge(free[0], free[1] + 2 * b + half)
                for i, (wt, x_part) in enumerate(PASSES):
                    mm = nc.tensor.matmul(banks[2 * b + half][:, :], a_chunk[:, x_part, b * P:(b + 1) * P],
                                          wt[:, g % 2, half * 512:(half + 1) * 512],
                                          start=(first and i == 0), stop=(last and i == 2))
                if last and 2 * b + half < 3:
                    mm.then_inc(bank_done, 1)
        mm.then_inc(gran_used, 1)

    def add_res(dve, n, g, banks, done, then=None):
        for b in range(TB):
            for half in range(2):
                r = res[:, b, half * 512:(half + 1) * 512]
                if 2 * b + half < 3:
                    dve.wait_ge(bank_done, 3 * n + 2 * b + half + 1)
                else:
                    dve.wait_ge(gran_used, g + 1)
                ins = nc.vector.tensor_tensor(r, r, banks[2 * b + half][:, :], ALU.add)
            ins.then_inc(done, 1)
            if then is not None:
                then(b)

    def log1p_pool(pool, u, u2, q, dst, add):
        link_pool(pool, nc.gpsimd.tensor_tensor(u2, u, u, ALU.mult))
        link_pool(pool, nc.gpsimd.tensor_scalar(q, u2, 1.0 / 15, 1.0 / 13, ALU.mult, ALU.add))
        for n in (11, 9, 7, 5, 3, 1):
            link_pool(pool, nc.gpsimd.tensor_tensor(q, q, u2, ALU.mult))
            link_pool(pool, nc.gpsimd.tensor_scalar(q, q, 1.0 / n, None, ALU.add))
        link_pool(pool, nc.gpsimd.tensor_tensor(q, q, u, ALU.mult))
        link_pool(pool, nc.gpsimd.tensor_scalar(q, q, 2.0, None, ALU.mult))
        link_pool(pool, nc.gpsimd.tensor_tensor(dst, q, add, ALU.add))

    PARTS_OF = []
    uses = [0] * SLOTS
    for u in range(UA):
        uses[u % SLOTS] += len(units[u])
        PARTS_OF.append(uses[u % SLOTS])

    uses_c = [0] * SLOTS
    for u in range(UA, len(units)):
        uses_c[u % SLOTS] += len(units[u])
        PARTS_OF.append(uses_c[u % SLOTS])

    last_gran = {}
    for g, (u, _, _) in enumerate(grans):
        last_gran[u] = g

    PAIR = (ring[:, 4:6, :], ring[:, 2:4, :], ring[:, 0:2, :], pair_d[:, :, :])
    DOWN = (down_a, down_b)
    PAIR_SLOT = (4, 2, 0)
    TURN_BANK = (0, 1, 2, 3, 5, 6, 7, 4)
    M_BANK = (1, 3, 7, 1)

    def pair_landed(i, n, turn):
        if i == 3:
            return landed_pair[n], 16 * turn
        s = PAIR_SLOT[i] + n
        return landed[s], 16 * turn + 16 * uses[s]

    block = ctx.enter_context(nc.Block())

    def load_rows(eng, tile_now):
        for name, tile, row, n in PROWS:
            if tile == tile_now:
                v = w[name]
                v = v.rearrange("a (c j) -> (a c) j", j=P) if len(v.shape) == 2 else v.rearrange("(c j) -> c j", j=P)
                eng.dma_start(prow[row:row + n, tile, :], v).then_inc(ld_par, 16)

    def load_small(eng):
        load_rows(eng, 1)
        for i, name in enumerate(("dt_bias", "a_log", "d_skip")):
            eng.dma_start(bc16[:, i, :], w[name].partition_broadcast(P)).then_inc(ld_par, 16)
        eng.dma_start(w_dt[:, :, :], w["w_in"].rearrange("(k p) n -> p k n", p=P)[:, :, O_DT:O_DT + HEADS])\
           .then_inc(ld_par, 16)
        eng.dma_start(w_z[:, :, :], w["w_in_2"].rearrange("(k p) n -> p k n", p=P)[:, :, O_Z:O_Z + RANK])\
           .then_inc(ld_par, 16)
        eng.dma_start(w_rt[:, :, 0:NG], w["w_router_group"].rearrange("(k p) g -> p k g", p=P)).then_inc(ld_par, 16)
        for g in range(NG):
            eng.dma_start(w_rt[:, :, NG + g * EPG:NG + (g + 1) * EPG],
                          w["w_router_expert"][g].rearrange("(k p) e -> p k e", p=P)).then_inc(ld_par, 16)
        eng.dma_start(w_al[0:RANK, :], w["gla_w_alpha_2"]).then_inc(ld_par, 16)
        eng.dma_start(w_al[RANK:RANK + 1, :], w["gla_b_alpha_2"].unsqueeze(0)).then_inc(ld_par, 16)

    @block.sync
    def _(sp):
        sp.dma_start(res[:, :, :], x.rearrange("(b p) d -> p b d", p=P)).then_inc(ld_x, 16)
        sp.wait_ge(ld_par, 16 * N_ROWS_A)
        for u in range(UA):
            if u >= SLOTS:
                sp.wait_ge(split_hi, last_gran[u - SLOTS] + 1)
                sp.wait_ge(split_lo, last_gran[u - SLOTS] + 1)
            for dst, src in units[u]:
                sp.dma_start(dst, src).then_inc(landed[u % SLOTS], 16)
            if u < 2:
                sp.wait_ge(*unit_landed(u))
            if u == 1:
                load_small(sp)

        def load_half(i, n, e):
            sp.dma_start(PAIR[i][:, n, :].rearrange("p (k n) -> p k n", k=KC),
                         w[("w_gate", "w_up")[n]][e].rearrange("(k p) n -> p k n", p=P))\
              .then_inc(landed_pair[n] if i == 3 else landed[PAIR_SLOT[i] + n], 16)

        def load_down(i, e):
            sp.dma_start(DOWN[i % 2][:, :].rearrange("p (k n) -> p k n", k=FF // P),
                         w["w_down"][e].rearrange("(k p) n -> p k n", p=P)).then_inc(landed_down[i % 2], 16)

        def load_expert(i, used, e, e_down):
            sp.wait_ge(gu_raw, used)
            load_half(i, 0, e)
            load_half(i, 1, e)
            sp.wait_ge(ye_raw, used)
            load_down(i, e_down)

        for i, n in ((1, 1), (0, 0), (0, 1), (2, 0), (2, 1), (1, 0)):
            u = max(u for u in range(UA) if u % SLOTS == PAIR_SLOT[i] + n)
            sp.wait_ge(split_hi, last_gran[u] + 1)
            sp.wait_ge(split_lo, last_gran[u] + 1)
            load_half(i, n, i)
        sp.wait_ge(gran_used, GA)
        load_half(3, 0, 3)
        load_half(3, 1, 3)
        load_down(1, 1)
        sp.wait_ge(routed, 1)
        load_down(0, 0)
        sp.dma_start(fgain[:, :], w["final_norm"].partition_broadcast(P)).then_inc(ld_fgain, 16)
        with sp.Fori(1, NE // 4) as j:
            for i in range(4):
                load_expert(i, 4 * j + i - 3, 4 * j + i, 4 * j + i - 2)
        n_rounds = sp.value_load(rounds_i[0:1, 0:1], min_val=1, max_val=T // CAP)
        with sp.If(n_rounds > 1):
            with sp.Fori(1, n_rounds) as r:
                for i in range(4):
                    load_expert(i, NE * r + i - 3, i, (i - 2) % NE)
                with sp.Fori(1, NE // 4) as j:
                    for i in range(4):
                        load_expert(i, NE * r + 4 * j + i - 3, 4 * j + i, 4 * j + i - 2)
        before_third = sp.value_load(rounds_i[0:1, 1:2], min_val=NE - 3, max_val=NE * T // CAP - 3)
        for i in range(2):
            sp.wait_ge(ye_raw, before_third + i)
            load_down(i, NE - 2 + i)
        for u in range(UA, len(units)):
            s = u % SLOTS
            if u < UA + SLOTS:
                sp.wait_ge(gu_raw, before_third + {4: 0, 2: 1, 0: 2}[s - s % 2])
            else:
                sp.wait_ge(split_hi, last_gran[u - SLOTS] + 1)
                sp.wait_ge(split_lo, last_gran[u - SLOTS] + 1)
            for dst, src in units[u]:
                sp.dma_start(dst, src).then_inc(landed_c[s], 16)
            if u == UA + SLOTS - 1:
                sp.wait_ge(const_ready, 5)
                for n, name in enumerate(("lru_wa_2", "lru_wi_2")):
                    for q in range(2):
                        lo_, hi_ = 64 * q, 64 * q + 64
                        sp.dma_start(lru_w[lo_:hi_, n, :, lo_:hi_],
                                     w[name].rearrange("(c q) i j -> q i c j", q=2)[q]).then_inc(ld_c, 16)
                sp.dma_start(gnorm[:, :], w["gla_norm_2"].partition_broadcast(P)).then_inc(ld_c, 16)
        for b in range(TB):
            sp.wait_ge(nrm_dve if b == 0 else nrm_act, 5)
            sp.dma_start(out[b * P:(b + 1) * P, :], nrm[:, b, :]).then_inc(stored, 16)
        sp.wait_ge(stored, 16 * TB)

    @block.gpsimd
    def _(pool):
        def mask(tile, op, step, mult, base=0):
            link_pool(pool, nc.gpsimd.memset(tile, 1.0))
            link_pool(pool, nc.gpsimd.affine_select(out=tile, in_=tile, compare_op=op, fill=0.0, base=base,
                                                    pattern=[[step, P]], channel_multiplier=mult))
        nc.gpsimd.memset(neg_half, -0.5)
        mask(ident[:, :], ALU.is_equal, 1, -1)
        nc.gpsimd.memset(ones[:, :], 1.0)
        nc.gpsimd.iota(iota_f[:, :], pattern=[[1, P]], base=0, channel_multiplier=0,
                       allow_small_or_imprecise_dtypes=True)
        nc.gpsimd.memset(pad[:, :, 0:3], 0.0).then_inc(const_ready, 1)
        norm_pool(pool, 0)
        mask(m_le[:, :], ALU.is_ge, 1, -1)
        mask(m_gt[:, :], ALU.is_gt, -1, 1)
        link_pool(pool, nc.gpsimd.memset(blk64[:, :], 1.0))
        v = blk64[:, :].rearrange("p (a j) -> p a j", a=2)
        link_pool(pool, nc.gpsimd.affine_select(out=v, in_=v, compare_op=ALU.is_ge, fill=0.0, base=0,
                                                pattern=[[-64, 2], [0, 64]], channel_multiplier=1))
        nc.gpsimd.affine_select(out=v, in_=v, compare_op=ALU.is_ge, fill=0.0, base=63,
                                pattern=[[64, 2], [0, 64]], channel_multiplier=-1).then_inc(const_ready, 1)

        pool.wait_ge(u_ready, 1)
        log1p_pool(pool, adt[:, 4, :, :], adt[:, 5, :, :], adt[:, 2, :, :], adt[:, 7, :, :], adt[:, 1, :, :])
        pool.wait_ge(exp_ready, 3)
        link_pool(pool, nc.gpsimd.tensor_tensor(adt[:, 0, :, :], adt[:, 7, :, :],
                                                bcast(adt[:, 6, 0, :].unsqueeze(1), [P, TB, HEADS]), ALU.mult))
        nc.gpsimd.tensor_scalar(adt[:, 0, :, :], adt[:, 0, :, :], -1.0, None, ALU.mult).then_inc(dt_ready, 1)

        def seg_left(it):
            b, q = divmod(it, 4)
            if it == 0:
                pool.wait_ge(dt_ready, 1)
                pool.wait_ge(par_turned, 2)
            else:
                pool.wait_ge(seg_raw, it)
            nc.gpsimd.tensor_tensor(seg_l[:, :, :], bcast(m_gt[:, :].unsqueeze(1), [P, 4, P]),
                                    bcast(adt[:, 0, b, 4 * q:4 * q + 4].unsqueeze(2), [P, 4, P]),
                                    ALU.mult).then_inc(seg_lhs, 1)

        def mask_seg(it):
            b, q = divmod(it, 4)
            pool.wait_ge(seg_exp, it + 1)
            if it == 0:
                pool.wait_ge(cb_ready, GROUPS)
            nc.gpsimd.tensor_tensor(seg_e[:, it % 2, :, :], seg_e[:, it % 2, :, :],
                                    bcast(cbm[:, q // 2, 2 * b, :].unsqueeze(1), [P, 4, P]),
                                    ALU.mult).then_inc(seg_m, 1)

        def by_head(tile, b):
            return tile[:, b, :].rearrange("p (h d) -> p h d", h=HEADS)

        def gate_y(n):
            b, g = divmod(n, GROUPS)
            z = z_tok[:, b, g * GW:(g + 1) * GW]
            y = x_tok[:, b, g * GW:(g + 1) * GW]
            pool.wait_ge(z_kept, 4)
            pool.wait_ge(y_kept, n + 1)
            if b == 1:
                pool.wait_ge(yoff_kept, g + 1)
                link_pool(pool, nc.gpsimd.tensor_tensor(y, y, xdt[:, 1, g * GW:(g + 1) * GW], ALU.add))
            nc.gpsimd.tensor_tensor(z, z, y, ALU.mult).then_inc(zy_ready, 1)

        def rstd_y(n):
            pool.wait_ge(ssd_ms, n + 1)
            nc.gpsimd.tensor_tensor(sm[:, 32 + n:33 + n], sm[:, 28 + n:29 + n], neg_half[:, 0:1],
                                    ALU.pow).then_inc(ssd_rstd, 1)

        seg_left(0)
        pool.wait_ge(x_kept, KC)
        for b in range(TB):
            ins = nc.gpsimd.tensor_tensor(by_head(xdt, b), by_head(x_tok, b),
                                          bcast(adt[:, 7, b, :].unsqueeze(2), [P, HEADS, HD]), ALU.mult)
        ins.then_inc(xdt_ready, 1)
        for it in range(9):
            if 1 <= it < 8:
                seg_left(it)
            if it >= 1:
                mask_seg(it - 1)
            if it == 0:
                pool.wait_ge(xdt_ready, 1)
            if it < TB:
                v = by_head(x_tok, it)
                nc.gpsimd.tensor_tensor(v, v, bcast(bc16[:, 2, :].unsqueeze(2), [P, HEADS, HD]),
                                        ALU.mult).then_inc(skip_ready, 1)
            if it == 5:
                pool.wait_ge(y_raw, 4)
                pool.wait_ge(ef_ready, 1)
                nc.gpsimd.tensor_tensor(by_head(xdt, 0), by_head(xdt, 0),
                                        bcast(ef[:, 0, :].unsqueeze(2), [P, HEADS, HD]),
                                        ALU.mult).then_inc(xdt_decayed, 1)
            if it == 7:
                gate_y(0)
                gate_y(1)
        rstd_y(0)
        rstd_y(1)
        gate_y(2)
        gate_y(3)
        rstd_y(2)
        rstd_y(3)
        pool.wait_ge(u_ready, 2)
        log1p_pool(pool, sp4[:, 2, :], sp4[:, 3, :], sp4[:, 4, :], sp4[:, 5, :], sp4[:, 6, :])
        nc.gpsimd.tensor_scalar(sp4[:, 7, :], sp4[:, 5, :], -4.0, None, ALU.mult)
        nc.gpsimd.tensor_scalar(sp4[:, 4, :], sp4[:, 5, :], -8.0, None, ALU.mult).then_inc(const_ready, 1)
        pool.wait_ge(res_mix, 2)
        link_pool(pool, nc.gpsimd.memset(m_lt[:, :], 1.0))
        nc.gpsimd.affine_select(out=m_lt[:, :], in_=m_lt[:, :], compare_op=ALU.is_gt, fill=0.0, base=0,
                                pattern=[[1, P]], channel_multiplier=-1).then_inc(const_ready, 1)
        norm_pool(pool, 1)
        pool.wait_ge(ms_ready, 3)
        nc.gpsimd.tensor_tensor(sm[:, 80:84], sm[:, 76:80], neg_half[:, 0:4], ALU.pow).then_inc(rstd_ready, 1)
        pool.wait_ge(res_mid, 1)
        nc.gpsimd.memset(lru_w[:, :, :, :], 0.0).then_inc(const_ready, 1)
        link_pool(pool, nc.gpsimd.memset(lpad[:, :, 0:3], 0.0))
        link_pool(pool, nc.gpsimd.memset(z_t[:, :], 1.0))
        link_pool(pool, nc.gpsimd.tensor_tensor(m_gtc[:, :], m_gt[:, :], blk64[:, :], ALU.mult))
        nc.gpsimd.memset(sm[:, 64:65], 1.0).then_inc(const_ready, 1)
        pool.wait_ge(g_kept, 2)
        pool.wait_ge(ld_c, 16 * 5)
        v = g_tok[:, :, :].rearrange("p b (h d) -> p (b h) d", h=4)
        nc.gpsimd.tensor_tensor(v, v, bcast(gnorm[:, :].unsqueeze(1), [P, 8, P]), ALU.mult).then_inc(g_gain, 1)
        pool.wait_ge(o_ms, 1)
        nc.gpsimd.tensor_tensor(sm[:, 56:64], sm[:, 48:56], neg_half[:, 0:8], ALU.pow).then_inc(o_rstd, 1)
        norm_pool(pool, 3)
        norm_pool(pool, 4)

    @block.scalar
    def _(act):
        load_rows(act, 0)
        act.wait_ge(ld_x, 16)
        norm_act(act, 0, res, xdt)
        act.wait_ge(par_turned, 1)
        nc.scalar.activation(par[:, 0:ROWS_A], bank[4][:, 0:ROWS_A], ACT.Copy).then_inc(par_ready, 1)
        act.wait_ge(par_ready, 1)
        turn_act(act, 0, "norm_mix")

        def copy_xbc(i):
            act.wait_ge(gran_used, i + 1)
            if 3 <= i < KC + 3:
                act.wait_ge(x_turned, i - 2)
            elif i >= KC + 3:
                act.wait_ge(silu_done, i - 2)
            nc.scalar.activation(pad[:, i % 3, 3:T + 3], bank[i % 4][:, 0:T], ACT.Copy)
            nc.scalar.activation(cv[:, i % 3, :], bank[i % 4][:, 0:T], ACT.Copy,
                                 scale=pcol("ssd_conv_w", 3 * XC + i)).then_inc(xbc_copied, 1)

        def silu_xbc(i):
            act.wait_ge(conv_done, i + 1)
            dst = cv[:, i % 3, :] if i < KC else bc_t[:, i - KC, :]
            nc.scalar.activation(dst, cv[:, i % 3, :], ACT.Silu, bias=pcol("ssd_conv_b", i)).then_inc(silu_done, 1)

        def keep_x(i):
            act.wait_ge(x_turned, i + 1)
            src = bank[4 + i % 2][:, 0:T].rearrange("p (b c) -> p b c", b=TB)
            nc.scalar.activation(x_tok[:, :, i * P:(i + 1) * P], src, ACT.Copy).then_inc(x_kept, 1)

        def keep_z(t):
            act.wait_ge(gran_used, G_Z + 4 * t + 4)
            for b in range(TB):
                nc.scalar.activation(z_tok[:, b, t * 512:(t + 1) * 512], bank[2 * t + b][:, :],
                                     ACT.Silu).then_inc(z_kept, 1)

        def exp_seg(it):
            act.wait_ge(seg_raw, it + 1)
            if it >= 2:
                act.wait_ge(y_raw, it - 1)
            nc.scalar.activation(seg_e[:, it % 2, :, :], bank[5][:, :].rearrange("p (h l) -> p h l", h=4),
                                 ACT.Exp).then_inc(seg_exp, 1)

        def keep_c(hf, j):
            act.wait_ge(gran_used, G_SC + 12 * hf + j + 1)
            nc.scalar.activation(sc_f[:, 1, 4 * hf + j, :], bank[j][:, 0:T],
                                 ACT.Copy).then_inc(c_kept, 1)

        def square_sc(hf, j):
            act.wait_ge(b_used, 4 * hf + j + 1)
            if 4 * hf + j >= 2:
                act.wait_ge(sc_sum, 4 * hf + j - 1)
            nc.scalar.activation(cv[:, j % 3, :], sc_f[:, 1, 4 * hf + j, :], ACT.Square).then_inc(sc_sq, 1)

        def log_sc(hf):
            act.wait_ge(sc_sum, 4 * hf + 4)
            for bk in (bank[4], bank[7]):
                nc.scalar.activation(bk[:, :], bk[:, :], ACT.Ln, scale=1.0 / 64, bias=sm[:, 24:25])\
                  .then_inc(sc_log, 1)

        def rstd_sc(hf):
            act.wait_ge(sc_log, 2 * hf + 2)
            for bk in (bank[4], bank[7]):
                nc.scalar.activation(bk[:, :], bk[:, :], ACT.Exp, scale=-0.5).then_inc(sc_rstd, 1)

        def hi_sc(hf):
            act.wait_ge(sc_scaled, hf + 1)
            nc.scalar.activation(act_q[:, 0, 4 * hf:4 * hf + 4, :], sc_raw(4 * hf, 4 * hf + 4),
                                 ACT.Copy).then_inc(sc_hi, 1)

        def square_y(n):
            b, g = divmod(n, GROUPS)
            act.wait_ge(zy_ready, n + 1)
            nc.scalar.activation(x_tok[:, b, g * GW:(g + 1) * GW], z_tok[:, b, g * GW:(g + 1) * GW], ACT.Square,
                                 accum_out=sm[:, 36 + n:37 + n]).then_inc(ssd_ss, 1)

        def hi_ssd(n):
            b, g = divmod(n, GROUPS)
            act.wait_ge(ssd_turned, n + 1)
            nc.scalar.activation(act_p[:, 0, 4 * g:4 * g + 4, b * P:(b + 1) * P],
                                 bank[5 + n % 2][:, :].rearrange("p (c t) -> p c t", c=4), ACT.Copy)\
              .then_inc(ssd_hi, 1)

        for g in range(GA):
            hi(act, g)
            if g == 8:
                act.wait_ge(ld_par, 16 * N_SMALL)
                nc.scalar.activation(ws_hi[:, :, :], w_dt[:, :, :], ACT.Copy).then_inc(narrow_hi, 1)
                act.wait_ge(par_turned, 2)
                nc.scalar.activation(par[:, P:P + ROWS_B], bank[7][:, 0:ROWS_B], ACT.Copy).then_inc(par_ready, 1)
            if g == G_Z:
                act.wait_ge(dt_raw, 1)
                nc.scalar.activation(dt_t[:, :], bank[7][0:HEADS, 0:T], ACT.Copy).then_inc(dt_kept, 1)
            if g == G_Z + 4:
                act.wait_ge(neg_abs, 1)
                nc.scalar.activation(sp4[:, 1, :], sp4[:, 0, :], ACT.Exp).then_inc(exp_ready, 1)
            if 2 <= g < 2 + XC:
                copy_xbc(g - 2)
            if 3 <= g < 3 + XC:
                silu_xbc(g - 3)
            if 5 <= g < 5 + KC:
                keep_x(g - 5)
            if g == G_Z + 4:
                act.wait_ge(neg_abs, 2)
                nc.scalar.activation(adt[:, 3, :, :], adt[:, 2, :, :], ACT.Exp).then_inc(exp_ready, 1)
                nc.scalar.activation(adt[:, 6, 0, :], bc16[:, 1, :], ACT.Exp).then_inc(exp_ready, 1)
            if g == G_Z + 5:
                keep_z(0)
            if g == G_Z + 9:
                keep_z(1)
                act.wait_ge(ef_raw, 1)
                nc.scalar.activation(ef[:, :, :], bank[7][:, 0:2 * HEADS].rearrange("p (a h) -> p a h", a=2),
                                     ACT.Exp).then_inc(ef_ready, 1)
            if G_SC + 2 <= g < G_SC + 18 and g % 2 == 0:
                exp_seg((g - G_SC - 2) // 2)
            for hf in range(2):
                base = G_SC + 12 * hf
                if base + 2 <= g < base + 6:
                    keep_c(hf, g - base - 2)
                if base + 11 <= g < base + 15:
                    square_sc(hf, g - base - 11)
            if g in (G_SC + 18, G_WO + 4):
                log_sc(g > G_WO)
            if g in (G_SC + 20, G_WO + 5):
                rstd_sc(g > G_WO)
            if g in (G_SC + 23, G_WO + 7):
                hi_sc(g > G_WO)
            if g in (G_SC + 19, G_SC + 23):
                for n in range(2):
                    square_y(n + 2 * (g == G_SC + 23))
            if g in (G_WO + 1, G_WO + 3):
                for n in range(2):
                    hi_ssd(n + 2 * (g == G_WO + 3))

        act.wait_ge(res_mix, 1)
        norm_act(act, 1, res, tok, (res_mix, 2))
        for c in range(0, KC, 2):
            act.wait_ge(tok_turned, c + 1)
            nc.scalar.activation(tok_t[:, c, :], bank[c % 4][:, 0:T], ACT.Copy,
                                 scale=pcol("norm_ffn", c)).then_inc(tok_act, 1)
        act.wait_ge(margin, 1)
        nc.scalar.activation(r8[:, 5, :, 0:NG], r8[:, 4, :, 0:NG], ACT.Exp).then_inc(exp_ready, 1)
        act.wait_ge(margin, 2)
        nc.scalar.activation(r1[:, 5, :], r1[:, 4, :], ACT.Exp).then_inc(exp_ready, 1)
        act.wait_ge(routed, 1)
        n_rounds = act.value_load(rounds_i[0:1, 0:1], min_val=1, max_val=T // CAP)

        def expert_act(x, e):
            act.wait_ge(gu_raw, x + 1)
            nc.scalar.activation(h_e[:, :], bank[0][:, 0:P], ACT.Silu).then_inc(gate_silu, 1)
            act.wait_ge(ht_raw, x + 1)
            nc.scalar.activation(h_t[:, :], bank[4][:, 0:P], ACT.Copy).then_inc(ht_kept, 1)
            act.wait_ge(ye_raw, x + 1)
            for j in range(2):
                ins = nc.scalar.activation(y_e[CAP * e:CAP * (e + 1), 256 * j:256 * (j + 1)],
                                           bank[2][CAP * j:CAP * (j + 1), 0:256], ACT.Copy)
            ins.then_inc(ye_act, 1)

        with act.Fori(0, n_rounds) as r:
            with act.Fori(0, NE // 4) as k:
                for e in range(4):
                    expert_act(NE * r + 4 * k + e, e)
        act.wait_ge(moe_added, NE * n_rounds + 1)
        spare = x_t[:, :, :, :].rearrange("p a c t -> p a (c t)")
        for b in range(TB):
            nc.scalar.activation(spare[:, b, :], res[:, b, :], ACT.Square, accum_out=sm[:, 72 + b:73 + b])
        act.wait_ge(res_moe, 1)
        nc.scalar.activation(y_e[:, :], tok[:, 0, :], ACT.Square, accum_out=sm[:, 74:75]).then_inc(ss_act, 1)
        for g in range(GA, GA + 2):
            hi(act, g)
        act.wait_ge(rstd_ready, 3)
        nc.scalar.activation(nrm[:, 1, :], tok[:, 1, :], ACT.Copy, scale=sm[:, 83:84]).then_inc(nrm_act, 1)

        nc.scalar.activation(ws_hi[:, :, :], w_z[:, :, :], ACT.Copy).then_inc(narrow_hi, 1)
        turn_act(act, 1, "norm1_2")
        li = lpad[:, :, 0:T]
        t1 = st[:, 0:2, :, :].rearrange("p n c d -> p n (c d)")
        la_f = nrm[:, 1, :].rearrange("p (c t) -> p c t", c=LC)

        def sigmoids(c):
            act.wait_ge(lg_raw, c + 1)
            nc.scalar.activation(lr[:, c, :], bank[4 + c % 2][:, 0:T], ACT.Sigmoid, bias=pcol("lru_ba_2", c))
            nc.scalar.activation(li[:, c, :], bank[4 + c % 2][:, T:2 * T], ACT.Sigmoid,
                                 bias=pcol("lru_bi_2", c)).then_inc(lg_sig, 1)

        for g in range(GA + 2, G_FF):
            hi(act, g)
            if g == GA + 2:
                act.wait_ge(const_ready, 6)
                act.wait_ge(z_raw, 1)
                nc.scalar.activation(z_t[0:RANK, :], bank[7][0:RANK, 0:T], ACT.Copy).then_inc(zt_kept, 1)
            if GA + 2 <= g < GA + 6:
                c = g - GA - 2
                act.wait_ge(gran_used, GA + c + 1)
                nc.scalar.activation(lpad[:, c, 3:T + 3], bank[c][:, 0:T], ACT.Copy).then_inc(lx_copied, 1)
            if g == GA + 5:
                act.wait_ge(zf_raw, 1)
                nc.scalar.activation(la[:, :, :], bank[6][:, :].rearrange("p (b n) -> p b n", b=TB),
                                     ACT.Copy).then_inc(zf_kept, 1)
            if g == GA + 6:
                act.wait_ge(neg_abs, 3)
                nc.scalar.activation(t1, t1, ACT.Exp).then_inc(exp_ready, 1)
            if g in (G_Q + 2, G_Q + 3):
                c = g - G_Q - 2
                act.wait_ge(gran_used, G_Q + c + 1)
                nc.scalar.activation(q_t[:, c, :], bank[c][:, 0:T], ACT.Copy, scale=0.125).then_inc(q_kept, 1)
            if g == GA + 7:
                act.wait_ge(exp_ready, 6)
                nc.scalar.activation(t1, t1, ACT.Ln, bias=1.0).then_inc(zf_log, 1)
            if g == GA + 8:
                sigmoids(0)
                sigmoids(1)
            if g == GA + 9:
                act.wait_ge(gran_used, G_K + 2)
                for b in range(TB):
                    ins = nc.scalar.activation(k_tok[:, b, :], bank[2 + b][:, 0:256], ACT.Copy)
                ins.then_inc(k_kept, 1)
            if g == GA + 12:
                act.wait_ge(suffix_raw, 1)
                act.wait_ge(la_ready, 1)
                nc.scalar.activation(t1, bank[6][:, :].rearrange("p (b n) -> p b n", b=TB), ACT.Exp,
                                     scale=1.0 / 16)
                nc.scalar.activation(dec[:, :, :], bank[7][:, 0:8].rearrange("p (c n) -> p c n", c=2), ACT.Exp,
                                     scale=1.0 / 16).then_inc(decay_exp, 1)
            if g == GA + 10:
                sigmoids(2)
                sigmoids(3)
                act.wait_ge(lg_sig, 4)
                act.wait_ge(const_ready, 3)
                for c in range(LC):
                    ins = nc.scalar.activation(lgate[:, c, :], lr[:, c, :], ACT.Tanh, scale=sp4[:, 7, c:c + 1])
                ins.then_inc(l_tanh, 1)
            if g == GA + 11:
                act.wait_ge(l_tanh, 1)
                for c in range(LC):
                    ins = nc.scalar.activation(la_f[:, c, :], lr[:, c, :], ACT.Exp, scale=sp4[:, 4, c:c + 1])
                ins.then_inc(l_exp, 1)
            if g == GA + 13:
                act.wait_ge(l_neg, 1)
                nc.scalar.activation(li, lgate[:, :, :], ACT.Sqrt).then_inc(l_sqrt, 1)
            if g == G_V + 5:
                act.wait_ge(gran_used, G_V + 4)
                for b in range(TB):
                    nc.scalar.activation(v_tok[:, b, :], bank[b][:, :], ACT.Copy).then_inc(v_kept, 1)
            if g == G_G + 4:
                act.wait_ge(gran_used, G_G + 4)
                for b in range(TB):
                    nc.scalar.activation(g_tok[:, b, :], bank[2 + b][:, :], ACT.Silu).then_inc(g_kept, 1)
            if G_LG + 1 <= g < G_LG + 5:
                c = g - G_LG - 1
                if c == 0:
                    act.wait_ge(l_sqrt, 1)
                act.wait_ge(gran_used, G_LG + c + 1)
                nc.scalar.activation(lgate[:, c, :], bank[c][:, 0:T], ACT.Gelu_apprx_tanh).then_inc(lgate_kept, 1)
            if g == G_LG + 2:
                act.wait_ge(o_raw, 1)
                act.wait_ge(upd_raw, 1)
                for n in range(2):
                    nc.scalar.activation(v_tok[:, n, :], bank[4 + n][:, :], ACT.Square).then_inc(o_sq, 1)
            if G_LG + 3 <= g < G_LG + 7:
                c = g - G_LG - 3
                act.wait_ge(lru_prod, c + 1)
                nc.scalar.activation(act_q[:, 0, c, :], nrm[:, 0, c * T:(c + 1) * T], ACT.Copy).then_inc(lru_hi, 1)
            if g == G_WO2 + 3:
                for b in range(TB):
                    act.wait_ge(gla_turned, b + 1)
                    nc.scalar.activation(act_q[:, 0, 4:8, b * P:(b + 1) * P],
                                         bank[6 + b][:, :].rearrange("p (c t) -> p c t", c=4), ACT.Copy)\
                      .then_inc(gla_hi, 1)
        hi(act, G_FF)
        act.wait_ge(res_mix2, 1)
        norm_act(act, 3, res, nrm, (res_mix2, 2), (G_FF + 1,))
        act.dma_start(fg2, w["final_norm_2"].partition_broadcast(P)).then_inc(ld_fgain, 16)
        turn_act(act, 2, "norm2_2")
        for g in range(G_FF + 2, GEND):
            hi(act, g)
            for f in range(FC):
                if g == GU[f] + 2:
                    act.wait_ge(gran_used, GU[f] + 1)
                    if f >= 4:
                        act.wait_ge(f_lo, f - 3)
                    nc.scalar.activation(lx[:, f % 4, :], bank[f % 4][:, 0:T], ACT.Silu).then_inc(f_silu, 1)
                if g == GU[f] + 3:
                    act.wait_ge(f_prod, f + 1)
                    if f >= 8:
                        act.wait_ge(gran_used, GO[f - 8] + 1)
                    nc.scalar.activation(act_q[:, 0, f % 8, :], lx[:, f % 4, :], ACT.Copy).then_inc(f_hi, 1)
        spare = lgate[:, :, :].rearrange("p c t -> p (c t)")
        for b in range(TB):
            act.wait_ge(res_ffn, b + 1)
            if b:
                act.wait_ge(sq_done, 1)
            ins = nc.scalar.activation(spare, res[:, b, :], ACT.Square, accum_out=sm[:, b:b + 1])
            ins.then_inc(sq_done if b == 0 else ss_act, 1)
        act.wait_ge(rstd_ready, 5)
        act.wait_ge(gained, 2)
        nc.scalar.activation(nrm[:, 1, :], nrm[:, 1, :], ACT.Copy, scale=sm[:, 5:6]).then_inc(nrm_act, 1)

    @block.vector
    def _(dve):
        dve.wait_ge(ld_x, 16)
        dve.wait_ge(const_ready, 1)
        link_dve(dve, nc.vector.memset(sm[:, 24:25], EPS))
        norm_dve(dve, 0, res, xdt)
        dve.wait_ge(par_ready, 1)
        turn_dve(dve, 0, "norm_mix")

        def lambda_start():
            dve.wait_ge(par_ready, 2)
            lam = par[:, PCOLS["lru_lambda_2"]:PCOLS["lru_lambda_2"] + LC]
            nc.vector.tensor_scalar(sp4[:, 6, :], lam, -1.0, 0.0, ALU.mult, ALU.max)
            nc.vector.scalar_tensor_tensor(out=sp4[:, 0, :], in0=lam, scalar=-1.0, in1=lam, op0=ALU.mult,
                                           op1=ALU.min).then_inc(neg_abs, 1)

        def lambda_quotient():
            dve.wait_ge(exp_ready, 1)
            quotient(sp4[:, 1, :], sp4[:, 2, :])

        def quotient(e, u):
            link_dve(dve, nc.vector.tensor_scalar(u, e, 2.0, None, ALU.add))
            link_dve(dve, nc.vector.reciprocal(u, u))
            nc.vector.tensor_tensor(u, u, e, ALU.mult).then_inc(u_ready, 1)

        def conv_xbc(i):
            dve.wait_ge(xbc_copied, i + 1)
            for tap in range(3):
                ins = nc.vector.scalar_tensor_tensor(out=cv[:, i % 3, :], in0=pad[:, i % 3, tap:tap + T],
                                                     scalar=pcol("ssd_conv_w", tap * XC + i), in1=cv[:, i % 3, :],
                                                     op0=ALU.mult, op1=ALU.add)
                if tap < 2:
                    link_dve(dve, ins)
            ins.then_inc(conv_done, 1)

        def dt_start():
            dve.wait_ge(dt_raw, 2)
            link_dve(dve, nc.vector.tensor_tensor(
                adt[:, 1, :, :], bank[6][:, 0:2 * HEADS].rearrange("p (b h) -> p b h", b=TB),
                bcast(bc16[:, 0, :].unsqueeze(1), [P, TB, HEADS]), ALU.add))
            nc.vector.scalar_tensor_tensor(out=adt[:, 2, :, :], in0=adt[:, 1, :, :], scalar=-1.0,
                                           in1=adt[:, 1, :, :], op0=ALU.mult, op1=ALU.min).then_inc(neg_abs, 1)
            dve.wait_ge(neg_abs, 2)
            nc.vector.tensor_scalar(adt[:, 1, :, :], adt[:, 1, :, :], 0.0, None, ALU.max)

        def dt_quotient():
            dve.wait_ge(exp_ready, 2)
            quotient(adt[:, 3, :, :], adt[:, 4, :, :])

        def keep_cb():
            for g in range(GROUPS):
                dve.wait_ge(cb_raw, g + 1)
                dve.wait_ge(const_ready, 2)
                bk = bank[5 + g]
                nc.vector.tensor_tensor(cbm[:, g, 0, :], bk[:, 0:P], m_le[:, :], ALU.mult)
                nc.vector.tensor_copy(cbm[:, g, 1, :], bk[:, P:2 * P])
                nc.vector.tensor_tensor(cbm[:, g, 2, :], bk[:, 2 * P:3 * P], m_le[:, :], ALU.mult)\
                  .then_inc(cb_ready, 1)

        def keep_y(n):
            b, g = divmod(n, GROUPS)
            dve.wait_ge(y_raw, 2 * n + 2)
            dve.wait_ge(skip_ready, TB)
            v = x_tok[:, b, g * GW:(g + 1) * GW]
            nc.vector.tensor_tensor(v, v, bank[6][:, :], ALU.add).then_inc(y_kept, 1)

        def keep_yoff(g):
            dve.wait_ge(yoff_raw, g + 1)
            t = xdt[:, 1, g * GW:(g + 1) * GW]
            dve.wait_ge(y_raw, 8)
            dve.wait_ge(ef_ready, 1)
            nc.vector.tensor_tensor(
                t.rearrange("p (h d) -> p h d", h=8), bank[5 + g][:, :].rearrange("p (h d) -> p h d", h=8),
                bcast(ef[:, 1, 8 * g:8 * g + 8].unsqueeze(2), [P, 8, HD]), ALU.mult).then_inc(yoff_kept, 1)

        def norm_y(n):
            b, g = divmod(n, GROUPS)
            dve.wait_ge(ssd_ss, n + 1)
            nc.vector.tensor_scalar(sm[:, 28 + n:29 + n], sm[:, 36 + n:37 + n], 1.0 / GW, EPS, ALU.mult,
                                    ALU.add).then_inc(ssd_ms, 1)

        def scale_y(n):
            b, g = divmod(n, GROUPS)
            z = z_tok[:, b, g * GW:(g + 1) * GW]
            dve.wait_ge(ssd_rstd, n + 1)
            nc.vector.tensor_scalar(z, z, sm[:, 32 + n:33 + n], None, ALU.mult).then_inc(ssd_norm, 1)

        def lo_ssd(n):
            b, g = divmod(n, GROUPS)
            dve.wait_ge(ssd_hi, n + 1)
            nc.vector.tensor_tensor(act_p[:, 1, 4 * g:4 * g + 4, b * P:(b + 1) * P],
                                    bank[5 + n % 2][:, :].rearrange("p (c t) -> p c t", c=4),
                                    act_p[:, 0, 4 * g:4 * g + 4, b * P:(b + 1) * P].bitcast(F32),
                                    ALU.subtract).then_inc(ssd_lo, 1)

        def conv_sc(hf, j):
            t = sc_f[:, 1, 4 * hf + j, :]
            dve.wait_ge(gran_used, G_SC + 12 * hf + 4 + j + 1)
            dve.wait_ge(c_kept, 4 * hf + j + 1)
            if hf == 0 and j == 0:
                dve.wait_ge(silu_done, XC)
            link_dve(dve, nc.vector.tensor_tensor(pad[:, j % 3, 3:T + 3], bank[j][:, 0:T], t, ALU.mult))
            for tap in range(3):
                wc = pcol("sc_conv_w", tap * 8 + 4 * hf + j)
                src = pad[:, j % 3, 1 + tap:1 + tap + T]
                if tap == 0:
                    link_dve(dve, nc.vector.tensor_scalar(t, src, wc, None, ALU.mult))
                    continue
                ins = nc.vector.scalar_tensor_tensor(out=t, in0=src, scalar=wc, in1=t, op0=ALU.mult, op1=ALU.add)
                if tap < 2:
                    link_dve(dve, ins)
            ins.then_inc(v_used, 1)

        def gate_sc(hf, j):
            t = sc_f[:, 1, 4 * hf + j, :]
            dve.wait_ge(gran_used, G_SC + 12 * hf + 8 + j + 1)
            dve.wait_ge(v_used, 4 * hf + j + 1)
            nc.vector.tensor_tensor(t, bank[j][:, 0:T], t, ALU.mult).then_inc(b_used, 1)

        def norm_sc(hf):
            for n, bk in enumerate((bank[4], bank[7])):
                dve.wait_ge(sc_rstd, 2 * hf + n + 1)
                v = sc_raw(4 * hf + 2 * n, 4 * hf + 2 * n + 2)
                ins = nc.vector.tensor_tensor(v, v, bk[:, :].rearrange("p (c t) -> p c t", c=2), ALU.mult)
            ins.then_inc(sc_scaled, 1)

        def lo_sc(hf):
            dve.wait_ge(sc_hi, hf + 1)
            nc.vector.tensor_tensor(act_q[:, 1, 4 * hf:4 * hf + 4, :], sc_raw(4 * hf, 4 * hf + 4),
                                    act_q[:, 0, 4 * hf:4 * hf + 4, :].bitcast(F32), ALU.subtract)\
              .then_inc(sc_lo, 1)

        for g in range(GA):
            for hf in range(2):
                if G_SC + 12 * hf + 10 <= g < G_SC + 12 * hf + 14:
                    gate_sc(hf, g - G_SC - 12 * hf - 10)
            lo(dve, g)
            if g == 9:
                lambda_start()
            if g == 8:
                dve.wait_ge(narrow_hi, 1)
                nc.vector.tensor_tensor(ws_lo[:, :, :], w_dt[:, :, :], ws_hi[:, :, :].bitcast(F32),
                                        ALU.subtract).then_inc(narrow_lo, 1)
            if 2 <= g < 2 + XC:
                conv_xbc(g - 2)
            if g == G_Z + 3:
                dt_start()
            if g == G_Z + 5:
                dt_quotient()
                lambda_quotient()
            if g == G_SC + 1:
                keep_cb()
            for hf in range(2):
                base = G_SC + 12 * hf
                if base + 6 <= g < base + 10:
                    conv_sc(hf, g - base - 6)
            if G_SC + 5 <= g < G_SC + 21 and (g - G_SC - 5) % 4 == 0:
                keep_y((g - G_SC - 5) // 4)
            if g in (G_SC + 19, G_SC + 20):
                keep_yoff(g - G_SC - 19)
            if g in (G_SC + 22, G_WO + 6):
                norm_sc(g > G_WO)
            if g in (G_SC + 23, G_WO + 8):
                lo_sc(g > G_WO)
            for h in range(2):
                for n in range(2 * h, 2 * h + 2):
                    if g == (G_SC + 21, G_WO)[h]:
                        norm_y(n)
                    if g == (G_SC + 22, G_WO + 1)[h]:
                        scale_y(n)
                    if g == (G_WO + 1, G_WO + 3)[h]:
                        lo_ssd(n)
        add_res(dve, 0, GA - 1, bank[0:4], res_mix)

        dve.wait_ge(res_mix, 2)
        norm_dve(dve, 1, res, tok)
        for c in range(1, KC, 2):
            dve.wait_ge(tok_turned, c + 1)
            nc.vector.tensor_scalar(tok_t[:, c, :], bank[c % 4][:, 0:T], pcol("norm_ffn", c), None,
                                    ALU.mult).then_inc(tok_dve, 1)

        def by_token(v, n):
            return bcast(v.unsqueeze(2), [P, TB, n])

        def first_max(v, top, n, eq, at, best, hot):
            link_dve(dve, nc.vector.tensor_reduce(top, v, AX_X, ALU.max))
            link_dve(dve, nc.vector.tensor_tensor(eq, v, by_token(top, n), ALU.is_equal))
            link_dve(dve, nc.vector.scalar_tensor_tensor(
                out=at, in0=eq, scalar=-100.0, in1=bcast(iota_f[:, 0:n].unsqueeze(1), [P, TB, n]),
                op0=ALU.mult, op1=ALU.add))
            link_dve(dve, nc.vector.tensor_reduce(best, at, AX_X, ALU.min))
            link_dve(dve, nc.vector.tensor_tensor(hot, at, by_token(best, n), ALU.is_equal))

        dve.wait_ge(logits_raw, 1)
        glog, elog, g_hot = lgt[:, :, 0:NG], lgt[:, :, NG:NG + NE], r8[:, 1, :, 0:NG]
        for b in range(TB):
            ins = nc.vector.tensor_copy(lgt[:, b, :], bank[6 + b][:, 0:NG + NE])
        link_dve(dve, ins)
        first_max(glog, r1[:, 0, :], NG, r8[:, 2, :, 0:NG], r8[:, 3, :, 0:NG], r1[:, 7, :], g_hot)
        nc.vector.tensor_tensor(r8[:, 4, :, 0:NG], glog, by_token(r1[:, 0, :], NG), ALU.subtract)\
          .then_inc(margin, 1)

        def by_group(v):
            return v.rearrange("p b (g e) -> p b g e", g=NG)

        def over_experts(v):
            return bcast(v.unsqueeze(3), [P, TB, NG, EPG])

        def over_groups(v):
            return bcast(v.unsqueeze(2), [P, TB, NG, EPG])
        link_dve(dve, nc.vector.tensor_tensor(by_group(rt[:, 1, :, :]), by_group(elog),
                                              over_experts(g_hot), ALU.mult))
        link_dve(dve, nc.vector.tensor_reduce(r8[:, 6, :, :], rt[:, 1, :, :].rearrange("p b (g e) -> p b e g", g=NG),
                                              AX_X, ALU.add))
        first_max(r8[:, 6, :, :], r1[:, 2, :], EPG, r8[:, 2, :, :], r8[:, 3, :, :], r1[:, 7, :], r8[:, 7, :, :])
        link_dve(dve, nc.vector.scalar_tensor_tensor(out=r8[:, 8, :, :], in0=r8[:, 7, :, :], scalar=-3e38,
                                                     in1=r8[:, 6, :, :], op0=ALU.mult, op1=ALU.add))
        first_max(r8[:, 8, :, :], r1[:, 3, :], EPG, r8[:, 2, :, :], r8[:, 3, :, :], r1[:, 7, :], r8[:, 9, :, :])
        nc.vector.tensor_tensor(r1[:, 4, :], r1[:, 3, :], r1[:, 2, :], ALU.subtract).then_inc(margin, 1)
        nc.vector.tensor_tensor(by_group(rt[:, 2, :, :]), over_experts(g_hot), over_groups(r8[:, 7, :, :]), ALU.mult)
        link_dve(dve, nc.vector.tensor_tensor(by_group(rt[:, 3, :, :]), over_experts(g_hot),
                                              over_groups(r8[:, 9, :, :]), ALU.mult))
        nc.vector.tensor_tensor(rt[:, 4, :, :], rt[:, 2, :, :], rt[:, 3, :, :], ALU.add).then_inc(member, 1)
        dve.wait_ge(exp_ready, 4)
        nc.vector.tensor_reduce(r1[:, 1, :], r8[:, 5, :, 0:NG], AX_X, ALU.add)
        dve.wait_ge(exp_ready, 5)
        link_dve(dve, nc.vector.tensor_scalar(r1[:, 6, :], r1[:, 5, :], 1.0, None, ALU.add))
        link_dve(dve, nc.vector.tensor_tensor(r1[:, 6, :], r1[:, 6, :], r1[:, 1, :], ALU.mult))
        link_dve(dve, nc.vector.reciprocal(pos[:, :, 2], r1[:, 6, :]))
        link_dve(dve, nc.vector.tensor_tensor(pos[:, :, 3], pos[:, :, 2], r1[:, 5, :], ALU.mult))
        dve.wait_ge(rank_raw, 1)
        ranks, places = rt[:, 5:8, :, :].rearrange("p n b e -> p (n b e)"), \
            rt[:, 8:11, :, :].rearrange("p n b e -> p (n b e)")
        n_all = TB * NE + 1
        nc.vector.tensor_copy(ranks[:, 0:n_all - 1], bank[5][:, 0:TB * NE])
        link_dve(dve, nc.vector.tensor_reduce(r1[:, 8, 0:1], bank[5][:, 2 * NE:3 * NE], AX_X, ALU.max))
        link_dve(dve, nc.vector.tensor_scalar(ranks[:, n_all - 1:n_all], r1[:, 8, 0:1], -1.0, None, ALU.add))
        link_dve(dve, nc.vector.tensor_copy(rank_i[:, :], ranks[:, 0:n_all]))
        link_dve(dve, nc.vector.tensor_scalar(rank_i[:, :], rank_i[:, :], CAP - 1, None, ALU.bitwise_and))
        link_dve(dve, nc.vector.tensor_copy(places[:, 0:n_all], rank_i[:, :]))
        link_dve(dve, nc.vector.scalar_tensor_tensor(
            out=places[:, 0:n_all], in0=places[:, 0:n_all], scalar=-1.0, in1=ranks[:, 0:n_all],
            op0=ALU.mult, op1=ALU.add))
        slot = ranks[:, 0:TB * NE].rearrange("p (b e) -> p b e", b=TB)
        full = places[:, 0:TB * NE].rearrange("p (b e) -> p b e", b=TB)
        link_dve(dve, nc.vector.scalar_tensor_tensor(out=slot, in0=full, scalar=float(NE - 1), in1=slot,
                                                     op0=ALU.mult, op1=ALU.add))
        link_dve(dve, nc.vector.scalar_tensor_tensor(
            out=slot, in0=bcast(iota_f[:, 0:NE].unsqueeze(1), [P, TB, NE]), scalar=float(CAP), in1=slot,
            op0=ALU.mult, op1=ALU.add))
        for choice in range(2):
            ins = nc.vector.tensor_tensor(rt[:, 2 + choice, :, :], rt[:, 2 + choice, :, :], slot, ALU.mult)
        link_dve(dve, ins)
        for choice in range(2):
            ins = nc.vector.tensor_reduce(pos[:, :, choice], rt[:, 2 + choice, :, :], AX_X, ALU.add)
        link_dve(dve, ins)
        last = places[0:1, n_all - 1:n_all]
        nc.vector.tensor_scalar(rounds_i[:, 0:1], last, 1.0 / CAP, 1.0, ALU.mult, ALU.add)
        nc.vector.tensor_scalar(rounds_i[:, 1:2], last, float(NE - 3), None, ALU.add).then_inc(routed, 1)

        def build_group(s, before):
            def place(b, choice, dst, gate):
                at = pos[:, b, choice:choice + 1]
                if gate:
                    return nc.vector.tensor_scalar(dst, iota_f[:, :], at, pos[:, b, 2 + choice:3 + choice],
                                                   ALU.is_equal, ALU.mult)
                return nc.vector.tensor_scalar(dst, iota_f[:, :], at, None, ALU.is_equal)

            for b in range(TB):
                ins = place(b, 0, onehot[:, s, b, :], False)
            ins.then_inc(built, 1)
            dve.wait_ge(built, 4 * before + 1)
            for b in range(TB):
                ins = nc.vector.scalar_tensor_tensor(out=onehot[:, s, b, :], in0=iota_f[:, :],
                                                     scalar=pos[:, b, 1:2], in1=onehot[:, s, b, :],
                                                     op0=ALU.is_equal, op1=ALU.add)
            ins.then_inc(built, 1)
            for b in range(TB):
                place(b, 0, gated[:, b, :], True)
                ins = place(b, 1, gtmp[:, b, :], True)
            ins.then_inc(built, 1)
            dve.wait_ge(built, 4 * before + 3)
            nc.vector.tensor_tensor(gated[:, :, :], gated[:, :, :], gtmp[:, :, :], ALU.add)
            nc.vector.tensor_scalar(pos[:, :, 0:2], pos[:, :, 0:2], -float(P), None, ALU.add).then_inc(built, 1)

        build_group(0, 0)
        nc.vector.memset(sm[:, 67:68], 0.0).then_inc(moe_added, 1)
        dve.wait_ge(built, 4)
        n_rounds = dve.value_load(rounds_i[0:1, 0:1], min_val=1, max_val=T // CAP)
        with dve.Fori(0, n_rounds) as r:
            with dve.Fori(0, NE // 8) as i:
                for s in range(2):
                    k = 8 * r + 2 * i + s
                    for half in range(2):
                        dve.wait_ge(xt_raw, 2 * k + half + 1)
                        nc.vector.tensor_tensor(
                            x_t[:, s, 4 * half:4 * half + 4, :],
                            bank[5 + half][:, :].rearrange("p (c j) -> p c j", c=4),
                            bcast(par[:, PCOLS["norm_ffn"] + 4 * half:PCOLS["norm_ffn"] + 4 * half + 4].unsqueeze(2),
                                  [P, 4, P]), ALU.mult).then_inc(xt_kept, 1)
                    dve.wait_ge(gmat_raw, k + 1)
                    nc.vector.tensor_copy(gmat[:, :], bank[5][:, 0:T]).then_inc(gmat_kept, 1)
                    dve.wait_ge(built, 4 * k + 4)
                    build_group(1 - s, k + 1)
                    for e in range(4):
                        x = 4 * k + e
                        dve.wait_ge(gate_silu, x + 1)
                        nc.vector.tensor_tensor(h_e[:, :], h_e[:, :], bank[0][:, P:2 * P], ALU.mult)\
                          .then_inc(h_ready, 1)
                        dve.wait_ge(ye_raw, x + 1)
                        for j in range(2, 4):
                            ins = nc.vector.tensor_copy(y_e[CAP * e:CAP * (e + 1), 256 * j:256 * (j + 1)],
                                                        bank[2][CAP * j:CAP * (j + 1), 0:256])
                        ins.then_inc(ye_dve, 1)
                    for q in range(4):
                        b, half = divmod(q, 2)
                        v = res[:, b, half * 512:(half + 1) * 512]
                        dve.wait_ge(moe_raw, 4 * k + q + 1)
                        nc.vector.tensor_tensor(v, v, bank[M_BANK[q]][:, :], ALU.add).then_inc(moe_added, 1)
        dve.wait_ge(moe_added, NE * n_rounds + 1)
        dve.wait_ge(ld_fgain, 16)
        for b in range(TB):
            nc.vector.tensor_tensor(tok[:, b, :], res[:, b, :], fgain[:, :], ALU.mult).then_inc(res_moe, 1)
        dve.wait_ge(res_moe, 2)
        link_dve(dve, nc.vector.tensor_tensor_reduce(
            out=fgain[:, :], in0=tok[:, 1, :], in1=tok[:, 1, :], scale=1.0, scalar=0.0,
            op0=ALU.mult, op1=ALU.add, accum_out=sm[:, 75:76]))
        dve.wait_ge(ss_act, 3)
        nc.vector.tensor_scalar(sm[:, 76:78], sm[:, 72:74], 1.0 / D, EPS, ALU.mult, ALU.add)
        link_dve(dve, nc.vector.tensor_scalar(sm[:, 78:80], sm[:, 74:76], 1.0 / D, None, ALU.mult))
        nc.vector.scalar_tensor_tensor(out=sm[:, 78:80], in0=sm[:, 76:78], scalar=EPS, in1=sm[:, 78:80],
                                       op0=ALU.mult, op1=ALU.add).then_inc(ms_ready, 1)
        lo(dve, GA)
        dve.wait_ge(rstd_ready, 3)
        nc.vector.tensor_scalar(nrm[:, 0, :], tok[:, 0, :], sm[:, 82:83], None, ALU.mult).then_inc(nrm_dve, 1)
        turn_dve(dve, 1, "norm1_2")
        lo(dve, GA + 1)
        for b in range(TB):
            ins = nc.vector.tensor_scalar(res[:, b, :], tok[:, b, :], sm[:, 80 + b:81 + b], None, ALU.mult)
        ins.then_inc(res_mid, 1)

        dve.wait_ge(narrow_hi, 2)
        nc.vector.tensor_tensor(ws_lo[:, :, :], w_z[:, :, :], ws_hi[:, :, :].bitcast(F32),
                                ALU.subtract).then_inc(narrow_lo, 1)
        li = lpad[:, :, 0:T]
        t1 = st[:, 0:2, :, :].rearrange("p n c d -> p n (c d)")
        lq = nrm[:, 1, :].rearrange("p (c t) -> p c t", c=LC)

        def conv_lru(c):
            dve.wait_ge(lx_copied, c + 1)
            dve.wait_ge(const_ready, 6)
            for tap in range(4):
                wc = pcol("conv_w_2", tap * LC + c)
                src = lpad[:, c, tap:tap + T]
                if tap == 0:
                    link_dve(dve, nc.vector.tensor_scalar(lx[:, c, :], src, wc, pcol("conv_b_2", c), ALU.mult,
                                                          ALU.add))
                    continue
                ins = nc.vector.scalar_tensor_tensor(out=lx[:, c, :], in0=src, scalar=wc, in1=lx[:, c, :],
                                                     op0=ALU.mult, op1=ALU.add)
                if tap < 3:
                    link_dve(dve, ins)
            ins.then_inc(lx_ready, 1)

        for g in range(GA + 2, G_FF):
            lo(dve, g)
            if GA + 2 <= g < GA + 6:
                conv_lru(g - GA - 2)
            if g == GA + 5:
                dve.wait_ge(zf_kept, 1)
                nc.vector.scalar_tensor_tensor(out=t1, in0=la[:, :, :], scalar=-1.0, in1=la[:, :, :],
                                               op0=ALU.mult, op1=ALU.min).then_inc(neg_abs, 1)
            if g == GA + 7:
                dve.wait_ge(zf_log, 1)
                nc.vector.scalar_tensor_tensor(out=la[:, :, :], in0=la[:, :, :], scalar=0.0, in1=t1, op0=ALU.min,
                                               op1=ALU.subtract).then_inc(la_ready, 1)
            if g == GA + 13:
                dve.wait_ge(decay_exp, 1)
                dve.wait_ge(k_kept, 1)
                nc.vector.tensor_tensor(k_tok[:, :, :], k_tok[:, :, :], t1, ALU.mult).then_inc(kdec_ready, 1)
            if g == GA + 11:
                dve.wait_ge(l_tanh, 1)
                nc.vector.tensor_tensor(lx[:, :, :], lx[:, :, :], li, ALU.mult)
                nc.vector.tensor_scalar(lgate[:, :, :], lgate[:, :, :], -1.0, 1e-30, ALU.mult, ALU.max)\
                  .then_inc(l_neg, 1)
            if g == GA + 14:
                dve.wait_ge(l_sqrt, 1)
                dve.wait_ge(l_exp, 1)
                link_dve(dve, nc.vector.scalar_tensor_tensor(out=li, in0=lq, scalar=1.0, in1=li, op0=ALU.add,
                                                             op1=ALU.mult))
            if g == GA + 15:
                link_dve(dve, nc.vector.tensor_tensor(li, li, lx[:, :, :], ALU.mult))
            if g in (GA + 17, GA + 18):
                for c in range(2 * (g - GA - 17), 2 * (g - GA - 17) + 2):
                    nc.vector.tensor_tensor_scan(lr[:, c, :], lq[:, c, :], li[:, c, :], 0.0, ALU.mult, ALU.add)\
                      .then_inc(lru_scan, 1)
            if g == G_G + 4:
                dve.wait_ge(upd_raw, 1)
                dve.wait_ge(kdec_ready, 1)
                dve.wait_ge(decay_exp, 1)
                link_dve(dve, nc.vector.tensor_copy(st[:, 0, :, :],
                                                    bank[6][:, 0:256].rearrange("p (c d) -> p c d", c=2)))
                for n in range(1, 4):
                    for c in range(2):
                        o = (n // 2) * 256 + c * P
                        ins = nc.vector.scalar_tensor_tensor(
                            out=st[:, n, c, :], in0=st[:, n - 1, c, :], scalar=dec[:, c, n:n + 1],
                            in1=bank[6 + n % 2][:, o:o + P], op0=ALU.mult, op1=ALU.add)
                    if n < 3:
                        link_dve(dve, ins)
                ins.then_inc(st_ready, 1)
            if g == G_LG + 2:
                dve.wait_ge(o_sq, 2)
                link_dve(dve, nc.vector.tensor_reduce(sm[:, 40:48], v_tok[:, :, :].rearrange(
                    "p n (c d) -> p (n c) d", c=4), AX_X, ALU.add))
                nc.vector.tensor_scalar(sm[:, 48:56], sm[:, 40:48], 1.0 / P, EPS, ALU.mult, ALU.add)\
                  .then_inc(o_ms, 1)
            if g == G_LG + 3:
                dve.wait_ge(o_rstd, 1)
                dve.wait_ge(g_gain, 1)
                for n in range(2):
                    v = v_tok[:, n, :].rearrange("p (c d) -> p c d", c=4)
                    nc.vector.tensor_tensor(v, bank[4 + n][:, :].rearrange("p (c d) -> p c d", c=4),
                                            bcast(sm[:, 56 + 4 * n:60 + 4 * n].unsqueeze(2), [P, 4, P]), ALU.mult)\
                      .then_inc(gla_ready, 1)
            if g == G_WO2:
                dve.wait_ge(gla_ready, 2)
                for n in range(2):
                    v = v_tok[:, n, :].rearrange("p (c d) -> p c d", c=4)
                    gv = g_tok[:, :, :].rearrange("p b (c q d) -> p q (b c) d", c=2, q=2)[:, n]
                    nc.vector.tensor_tensor(v, v, gv, ALU.mult).then_inc(gla_ready, 1)
            if G_LG + 2 <= g < G_LG + 6:
                c = g - G_LG - 2
                if c == 0:
                    dve.wait_ge(lru_scan, LC)
                dve.wait_ge(lgate_kept, c + 1)
                nc.vector.tensor_tensor(lr[:, c, :], lr[:, c, :], lgate[:, c, :], ALU.mult).then_inc(lru_prod, 1)
            if G_LG + 3 <= g < G_LG + 7:
                c = g - G_LG - 3
                dve.wait_ge(lru_hi, c + 1)
                nc.vector.tensor_tensor(act_q[:, 1, c, :], lr[:, c, :], act_q[:, 0, c, :].bitcast(F32),
                                        ALU.subtract).then_inc(lru_lo, 1)
            if g == G_WO2 + 3:
                for b in range(TB):
                    dve.wait_ge(gla_hi, b + 1)
                    nc.vector.tensor_tensor(act_q[:, 1, 4:8, b * P:(b + 1) * P],
                                            bank[6 + b][:, :].rearrange("p (c t) -> p c t", c=4),
                                            act_q[:, 0, 4:8, b * P:(b + 1) * P].bitcast(F32), ALU.subtract)\
                      .then_inc(gla_lo, 1)
        lo(dve, G_FF)
        add_res(dve, 1, G_FF - 1, bank[0:4], res_mix2)
        dve.wait_ge(res_mix2, 2)
        norm_dve(dve, 3, res, nrm)
        turn_dve(dve, 2, "norm2_2")
        lo(dve, G_FF + 1)

        def final_gain(b):
            dve.wait_ge(ld_fgain, 32)
            dve.wait_ge(res_ffn, b + 1)
            nc.vector.tensor_tensor(nrm[:, b, :], res[:, b, :], fg2, ALU.mult).then_inc(gained, 1)

        for g in range(G_FF + 2, GEND):
            lo(dve, g)
            for f in range(FC):
                if g == GU[f] + 2:
                    dve.wait_ge(f_silu, f + 1)
                    nc.vector.tensor_tensor(lx[:, f % 4, :], lx[:, f % 4, :], bank[f % 4][:, T:2 * T],
                                            ALU.mult).then_inc(f_prod, 1)
                if g == GU[f] + 3:
                    dve.wait_ge(f_hi, f + 1)
                    nc.vector.tensor_tensor(act_q[:, 1, f % 8, :], lx[:, f % 4, :],
                                            act_q[:, 0, f % 8, :].bitcast(F32), ALU.subtract).then_inc(f_lo, 1)
        add_res(dve, 2, GEND - 1, bank[4:8], res_ffn, final_gain)
        dve.wait_ge(ss_act, 5)
        nc.vector.tensor_scalar(sm[:, 2:4], sm[:, 0:2], 1.0 / D, EPS, ALU.mult, ALU.add).then_inc(ms_ready, 1)
        dve.wait_ge(rstd_ready, 5)
        nc.vector.tensor_scalar(nrm[:, 0, :], nrm[:, 0, :], sm[:, 4:5], None, ALU.mult).then_inc(nrm_dve, 1)

    @block.tensor
    def _(pe):
        pe.wait_ge(ld_par, 16 * N_ROWS_A)
        pe.wait_ge(const_ready, 1)
        nc.tensor.transpose(bank[4][:, 0:ROWS_A], prow[0:ROWS_A, 0, :], ident[0:ROWS_A, 0:ROWS_A])\
          .then_inc(par_turned, 1)
        turn_pe(pe, 0, 0, xdt)

        def turn_x(i):
            pe.wait_ge(silu_done, i + 1)
            if i >= 2:
                pe.wait_ge(x_kept, i - 1)
            elif i == 0:
                pe.wait_ge(par_ready, 1)
            for b in range(TB):
                mm = nc.tensor.transpose(bank[4 + i % 2][:, b * P:(b + 1) * P], cv[:, i % 3, b * P:(b + 1) * P],
                                         ident[:, :])
            mm.then_inc(x_turned, 1)

        def ssd_start():
            pe.wait_ge(dt_ready, 1)
            pe.wait_ge(const_ready, 2)
            nc.tensor.matmul(bank[7][:, 0:HEADS], m_gt[:, :], adt[:, 0, 0, :], start=True, stop=True)
            nc.tensor.matmul(bank[7][:, HEADS:2 * HEADS], m_le[:, :], adt[:, 0, 1, :], start=True, stop=True)\
              .then_inc(ef_raw, 1)
            pe.wait_ge(silu_done, XC)
            pe.wait_ge(x_kept, KC)
            for g in range(GROUPS):
                nc.tensor.matmul(bank[5 + g][:, 0:T], bc_t[:, g, 0:P], bc_t[:, 2 + g, :], start=True, stop=True)
                nc.tensor.matmul(bank[5 + g][:, T:T + P], bc_t[:, g, P:T], bc_t[:, 2 + g, P:T], start=True,
                                 stop=True).then_inc(cb_raw, 1)

        def seg(it):
            pe.wait_ge(seg_lhs, it + 1)
            if it == 0:
                pe.wait_ge(cb_ready, GROUPS)
            else:
                pe.wait_ge(seg_exp, it)
            for j in range(4):
                mm = nc.tensor.matmul(bank[5][:, j * P:(j + 1) * P], seg_l[:, j, :], m_le[:, :], start=True,
                                      stop=True)
            mm.then_inc(seg_raw, 1)

        def y_same(it):
            b, q = divmod(it, 4)
            pe.wait_ge(seg_m, it + 1)
            if it == 0:
                pe.wait_ge(xdt_ready, 1)
            if it % 2 == 0 and it >= 2:
                pe.wait_ge(y_kept, it // 2)
            for j in range(4):
                o = (q % 2) * 256 + j * HD
                mm = nc.tensor.matmul(bank[6][:, o:o + HD], seg_e[:, it % 2, j, :],
                                      xdt[:, b, (4 * q + j) * HD:(4 * q + j + 1) * HD], start=True, stop=True)
            mm.then_inc(y_raw, 1)

        def y_off(g):
            pe.wait_ge(xdt_decayed, 1)
            if g == 0:
                pe.wait_ge(seg_exp, 8)
            else:
                pe.wait_ge(y_kept, 4)
            nc.tensor.matmul(bank[5 + g][:, :], cbm[:, g, 1, :], xdt[:, 0, g * GW:(g + 1) * GW], start=True,
                             stop=True).then_inc(yoff_raw, 1)

        def sum_sc(hf, j):
            n = 4 * hf + j
            pe.wait_ge(sc_sq, n + 1)
            if n == 0:
                pe.wait_ge(ef_ready, 1)
                pe.wait_ge(x_kept, KC)
            if hf and j == 0:
                pe.wait_ge(sc_scaled, 1)
            bk = bank[4] if j < 2 else bank[7]
            nc.tensor.matmul(bk[:, (j % 2) * T:(j % 2 + 1) * T], blk64[:, :], cv[:, j % 3, :], start=True,
                             stop=True).then_inc(sc_sum, 1)

        def turn_ssd(n):
            b, g = divmod(n, GROUPS)
            pe.wait_ge(ssd_norm, n + 1)
            if n >= 2:
                pe.wait_ge(ssd_lo, n - 1)
            else:
                pe.wait_ge(yoff_kept, 2)
            for j in range(4):
                mm = nc.tensor.transpose(bank[5 + n % 2][:, j * P:(j + 1) * P],
                                         z_tok[:, b, g * GW + j * P:g * GW + (j + 1) * P], ident[:, :])
            mm.then_inc(ssd_turned, 1)

        for g in range(G_Z):
            if g >= 4:
                pe.wait_ge(xbc_copied, g - 3)
            turn_gran(pe, g, bank[g % 4][:, 0:T], act_p, 0 if g == 0 else None)
            if g == 6:
                pe.wait_ge(ld_par, 16 * N_SMALL)
                nc.tensor.transpose(bank[7][:, 0:ROWS_B], prow[0:ROWS_B, 1, :], ident[0:ROWS_B, 0:ROWS_B])\
                  .then_inc(par_turned, 1)
            if 3 <= g < 3 + KC:
                turn_x(g - 3)
        pe.wait_ge(narrow_lo, 1)
        pe.wait_ge(par_ready, 2)
        narrow_gran(pe, bank[7][0:HEADS, 0:T]).then_inc(dt_raw, 1)
        for t in range(2):
            pe.wait_ge(xbc_copied, 10 + 2 * t)
            for j in range(4):
                g = G_Z + 4 * t + j
                flow_gran(pe, g, [bank[2 * t + b][:, :] for b in range(TB)], act_p, 2 * j)
                if g == G_Z + 1:
                    pe.wait_ge(dt_kept, 1)
                    for b in range(TB):
                        mm = nc.tensor.transpose(bank[6][:, b * HEADS:(b + 1) * HEADS],
                                                 dt_t[:, b * P:(b + 1) * P], ident[0:HEADS, 0:HEADS])
                    mm.then_inc(dt_raw, 1)
        ssd_start()
        for g in range(G_SC, G_WO):
            hf, j = divmod(g - G_SC, 12)
            kind, c = divmod(j, 4)
            if kind == 0 and hf == 0:
                pe.wait_ge(z_kept, c + 1)
            elif kind == 0:
                pe.wait_ge(b_used, c + 1)
            elif kind == 1:
                pe.wait_ge(c_kept, 4 * hf + c + 1)
            else:
                pe.wait_ge(v_used, 4 * hf + c + 1)
            turn_gran(pe, g, bank[c][:, 0:T], act_p)
            if g % 2 == 0 and g < G_SC + 16:
                seg((g - G_SC) // 2)
            if g % 2 == 0 and G_SC + 2 <= g < G_SC + 18:
                y_same((g - G_SC - 2) // 2)
            for h in range(2):
                if G_SC + 12 * h + 11 <= g < G_SC + 12 * h + 15 and g < G_WO:
                    sum_sc(h, g - G_SC - 12 * h - 11)
            if g == G_SC + 18:
                y_off(0)
                y_off(1)
        for g in range(G_WO, GA):
            k = MIX[g - G_WO]
            if k == 8:
                pe.wait_ge(sc_lo, 1)
            if g in (G_WO, G_WO + 2):
                for n in range(2):
                    turn_ssd(n + 2 * (g == G_WO + 2))
            if k == 0:
                pe.wait_ge(ssd_lo, 4)
            if k == 12:
                pe.wait_ge(sc_lo, 2)
            a = act_q[:, :, k - 8, :] if k >= 8 else act_p[:, :, k, :]
            row_gran(pe, g, bank[0:4], a, g == G_WO, g == GA - 1, (b_used, 5) if g == G_WO else None)
            if g < G_WO + 3:
                sum_sc(1, g - G_WO + 1)

        pe.wait_ge(res_mix, 2)
        pe.wait_ge(nrm_act, 2)
        pe.wait_ge(nrm_dve, 2)
        for c in range(KC + 2):
            if c < KC:
                if c >= 4:
                    pe.wait_ge(*((tok_act, (c - 4) // 2 + 1) if c % 2 == 0 else (tok_dve, (c - 5) // 2 + 1)))
                for b in range(TB):
                    mm = nc.tensor.transpose(bank[c % 4][:, b * P:(b + 1) * P], tok[:, b, c * P:(c + 1) * P],
                                             ident[:, :])
                mm.then_inc(tok_turned, 1)
            if c >= 2:
                k = c - 2
                pe.wait_ge(tok_act if k % 2 == 0 else tok_dve, k // 2 + 1)
                for b in range(TB):
                    mm = nc.tensor.matmul(bank[6 + b][:, 0:NG + NE], tok_t[:, k, b * P:(b + 1) * P],
                                          w_rt[:, k, :], start=(k == 0), stop=(k == KC - 1))
        mm.then_inc(logits_raw, 1)
        pe.wait_ge(const_ready, 4)
        pe.wait_ge(member, 1)
        nc.tensor.matmul(bank[5][:, 0:NE], m_lt[:, :], rt[:, 4, 0, :], start=True, stop=True)
        for o, last in ((NE, m_lt), (2 * NE, ones)):
            nc.tensor.matmul(bank[5][:, o:o + NE], ones[:, :], rt[:, 4, 0, :], start=True, stop=False)
            mm = nc.tensor.matmul(bank[5][:, o:o + NE], last[:, :], rt[:, 4, 1, :], start=False, stop=True)
        mm.then_inc(rank_raw, 1)

        pe.wait_ge(routed, 1)
        n_rounds = pe.value_load(rounds_i[0:1, 0:1], min_val=1, max_val=T // CAP)
        with pe.Fori(0, n_rounds) as r:
            with pe.Fori(0, NE // 8) as i:
                for s in range(2):
                    k = 8 * r + 2 * i + s
                    pe.wait_ge(built, 4 * k + 2)
                    for half in range(2):
                        for c in range(4):
                            for b in range(TB):
                                o = (4 * half + c) * P
                                mm = nc.tensor.matmul(bank[5 + half][:, c * P:(c + 1) * P], tok[:, b, o:o + P],
                                                      onehot[:, s, b, :], start=(b == 0), stop=(b == TB - 1))
                        mm.then_inc(xt_raw, 1)
                    pe.wait_ge(xt_kept, 2 * k + 2)
                    pe.wait_ge(built, 4 * k + 4)
                    for b in range(TB):
                        mm = nc.tensor.transpose(bank[5][:, b * P:(b + 1) * P], gated[:, b, :], ident[:, :])
                    mm.then_inc(gmat_raw, 1)
                    for e in range(4):
                        x = 4 * k + e
                        for n in range(2):
                            pe.wait_ge(*pair_landed(e, n, k + 1))
                        gu = PAIR[e].rearrange("p s (k n) -> p s k n", k=KC)
                        for c in range(KC):
                            for j in range(4):
                                mm = nc.tensor.matmul(bank[0][CAP * j:CAP * (j + 1), 0:2 * P],
                                                      x_t[:, s, c, CAP * e:CAP * (e + 1)],
                                                      gu[:, :, c, j * P:(j + 1) * P],
                                                      start=(c == 0), stop=(c == KC - 1))
                        mm.then_inc(gu_raw, 1)
                        pe.wait_ge(h_ready, x + 1)
                        nc.tensor.transpose(bank[4][:, 0:P], h_e[:, :], ident[:, :]).then_inc(ht_raw, 1)
                        pe.wait_ge(ht_kept, x + 1)
                        pe.wait_ge(landed_down[e % 2], 16 * (2 * k + e // 2 + 1))
                        if e:
                            pe.wait_ge(ye_act, x)
                            pe.wait_ge(ye_dve, x)
                        dn = DOWN[e % 2][:, :].rearrange("p (k n) -> p k n", k=FF // P)
                        for c in range(FF // P):
                            for j in range(4):
                                mm = nc.tensor.matmul(bank[2][CAP * j:CAP * (j + 1), 0:256],
                                                      h_t[:, CAP * c:CAP * (c + 1)],
                                                      dn[:, c, 256 * j:256 * (j + 1)],
                                                      start=(c == 0), stop=(c == FF // P - 1))
                        mm.then_inc(ye_raw, 1)
                    pe.wait_ge(ye_act, 4 * k + 4)
                    pe.wait_ge(ye_dve, 4 * k + 4)
                    pe.wait_ge(gmat_kept, k + 1)
                    for q in range(4):
                        b, half = divmod(q, 2)
                        pe.wait_ge(moe_added, 4 * k + (2 if q == 3 else 1))
                        nc.tensor.matmul(bank[M_BANK[q]][:, :], gmat[:, b * P:(b + 1) * P],
                                         y_e[:, half * 512:(half + 1) * 512], start=True, stop=True)\
                          .then_inc(moe_raw, 1)

        turn_pe(pe, 2, 1, nrm)

        def lru_gates(c):
            pe.wait_ge(lx_ready, c + 1)
            if c == 0:
                pe.wait_ge(ld_c, 16 * 5)
            if c >= 2:
                pe.wait_ge(lg_sig, c - 1)
            for n in range(2):
                mm = nc.tensor.matmul(bank[4 + c % 2][:, n * T:(n + 1) * T], lru_w[:, n, c, :], lx[:, c, :],
                                      start=True, stop=True)
            mm.then_inc(lg_raw, 1)

        for g in range(GA, G_WO2):
            if g < G_Q:
                turn_gran(pe, g, bank[g - GA][:, 0:T], act_p, 1 if g == GA else None)
            elif g < G_K:
                pe.wait_ge(lx_copied, g - G_Q + 1)
                turn_gran(pe, g, bank[g - G_Q][:, 0:T], act_p)
            elif g < G_V:
                pe.wait_ge(lx_copied, 4)
                flow_gran(pe, g, [bank[2 + b][:, 0:256] for b in range(TB)], act_p, 4 * (g - G_K))
            elif g < G_G:
                pe.wait_ge(q_kept, 2)
                flow_gran(pe, g, [bank[b][:, :] for b in range(TB)], act_p, 2 * (g - G_V))
            elif g < G_LG:
                pe.wait_ge(k_kept, 1)
                flow_gran(pe, g, [bank[2 + b][:, :] for b in range(TB)], act_p, 2 * (g - G_G))
            else:
                c = g - G_LG
                if c < 2:
                    pe.wait_ge(v_kept, c + 1)
                else:
                    pe.wait_ge(g_kept, c - 1)
                turn_gran(pe, g, bank[c][:, 0:T], act_p)
            if g == GA:
                pe.wait_ge(narrow_lo, 2)
                narrow_gran(pe, bank[7][0:RANK, 0:T]).then_inc(z_raw, 1)
            if g == GA + 2:
                pe.wait_ge(zt_kept, 1)
                for b in range(TB):
                    mm = nc.tensor.matmul(bank[6][:, b * 256:(b + 1) * 256], z_t[:, b * P:(b + 1) * P], w_al[:, :],
                                          start=True, stop=True)
                mm.then_inc(zf_raw, 1)
            if g == GA + 5:
                lru_gates(0)
                lru_gates(1)
            if g == GA + 7:
                pe.wait_ge(la_ready, 1)
                for b in range(TB):
                    nc.tensor.matmul(bank[6][:, b * 256:(b + 1) * 256], m_gtc[:, :], la[:, b, :], start=True,
                                     stop=True)
                for c in range(2):
                    for b in range(TB):
                        o = 4 * c + 2 * b
                        mm = nc.tensor.matmul(bank[7][:, o:o + 2], la[:, b, c * P:(c + 1) * P],
                                              blk64[:, 0:P:64], start=True, stop=True)
                mm.then_inc(suffix_raw, 1)
            if g == GA + 8:
                lru_gates(2)
                lru_gates(3)
            if g == G_G + 2:
                pe.wait_ge(kdec_ready, 1)
                pe.wait_ge(v_kept, 2)
                for n in range(4):
                    b, r0 = n // 2, 64 * (n % 2)
                    for h in range(4):
                        o = b * 256 + (h // 2) * P
                        mm = nc.tensor.matmul(bank[6 + n % 2][64 * (h % 2):64 * (h % 2) + 64, o:o + P],
                                              k_tok[r0:r0 + 64, b, h * 64:(h + 1) * 64],
                                              v_tok[r0:r0 + 64, b, h * P:(h + 1) * P], start=True, stop=True)
                mm.then_inc(upd_raw, 1)
            if g == G_G + 5:
                pe.wait_ge(st_ready, 1)
                pe.wait_ge(q_kept, 2)
                pe.wait_ge(lg_sig, 4)
                for n in range(4):
                    for h in range(4):
                        r0, o = 64 * (h % 2), (n // 2) * 256 + (h // 2) * P
                        mm = nc.tensor.matmul(bank[4 + h % 2][64 * (n % 2):64 * (n % 2) + 64, o:o + P],
                                              q_t[r0:r0 + 64, h // 2, n * 64:(n + 1) * 64],
                                              st[r0:r0 + 64, n, h // 2, :], start=True, stop=True)
                mm.then_inc(o_raw, 1)
        for g in range(G_WO2, G_FF):
            c = g - G_WO2
            if c < LC:
                pe.wait_ge(lru_lo, c + 1)
            else:
                pe.wait_ge(gla_lo, TB)
            row_gran(pe, g, bank[0:4], act_q[:, :, c, :], c == 0, c == KC - 1, (lgate_kept, 1) if c == 0 else None)
            if c == 1:
                pe.wait_ge(gla_ready, 4)
                for b in range(TB):
                    for h in range(4):
                        o = (2 * b + h // 2) * P
                        mm = nc.tensor.transpose(bank[6 + b][:, h * P:(h + 1) * P], v_tok[:, h % 2, o:o + P],
                                                 ident[:, :])
                    mm.then_inc(gla_turned, 1)

        pe.wait_ge(res_mix2, 2)
        turn_pe(pe, 3, 2, nrm)
        in_of = {}
        for f in range(FC):
            in_of[GU[f] - 1], in_of[GU[f]] = (f, 0), (f, 1)
        out_of = {g: f for f, g in GO.items()}
        for g in range(G_FF, GEND):
            if g in in_of:
                f, up = in_of[g]
                if not up and f >= 4:
                    pe.wait_ge(f_prod, f - 3)
                turn_gran(pe, g, bank[f % 4][:, up * T:(up + 1) * T], act_p, 2 if g == G_FF else None)
            else:
                f = out_of[g]
                pe.wait_ge(f_lo, f + 1)
                row_gran(pe, g, bank[4:8], act_q[:, :, f % 8, :], f == 0, f == FC - 1)


_OUTS = [((1, 256, 1024), "float32")]


def kernel(**inputs):
    import numpy as _np
    import concourse.bacc as _bacc
    from concourse import mybir as _mybir
    from concourse.bass_utils import run_bass_kernel_spmd as _run

    nc = _bacc.Bacc("TRN2", target_bir_lowering=False, num_devices=1)
    arrays, aps = {}, {}
    for name, value in inputs.items():
        a = _np.ascontiguousarray(value)
        arrays[f"in_{name}_dram"] = a
        ap = nc.dram_tensor(f"in_{name}_dram", a.shape, _mybir.dt.from_np(a.dtype), kind="ExternalInput").ap()
        aps[name] = ap if name in ("final_norm", "final_norm_2") else ap[0]
    out = nc.dram_tensor("out_0_dram", _OUTS[0][0], _mybir.dt.from_np(_np.dtype(_OUTS[0][1])),
                         kind="ExternalOutput").ap()
    two_block_layer(nc, aps.pop("x"), aps, out[0])
    r = _run(nc, [arrays], core_ids=[0])
    return r.results[0]["out_0_dram"]
```
